# Optimizing a Trainium2 kernel written in Bass

```python
import jax, jax.numpy as jnp
from jax import lax
import numpy as np

D_MODEL = 1024
BATCH = 1
SEQ = 256
DEPTH = 2

CHUNK = 64
N_META = 16
D_MIX = D_MODEL
D_POOL = D_MIX // 4
D_CONV = D_MIX // 4
D_RET = D_MIX - D_POOL - D_CONV
POOL_WINDOWS = (2, 4, 8, 16)
N_POOL_GROUPS = len(POOL_WINDOWS)
POOL_GROUP = D_POOL // N_POOL_GROUPS
CONV_WIDTH = 31
RET_HEADS = 4
RET_HEAD_DIM = D_RET // RET_HEADS
ROPE_BASE = 10000.0
D_FF = ((8 * D_MODEL // 3 + 63) // 64) * 64
D_IN = D_POOL + 2 * D_CONV + 4 * D_RET
DEEPNORM_ALPHA = (2.0 * DEPTH) ** 0.25
DEEPNORM_BETA = (8.0 * DEPTH) ** -0.25
LN_EPS = 1e-5


def layer_norm(x, g, b):
    xf = x.astype(jnp.float32)
    mu = jnp.mean(xf, axis=-1, keepdims=True)
    var = jnp.mean(jnp.square(xf - mu), axis=-1, keepdims=True)
    return ((xf - mu) * lax.rsqrt(var + LN_EPS) * g + b).astype(x.dtype)

def swiglu_ffn(x, w13, w2):
    a, u = jnp.split(x @ w13, 2, axis=-1)
    return (jax.nn.silu(a) * u) @ w2

def pool_mixer(xp, w_pool, scale):
    B, L, _ = xp.shape
    xf = xp.astype(jnp.float32)
    cs = jnp.concatenate([jnp.zeros((B, 1, D_POOL), jnp.float32), jnp.cumsum(xf, axis=1)], axis=1)
    t = jnp.arange(L)
    outs = []
    for gi, w in enumerate(POOL_WINDOWS):
        lo, hi = gi * POOL_GROUP, (gi + 1) * POOL_GROUP
        csg = cs[..., lo:hi]
        start = jnp.maximum(t + 1 - w, 0)
        win_sum = csg[:, 1:] - csg[:, start]
        count = (t + 1 - start).astype(jnp.float32)
        outs.append(win_sum / count[None, :, None] - xf[..., lo:hi])
    y = jnp.stack(outs, axis=2)
    y = jnp.einsum('blgc,gcd->blgd', y, w_pool.astype(jnp.float32)).reshape(B, L, D_POOL)
    return (y * scale).astype(xp.dtype)

def conv_module(a, gate, w_dw, b_dw, ln_g, ln_b, w_pw):
    u = a * jax.nn.sigmoid(gate)
    y = lax.conv_general_dilated(u, w_dw[:, None, :], window_strides=(1,),
                                 padding=[(CONV_WIDTH - 1, 0)],
                                 dimension_numbers=('NWC', 'WIO', 'NWC'),
                                 feature_group_count=D_CONV) + b_dw
    y = jax.nn.silu(layer_norm(y, ln_g, ln_b))
    return y @ w_pw

def rope(x, cos, sin):
    x1, x2 = jnp.split(x, 2, axis=-1)
    return jnp.concatenate([x1 * cos - x2 * sin, x2 * cos + x1 * sin], axis=-1)

def retention(q, k, v, g, gn_g):
    B, L, _ = q.shape
    f32 = jnp.float32
    pos = jnp.arange(L, dtype=f32)
    inv_freq = ROPE_BASE ** (-jnp.arange(0, RET_HEAD_DIM, 2, dtype=f32) / RET_HEAD_DIM)
    ang = pos[:, None] * inv_freq[None, :]
    cos, sin = jnp.cos(ang), jnp.sin(ang)
    heads = lambda t: t.astype(f32).reshape(B, L, RET_HEADS, RET_HEAD_DIM).transpose(0, 2, 1, 3)
    qh = rope(heads(q), cos, sin)
    kh = rope(heads(k), cos, sin) * (RET_HEAD_DIM ** -0.5)
    vh = heads(v)
    P = (-N_META) % CHUNK
    NC = (L + P) // CHUNK
    chunk = lambda t: jnp.pad(t, ((0, 0), (0, 0), (P, 0), (0, 0))).reshape(B, RET_HEADS, NC, CHUNK, RET_HEAD_DIM)
    qc, kc, vc = chunk(qh), chunk(kh), chunk(vh)
    log_gamma = jnp.log(1.0 - 2.0 ** (-5.0 - jnp.arange(RET_HEADS, dtype=f32)))
    i = jnp.arange(CHUNK, dtype=f32)
    intra_decay = jnp.exp(log_gamma[:, None, None] * jnp.abs(i[:, None] - i[None, :]))
    s = jnp.einsum('bhnid,bhnjd->bhnij', qc, kc) * intra_decay[None, :, None]
    o_intra = jnp.einsum('bhnij,bhnjd->bhnid', s, vc)
    q_decay = jnp.exp(log_gamma[:, None] * (i + 1.0))[None, :, :, None]
    k_decay = jnp.exp(log_gamma[:, None] * (CHUNK - 1.0 - i))[None, :, :, None]
    chunk_decay = jnp.exp(log_gamma * CHUNK)[None, :, None, None]

    def step(state, inp):
        q_n, k_n, v_n = inp
        o = jnp.einsum('bhid,bhde->bhie', q_n * q_decay, state)
        state = state * chunk_decay + jnp.einsum('bhjd,bhje->bhde', k_n * k_decay, v_n)
        return state, o

    to_scan = lambda t: t.transpose(2, 0, 1, 3, 4)
    state0 = jnp.zeros((B, RET_HEADS, RET_HEAD_DIM, RET_HEAD_DIM), f32)
    _, o_cross = lax.scan(step, state0, (to_scan(qc), to_scan(kc), to_scan(vc)))
    o = o_intra + o_cross.transpose(1, 2, 0, 3, 4)
    o = o.reshape(B, RET_HEADS, NC * CHUNK, RET_HEAD_DIM)[:, :, P:]
    mu = jnp.mean(o, axis=-1, keepdims=True)
    var = jnp.mean(jnp.square(o - mu), axis=-1, keepdims=True)
    o = ((o - mu) * lax.rsqrt(var + LN_EPS)).transpose(0, 2, 1, 3).reshape(B, L, D_RET) * gn_g
    return (jax.nn.silu(g.astype(f32)) * o).astype(g.dtype)

def token_mix(h, w_in, pool_w, pool_scale, conv_dw, conv_db, conv_ln_g, conv_ln_b, conv_pw, ret_gn_g, w_out):
    z = h @ w_in
    splits = [D_POOL, D_POOL + D_CONV, D_POOL + 2 * D_CONV,
              D_POOL + 2 * D_CONV + D_RET, D_POOL + 2 * D_CONV + 2 * D_RET,
              D_POOL + 2 * D_CONV + 3 * D_RET]
    xp, ca, cg, q, k, v, g = jnp.split(z, splits, axis=-1)
    y_pool = pool_mixer(xp, pool_w, pool_scale)
    y_conv = conv_module(ca, cg, conv_dw, conv_db, conv_ln_g, conv_ln_b, conv_pw)
    y_ret = retention(q, k, v, g, ret_gn_g)
    return jnp.concatenate([y_pool, y_conv, y_ret], axis=-1) @ w_out

def first_inputs(seed: int = 0) -> dict:
    key = jax.random.key(seed)
    ks = jax.random.split(key, 24)
    nrm = lambda k, shape, s: jax.random.normal(k, shape, jnp.float32) * s
    ones_n = lambda k, shape: 1.0 + 0.05 * jax.random.normal(k, shape, jnp.float32)
    return {
        "x": nrm(ks[0], (BATCH, SEQ, D_MODEL), 1.0),
        "meta": nrm(ks[1], (N_META, D_MODEL), 1.0),
        "ln_in_g": ones_n(ks[2], (D_MODEL,)),
        "ln_in_b": nrm(ks[3], (D_MODEL,), 0.02),
        "ffn1_w13": nrm(ks[4], (DEPTH, D_MODEL, 2 * D_FF), D_MODEL ** -0.5),
        "ffn1_w2": nrm(ks[5], (DEPTH, D_FF, D_MODEL), DEEPNORM_BETA * D_FF ** -0.5),
        "w_in": nrm(ks[6], (DEPTH, D_MODEL, D_IN), D_MODEL ** -0.5),
        "pool_w": nrm(ks[7], (DEPTH, N_POOL_GROUPS, POOL_GROUP, POOL_GROUP), POOL_GROUP ** -0.5),
        "pool_scale": ones_n(ks[8], (DEPTH, D_POOL)),
        "conv_dw": nrm(ks[9], (DEPTH, CONV_WIDTH, D_CONV), CONV_WIDTH ** -0.5),
        "conv_db": nrm(ks[10], (DEPTH, D_CONV), 0.02),
        "conv_ln_g": ones_n(ks[11], (DEPTH, D_CONV)),
        "conv_ln_b": nrm(ks[12], (DEPTH, D_CONV), 0.02),
        "conv_pw": nrm(ks[13], (DEPTH, D_CONV, D_CONV), D_CONV ** -0.5),
        "ret_gn_g": ones_n(ks[14], (DEPTH, D_RET)),
        "w_out": nrm(ks[15], (DEPTH, D_MIX, D_MODEL), DEEPNORM_BETA * D_MIX ** -0.5),
        "ffn2_w13": nrm(ks[16], (DEPTH, D_MODEL, 2 * D_FF), D_MODEL ** -0.5),
        "ffn2_w2": nrm(ks[17], (DEPTH, D_FF, D_MODEL), DEEPNORM_BETA * D_FF ** -0.5),
        "ln_g": ones_n(ks[18], (DEPTH, 3, D_MODEL)),
        "ln_b": nrm(ks[19], (DEPTH, 3, D_MODEL), 0.02),
    }

def first_block(x, meta, ln_in_g, ln_in_b, ffn1_w13, ffn1_w2, w_in, pool_w, pool_scale,
              conv_dw, conv_db, conv_ln_g, conv_ln_b, conv_pw, ret_gn_g, w_out,
              ffn2_w13, ffn2_w2, ln_g, ln_b):
    B = x.shape[0]
    h = jnp.concatenate([jnp.broadcast_to(meta[None].astype(x.dtype), (B, N_META, D_MODEL)), x], axis=1)
    h = layer_norm(h, ln_in_g, ln_in_b)
    for l in range(DEPTH):
        h = layer_norm(DEEPNORM_ALPHA * h + 0.5 * swiglu_ffn(h, ffn1_w13[l], ffn1_w2[l]), ln_g[l, 0], ln_b[l, 0])
        mix = token_mix(h, w_in[l], pool_w[l], pool_scale[l], conv_dw[l], conv_db[l],
                        conv_ln_g[l], conv_ln_b[l], conv_pw[l], ret_gn_g[l], w_out[l])
        h = layer_norm(DEEPNORM_ALPHA * h + mix, ln_g[l, 1], ln_b[l, 1])
        h = layer_norm(DEEPNORM_ALPHA * h + 0.5 * swiglu_ffn(h, ffn2_w13[l], ffn2_w2[l]), ln_g[l, 2], ln_b[l, 2])
    return h[:, N_META:]


HEAD_DIM = 64
Q_BLOCK = 128
EPS = 1e-6
NEG_INF = -1e30
A_HEADS = 8
A_PATTERNS = ((128, 1), (512, 4), (2048, 16))
B_HEADS = 4
B_DK = 64
B_DV = 128
B_GATE_RANK = 16
B_GATE_TAU = 16.0
B_CHUNK = 64
C_HEADS = 8
C_KV_HEADS = 2
C_WINDOW = 128
D_HEADS = 8
D_Q_RANK = 384
D_KV_RANK = 256
D_NOPE = 64
D_ROPE = 32
D_V = 64
D_FF_2 = -(-8 * D_MODEL // (3 * 256)) * 256

L0_IN_SIZES = (A_HEADS * HEAD_DIM, A_HEADS * HEAD_DIM, A_HEADS * HEAD_DIM,
               B_HEADS * B_DK, B_HEADS * B_DK, B_HEADS * B_DV, B_HEADS * B_DV, B_GATE_RANK)
L0_IN = sum(L0_IN_SIZES)
L0_MIX = A_HEADS * HEAD_DIM + B_HEADS * B_DV
L1_IN_SIZES = (C_HEADS * HEAD_DIM, C_KV_HEADS * HEAD_DIM, C_KV_HEADS * HEAD_DIM,
               D_Q_RANK, D_KV_RANK, D_ROPE)
L1_IN = sum(L1_IN_SIZES)
L1_MIX = C_HEADS * HEAD_DIM + D_HEADS * D_V
N_EVEN = (DEPTH + 1) // 2
N_ODD = DEPTH // 2


def rmsnorm(x, g):
    xf = x.astype(jnp.float32)
    y = xf * lax.rsqrt(jnp.mean(xf * xf, axis=-1, keepdims=True) + EPS)
    return (y * g.astype(jnp.float32)).astype(x.dtype)

def alibi_slopes(n):
    return jnp.asarray(np.array([2.0 ** (-8.0 * (i + 1) / n) for i in range(n)], dtype=np.float32))

def split_cols(t, sizes):
    return jnp.split(t, [int(c) for c in np.cumsum(sizes)[:-1]], axis=-1)

def with_prev_block(t, blk):
    lead = t.shape[:-2]
    L, dh = t.shape[-2:]
    tb = t.reshape(*lead, L // blk, blk, dh)
    prev = jnp.concatenate([jnp.zeros_like(tb[..., :1, :, :]), tb[..., :-1, :, :]], axis=-3)
    return jnp.concatenate([prev, tb], axis=-2)

def band_geometry(nb, blk, max_rel):
    i = jnp.arange(blk)[:, None]
    j = jnp.arange(2 * blk)[None, :]
    rel = i + blk - j
    key_pos = jnp.arange(nb)[:, None, None] * blk + j - blk
    valid = (rel >= 0) & (rel <= max_rel) & (key_pos >= 0)
    return rel.astype(jnp.float32), valid

def rope_2(t, pos):
    half = t.shape[-1] // 2
    freqs = ROPE_BASE ** (-jnp.arange(half, dtype=jnp.float32) / half)
    ang = pos.astype(jnp.float32)[:, None] * freqs[None, :]
    cos, sin = jnp.cos(ang)[:, None, :], jnp.sin(ang)[:, None, :]
    tf = t.astype(jnp.float32)
    t1, t2 = tf[..., :half], tf[..., half:]
    return jnp.concatenate([t1 * cos - t2 * sin, t2 * cos + t1 * sin], axis=-1).astype(t.dtype)

def dilated_branch(q, k, v, slopes, window, dilation):
    B_, H, S, dh = q.shape
    L = S // dilation
    Lp = -(-L // Q_BLOCK) * Q_BLOCK
    nb = Lp // Q_BLOCK

    def by_residue(t):
        t = t.reshape(B_, H, L, dilation, dh).transpose(0, 1, 3, 2, 4)
        return jnp.pad(t, ((0, 0), (0, 0), (0, 0), (0, Lp - L), (0, 0)))

    qb = by_residue(q).reshape(B_, H, dilation, nb, Q_BLOCK, dh)
    kb = with_prev_block(by_residue(k), Q_BLOCK)
    vb = with_prev_block(by_residue(v), Q_BLOCK).astype(jnp.float32)
    rel, valid = band_geometry(nb, Q_BLOCK, window // dilation)
    s = jnp.einsum('bhrnid,bhrnjd->bhrnij', qb, kb, preferred_element_type=jnp.float32) * dh ** -0.5
    s = s - slopes[:, None, None, None, None] * (rel * dilation)
    s = jnp.where(valid, s, NEG_INF)
    m = s.max(-1)
    p = jnp.exp(s - m[..., None])
    den = p.sum(-1)
    o = jnp.einsum('bhrnij,bhrnjd->bhrnid', p, vb) / den[..., None]

    def back(t):
        t = t.reshape(B_, H, dilation, Lp, *t.shape[5:])[:, :, :, :L]
        t = jnp.moveaxis(t, 2, 3)
        return t.reshape(B_, H, S, *t.shape[4:])

    return back(o), back(m), back(den)

def dilated_attention(q, k, v):
    slopes = alibi_slopes(A_HEADS)
    outs, maxes, dens = zip(*[dilated_branch(q, k, v, slopes, w, d) for (w, d) in A_PATTERNS])
    m_all = jnp.stack(maxes)
    wts = jnp.stack(dens) * jnp.exp(m_all - m_all.max(0))
    return jnp.einsum('pbhs,pbhsd->bhsd', wts, jnp.stack(outs)) / wts.sum(0)[..., None]

def gla(q, k, v, r, g_low, w_gate_up, b_gate, norm_g):
    B_, S, _ = q.shape
    C = B_CHUNK
    nc = S // C
    log_a = jax.nn.log_sigmoid((g_low @ w_gate_up + b_gate).astype(jnp.float32)) / B_GATE_TAU

    def chunks(t, dh):
        return t.reshape(B_, nc, C, B_HEADS, dh).transpose(0, 3, 1, 2, 4).astype(jnp.float32)

    qc = chunks(q, B_DK) * B_DK ** -0.5
    kc = chunks(k, B_DK)
    vc = chunks(v, B_DV)
    bcum = jnp.cumsum(chunks(log_a, B_DK), axis=-2)
    b_last = bcum[..., -1:, :]
    b_mid = bcum[..., C // 2 - 1:C // 2, :]
    att = jnp.einsum('bhncd,bhnsd->bhncs', qc * jnp.exp(bcum - b_mid), kc * jnp.exp(b_mid - bcum))
    att = jnp.where(jnp.tril(jnp.ones((C, C), dtype=bool)), att, 0.0)
    o_intra = jnp.einsum('bhncs,bhnse->bhnce', att, vc)
    dS = jnp.einsum('bhnsd,bhnse->bhnde', kc * jnp.exp(b_last - bcum), vc)
    decay = jnp.exp(b_last[..., 0, :])

    def step(state, inp):
        dS_n, dec_n = inp
        return dec_n[..., None] * state + dS_n, state

    init = jnp.zeros((B_, B_HEADS, B_DK, B_DV), jnp.float32)
    _, s_prev = lax.scan(step, init, (jnp.moveaxis(dS, 2, 0), jnp.moveaxis(decay, 2, 0)))
    s_prev = jnp.moveaxis(s_prev, 0, 2)
    o_inter = jnp.einsum('bhncd,bhnde->bhnce', qc * jnp.exp(bcum), s_prev)
    o = (o_intra + o_inter).transpose(0, 2, 3, 1, 4).reshape(B_, S, B_HEADS, B_DV)
    o = rmsnorm(o, norm_g)
    o = o * jax.nn.silu(r.astype(jnp.float32)).reshape(B_, S, B_HEADS, B_DV)
    return o.reshape(B_, S, B_HEADS * B_DV)

def swa_sink_attention(q, k, v, sinks):
    B_, S, _ = q.shape
    G = C_HEADS // C_KV_HEADS
    nb = S // Q_BLOCK
    qb = q.reshape(B_, nb, Q_BLOCK, C_KV_HEADS, G, HEAD_DIM).transpose(0, 3, 4, 1, 2, 5)
    kt = k.reshape(B_, S, C_KV_HEADS, HEAD_DIM).transpose(0, 2, 1, 3)
    vt = v.reshape(B_, S, C_KV_HEADS, HEAD_DIM).transpose(0, 2, 1, 3)
    kb = with_prev_block(kt, Q_BLOCK)
    vb = with_prev_block(vt, Q_BLOCK).astype(jnp.float32)
    rel, valid = band_geometry(nb, Q_BLOCK, C_WINDOW - 1)
    slopes = alibi_slopes(C_HEADS).reshape(C_KV_HEADS, G)[:, :, None, None, None]
    s = jnp.einsum('bkgnid,bknjd->bkgnij', qb, kb, preferred_element_type=jnp.float32) * HEAD_DIM ** -0.5
    s = jnp.where(valid, s - slopes * rel, NEG_INF)
    sink = sinks.astype(jnp.float32).reshape(C_KV_HEADS, G)[:, :, None, None, None]
    m = jnp.maximum(s.max(-1, keepdims=True), sink)
    p = jnp.exp(s - m)
    den = p.sum(-1, keepdims=True) + jnp.exp(sink - m)
    o = jnp.einsum('bkgnij,bknjd->bkgnid', p / den, vb)
    return o.transpose(0, 3, 4, 1, 2, 5).reshape(B_, S, C_HEADS * HEAD_DIM)

def mla(c_q, c_kv, k_rope, q_norm, w_uq, kv_norm, w_ukv):
    B_, S, _ = c_q.shape
    pos = jnp.arange(S)
    q = (rmsnorm(c_q, q_norm) @ w_uq).reshape(B_, S, D_HEADS, D_NOPE + D_ROPE)
    kv = (rmsnorm(c_kv, kv_norm) @ w_ukv).reshape(B_, S, D_HEADS, D_NOPE + D_V)
    q_nope, q_pe = q[..., :D_NOPE], rope_2(q[..., D_NOPE:], pos)
    k_nope, v = kv[..., :D_NOPE], kv[..., D_NOPE:].astype(jnp.float32)
    k_pe = rope_2(k_rope[:, :, None, :], pos)[:, :, 0, :]
    scale = (D_NOPE + D_ROPE) ** -0.5
    nb = S // Q_BLOCK
    qn_b = q_nope.reshape(B_, nb, Q_BLOCK, D_HEADS, D_NOPE).transpose(1, 0, 2, 3, 4)
    qp_b = q_pe.reshape(B_, nb, Q_BLOCK, D_HEADS, D_ROPE).transpose(1, 0, 2, 3, 4)
    kpos = jnp.arange(S)

    def block(args):
        qn, qp, n = args
        s = (jnp.einsum('bihd,bjhd->bhij', qn, k_nope, preferred_element_type=jnp.float32)
             + jnp.einsum('bihd,bjd->bhij', qp, k_pe, preferred_element_type=jnp.float32)) * scale
        qpos = n * Q_BLOCK + jnp.arange(Q_BLOCK)
        s = jnp.where(qpos[:, None] >= kpos[None, :], s, NEG_INF)
        return jnp.einsum('bhij,bjhd->bihd', jax.nn.softmax(s, axis=-1), v)

    o = lax.map(block, (qn_b, qp_b, jnp.arange(nb)))
    return o.transpose(1, 0, 2, 3, 4).reshape(B_, S, D_HEADS * D_V)

def mix_even(h, w_in, w_out, gla_w_gate_up, gla_b_gate, gla_norm):
    B_, S, _ = h.shape
    qa, ka, va, qb, kb, vb, rb, gb = split_cols(h @ w_in, L0_IN_SIZES)
    heads = lambda t: t.reshape(B_, S, A_HEADS, HEAD_DIM).transpose(0, 2, 1, 3)
    o_a = dilated_attention(heads(qa), heads(ka), heads(va))
    o_a = o_a.transpose(0, 2, 1, 3).reshape(B_, S, A_HEADS * HEAD_DIM)
    o_b = gla(qb, kb, vb, rb, gb, gla_w_gate_up, gla_b_gate, gla_norm)
    return jnp.concatenate([o_a, o_b], axis=-1).astype(h.dtype) @ w_out

def mix_odd(h, w_in, w_out, sinks, q_norm, w_uq, kv_norm, w_ukv):
    qc, kc, vc, c_q, c_kv, k_rope = split_cols(h @ w_in, L1_IN_SIZES)
    o_c = swa_sink_attention(qc, kc, vc, sinks)
    o_d = mla(c_q, c_kv, k_rope, q_norm, w_uq, kv_norm, w_ukv)
    return jnp.concatenate([o_c, o_d], axis=-1).astype(h.dtype) @ w_out

def swiglu(h, w_gate, w_up, w_down):
    return (jax.nn.silu(h @ w_gate) * (h @ w_up)) @ w_down

def second_inputs(seed: int = 0) -> dict:
    key = jax.random.key(seed)
    ks = jax.random.split(key, 24)
    nrm = lambda k, shape, fan_in: jax.random.normal(k, shape, jnp.float32) * fan_in ** -0.5
    gain = lambda k, shape: 1.0 + 0.02 * jax.random.normal(k, shape, jnp.float32)
    return {
        "x": jax.random.normal(ks[0], (BATCH, SEQ, D_MODEL), jnp.float32),
        "norm_mix_pre": gain(ks[1], (DEPTH, D_MODEL)),
        "norm_mix_post": gain(ks[2], (DEPTH, D_MODEL)),
        "norm_ffn_pre": gain(ks[3], (DEPTH, D_MODEL)),
        "norm_ffn_post": gain(ks[4], (DEPTH, D_MODEL)),
        "ffn_w_gate": nrm(ks[5], (DEPTH, D_MODEL, D_FF_2), D_MODEL),
        "ffn_w_up": nrm(ks[6], (DEPTH, D_MODEL, D_FF_2), D_MODEL),
        "ffn_w_down": nrm(ks[7], (DEPTH, D_FF_2, D_MODEL), D_FF_2),
        "ab_w_in": nrm(ks[8], (N_EVEN, D_MODEL, L0_IN), D_MODEL),
        "ab_w_out": nrm(ks[9], (N_EVEN, L0_MIX, D_MODEL), L0_MIX),
        "gla_w_gate_up": nrm(ks[10], (N_EVEN, B_GATE_RANK, B_HEADS * B_DK), B_GATE_RANK),
        "gla_b_gate": 0.1 * jax.random.normal(ks[11], (N_EVEN, B_HEADS * B_DK), jnp.float32),
        "gla_norm": gain(ks[12], (N_EVEN, B_DV)),
        "cd_w_in": nrm(ks[13], (N_ODD, D_MODEL, L1_IN), D_MODEL),
        "cd_w_out": nrm(ks[14], (N_ODD, L1_MIX, D_MODEL), L1_MIX),
        "swa_sinks": jax.random.normal(ks[15], (N_ODD, C_HEADS), jnp.float32),
        "mla_q_norm": gain(ks[16], (N_ODD, D_Q_RANK)),
        "mla_w_uq": nrm(ks[17], (N_ODD, D_Q_RANK, D_HEADS * (D_NOPE + D_ROPE)), D_Q_RANK),
        "mla_kv_norm": gain(ks[18], (N_ODD, D_KV_RANK)),
        "mla_w_ukv": nrm(ks[19], (N_ODD, D_KV_RANK, D_HEADS * (D_NOPE + D_V)), D_KV_RANK),
    }

def second_block(x, norm_mix_pre, norm_mix_post, norm_ffn_pre, norm_ffn_post,
              ffn_w_gate, ffn_w_up, ffn_w_down,
              ab_w_in, ab_w_out, gla_w_gate_up, gla_b_gate, gla_norm,
              cd_w_in, cd_w_out, swa_sinks, mla_q_norm, mla_w_uq, mla_kv_norm, mla_w_ukv):
    for layer in range(DEPTH):
        i = layer // 2
        h = rmsnorm(x, norm_mix_pre[layer])
        if layer % 2 == 0:
            y = mix_even(h, ab_w_in[i], ab_w_out[i], gla_w_gate_up[i], gla_b_gate[i], gla_norm[i])
        else:
            y = mix_odd(h, cd_w_in[i], cd_w_out[i], swa_sinks[i], mla_q_norm[i], mla_w_uq[i],
                        mla_kv_norm[i], mla_w_ukv[i])
        x = x + rmsnorm(y, norm_mix_post[layer]).astype(x.dtype)
        h = rmsnorm(x, norm_ffn_pre[layer])
        f = swiglu(h, ffn_w_gate[layer], ffn_w_up[layer], ffn_w_down[layer])
        x = x + rmsnorm(f, norm_ffn_post[layer]).astype(x.dtype)
    return x


def setup_inputs(seed=0):
    out = dict(first_inputs(seed))
    for name, value in second_inputs(seed + 1).items():
        if name != "x":
            out[name + "_2"] = value
    return out


def reference(
    x, meta, ln_in_g, ln_in_b, ffn1_w13, ffn1_w2, w_in, pool_w, pool_scale, conv_dw, conv_db,
    conv_ln_g, conv_ln_b, conv_pw, ret_gn_g, w_out, ffn2_w13, ffn2_w2, ln_g, ln_b,
    norm_mix_pre_2, norm_mix_post_2, norm_ffn_pre_2, norm_ffn_post_2, ffn_w_gate_2, ffn_w_up_2,
    ffn_w_down_2, ab_w_in_2, ab_w_out_2, gla_w_gate_up_2, gla_b_gate_2, gla_norm_2, cd_w_in_2,
    cd_w_out_2, swa_sinks_2, mla_q_norm_2, mla_w_uq_2, mla_kv_norm_2, mla_w_ukv_2,
):
    x = first_block(
        x, meta, ln_in_g, ln_in_b, ffn1_w13, ffn1_w2, w_in, pool_w, pool_scale, conv_dw,
        conv_db, conv_ln_g, conv_ln_b, conv_pw, ret_gn_g, w_out, ffn2_w13, ffn2_w2, ln_g, ln_b,
    )
    return second_block(
        x, norm_mix_pre_2, norm_mix_post_2, norm_ffn_pre_2, norm_ffn_post_2, ffn_w_gate_2,
        ffn_w_up_2, ffn_w_down_2, ab_w_in_2, ab_w_out_2, gla_w_gate_up_2, gla_b_gate_2,
        gla_norm_2, cd_w_in_2, cd_w_out_2, swa_sinks_2, mla_q_norm_2, mla_w_uq_2, mla_kv_norm_2,
        mla_w_ukv_2,
    )


_drawn_inputs = setup_inputs


def setup_inputs(seed=0):
    import zlib

    import numpy as np

    out = dict(_drawn_inputs(seed))
    spreads = {}
    factors = {'conv_db': 3.476,
     'conv_ln_b': 6.91,
     'norm_ffn_post_2': 3.329,
     'gla_norm_2': 3.473,
     'mla_q_norm_2': 8.0,
     'mla_kv_norm_2': 7.509}
    for name, (base, spread) in spreads.items():
        noise = np.random.default_rng([zlib.crc32(name.encode()), seed]).standard_normal(out[name].shape)
        drawn = base * np.exp(spread * noise) if base else spread * noise
        out[name] = __import__('jax').numpy.asarray(drawn.astype(out[name].dtype))
    for name, factor in factors.items():
        out[name] = (out[name] * factor).astype(out[name].dtype)
    return out
```

```python
from contextlib import ExitStack

import numpy as np

import concourse.bass as bass
from concourse import mybir

F32 = mybir.dt.float32
F32R = mybir.dt.float32r
I32 = mybir.dt.int32
ALU = mybir.AluOpType
ACT = mybir.ActivationFunctionType
AX = mybir.AxisListType

P = 128
D = 1024
KD = D // P
META = 16
SEQ = 256
T = META + SEQ
LAYERS = 2
FT = 22
ALPHA = (2.0 * LAYERS) ** 0.25
LN_EPS = 1e-5
RMS_EPS = 1e-6
HEADS = 4
TAPS = 31
KTOK = [(0, 128), (128, 128), (256, 16)]
UP_BLOCKS = 2 * KD
DOWN_BLOCKS = FT
SLOT = DOWN_BLOCKS * P
FFN_CHUNKS = FT + KD
IN_GROUPS = [2] * 10 + [1] * 2
OUT_CHUNKS = KD // 2
EVEN_GROUPS = [2] * 12 + [1]
ODD_GROUPS = [2] * 6
LAYER_CHUNKS = 2 * FFN_CHUNKS + len(IN_GROUPS) + OUT_CHUNKS
V_LN, V_PSC, V_CDB, V_CG, V_CB, V_GN, V_DW = 0, 48, 50, 52, 54, 56, 60
DVE_LINKS = 51
NV = V_DW + 2 * TAPS
U_ING, U_INB, U_RMS, U_GATEB, U_GLAN, U_QN, U_KVN = 0, 8, 16, 80, 82, 83, 86
NU = 88


class Seen:

    def __init__(self, per_layer):
        self.n, self.per, self.layer = {}, per_layer, None

    def at(self, sem, ahead):
        v = self.n.get(sem.name, 0) + ahead
        return v if self.layer is None else self.layer * self.per[sem.name] + v

    def skip(self, sem, by):
        self.n[sem.name] = self.n.get(sem.name, 0) + by

    def next(self, sem, by=1):
        self.skip(sem, by)
        return self.at(sem, 0)

    def enter(self, layer):
        self.layer, self.before = layer, dict(self.n)

    def leave(self):
        self.layer = None
        self.n = {s: self.before.get(s, 0) + LAYERS * self.per[s] for s in self.per}


class Stream:

    def __init__(self):
        self.c, self.layer = 0, None

    def value(self, ahead, pairs=0, plus=0):
        v = pairs * 2 + (self.c + ahead + plus)
        return v if self.layer is None else self.layer * LAYER_CHUNKS + v

    def loads(self, ahead, pairs=0):
        v = pairs * 16 + ((self.c + ahead) // 2 + 1) * 16
        return v if self.layer is None else self.layer * (8 * LAYER_CHUNKS) + v

    def slot(self, ahead):
        return (self.c + ahead) % 2

    def enter(self, layer):
        assert self.c == 0
        self.layer = layer

    def leave(self):
        assert self.c == LAYER_CHUNKS
        self.layer, self.c = None, LAYERS * LAYER_CHUNKS


def region(*spans):
    spans = [list(s) for s in spans]

    def take(size):
        size = -(-size // 32) * 32
        for s in spans:
            if s[1] - s[0] >= size:
                s[0] += size
                return s[0] - size
        raise AssertionError((size, spans))

    take.spans = spans
    return take


def pairs_of(eng, n, step):
    for j in range(2):
        step(0, j, False)
    with eng.Fori(1, n // 2 - 1) as i:
        for j in range(2):
            step(i, j, False)
    for j in range(2):
        step(n // 2 - 1, j, j == 1)


def forward(nc, a):
    with ExitStack() as ctx:
        cursor = [-(-nc.sbuf_base // 32) * 32]
        limit = nc.sbuf_usable_end
        T4 = T * 4
        S = SEQ

        def place(name, shape, dt=F32, offset=None):
            if offset is None:
                offset = cursor[0]
                cursor[0] += -(-int(np.prod(shape[1:])) * 4 // 32) * 32
                assert cursor[0] <= limit, (name, cursor[0], limit)
            return nc.alloc_sbuf_tensor_at(name, list(shape), dt, offset=offset)

        def placer(take):
            return lambda name, shape, dt=F32: place(name, shape, dt, take(int(np.prod(shape[1:])) * 4))

        raw = place("raw", [P, 2, SLOT])
        w_hi = place("w_hi", [P, 2, SLOT], F32R)
        w_lo = place("w_lo", [P, 2, SLOT], F32R)
        h = place("h", [P, KD, T])
        h_hi = place("h_hi", [P, KD * T + P], F32R)
        h_lo = place("h_lo", [P, KD * T + P], F32R)
        y = place("y", [P, KD, T])
        sq_at = cursor[0]
        sq = place("sq", [P, KD, T])
        ghi_at = cursor[0]
        g_hi = place("g_hi", [P, FT, T], F32R)
        glo_at = cursor[0]
        g_lo = place("g_lo", [P, FT, T], F32R)
        g_end = cursor[0]
        ones = place("ones", [P, P])
        ident = place("ident", [P, P])
        vec = place("vec", [P, LAYERS, NV])
        uvec = place("uvec", [P, NU])
        sinks = place("sinks", [P, 8])
        eps = place("eps", [P, 2])
        std = place("std", [P, T])
        rstd = place("rstd", [P, T])
        sig = place("sig", [P, 2, T])
        gf = place("gf", [P, 2, T])
        decay_at = cursor[0]
        decay = place("decay", [P, 3, HEADS, T])
        rope_cos = place("rope_cos", [P, T])
        rope_sin = place("rope_sin", [P, T])
        inv_count = place("inv_count", [P, 2, T])
        mixw = place("mixw", [P, 6, P])
        rest_at = cursor[0]

        spans = ((ghi_at + KD * T4, glo_at), (glo_at + KD * T4, g_end), (rest_at, limit))
        one = placer(region(*spans))
        xpad = one("xpad", [P, 2, 16 + T])
        upad = one("upad", [P, 2, TAPS - 1 + T])
        ca = one("ca", [P, 2, T])
        cg = one("cg", [P, 2, T])
        qk_raw = one("qk_raw", [P, 2, T])
        qk_swap = one("qk_swap", [P, 2, T])
        qT = one("qT", [P, HEADS, T])
        kT = one("kT", [P, HEADS, T])
        v_tok = one("v_tok", [P, 3, HEADS * P])
        gate_s = one("gate_s", [P, HEADS, T])
        conv_y = one("conv_y", [P, 2, T])
        conv_sq = one("conv_sq", [P, 2, T])
        pool_y = one("pool_y", [P, 2, T])
        o_c = one("o_c", [P, HEADS, T])
        o_rstd = one("o_rstd", [P, HEADS, T])
        win = [place(f"win{i}", [P, 2, 16 + T], offset=sq_at + i * 2 * (16 + T) * 4) for i in range(3)]
        pT = place("pT", [P, 2, 3, T], offset=sq_at)
        o_sq = place("o_sq", [P, HEADS, T], offset=sq_at)
        o_std = place("o_std", [P, HEADS, T], offset=sq_at + HEADS * T4)
        x_tok = place("x_tok", [P, 3, D], offset=ghi_at)

        table = placer(region((decay_at, rest_at)))
        rel_a = table("rel_a", [P, 2, S])
        logc = table("logc", [P, 2, S])
        rel_c = table("rel_c", [P, 2, S])
        mask_d = table("mask_d", [P, 2, S])
        tril = table("tril", [P, P])
        scan_m = table("scan_m", [P, S])
        gup = table("gup", [P, 2, P])
        rcos = table("rcos", [P, S])
        rsin = table("rsin", [P, S])
        both_at = region(*spans)
        both = placer(both_at)
        att_s = both("att_s", [P, 2, 2, S + 1])
        att_p = both("att_p", [P, 2, 2, S + 1])
        att_pT = both("att_pT", [P, 2, 4, P])
        att_max = both("att_max", [P, 2, 2])
        att_sum = both("att_sum", [P, 2, 2])
        att_inv = both("att_inv", [P, 2, 2])
        even = placer(region(*both_at.spans))
        odd = placer(region(*both_at.spans))
        qa = even("qa", [P, 4, S])
        ka = even("ka", [P, 4, S])
        va = even("va", [P, 2, 512])
        qb = even("qb", [P, 2, S])
        kb = even("kb", [P, 2, S])
        vb = even("vb", [P, 2, 512])
        rb = even("rb", [P, 4, S])
        gb = even("gb", [P, S])
        bc = even("bc", [P, 2, S])
        khat = even("khat", [P, 2, S])
        qhat = even("qhat", [P, 2, S])
        att = even("att", [P, 2, 4, P])
        za = place("za", [P, 2, S], offset=sq_at)
        zb = place("zb", [P, 2, S], offset=sq_at + 2048)
        dmid = place("dmid", [P, 2, S], offset=sq_at + 4096)
        dlast = place("dlast", [P, 2, S], offset=sq_at + 6144)
        k_tok = place("k_tok", [P, 2, 2, P], offset=sq_at)
        state = place("state", [P, 3, 2, P], offset=sq_at + 2048)
        dec = place("dec", [P, 2, 4], offset=sq_at + 5120)
        g_sq = place("g_sq", [P, 4, S], offset=sq_at)
        g_std = place("g_std", [P, 4, S], offset=sq_at + 4096)
        qc = odd("qc", [P, 4, S])
        kdup = odd("kdup", [P, 2, S])
        vc = odd("vc", [P, 2, P])
        qd = odd("qd", [P, 8, S])
        kd = odd("kd", [P, 8, S])
        vd = odd("vd", [P, 2, 512])
        rt = odd("rt", [P, 2, S])
        cqkv = place("cqkv", [P, 5, S], offset=sq_at)
        c_sq = place("c_sq", [P, 3, S], offset=sq_at + 5120)

        ps = [ctx.enter_context(nc.psum_tensor(f"bank{i}", [P, 512], F32)) for i in range(8)]

        per_layer = {}

        def sem(name, in_layer=0):
            s = ctx.enter_context(nc.semaphore(name))
            per_layer[s.name] = in_layer
            return s

        loaded = [sem(f"raw_loaded{i}") for i in range(2)]
        w_hi_done = sem("w_hi_done")
        w_ready = sem("w_ready")
        chunk_used = sem("chunk_used")
        tile_ready = sem("tile_ready", 10 + OUT_CHUNKS)
        x_loaded = sem("x_loaded")
        consts_loaded = sem("consts_loaded")
        consts_set = sem("consts_set")
        tables_loaded = sem("tables_loaded")
        mixw_loaded = sem("mixw_loaded", 16)
        xT_ready = sem("xT_ready")
        y_ready = sem("y_ready", 3 * KD)
        mean_ready = sem("mean_ready", 3)
        centered = sem("centered", 3 * KD)
        squared = sem("squared", 3 * KD)
        var_ready = sem("var_ready", 3)
        std_ready = sem("std_ready", 3)
        normed = sem("normed", 3 * KD)
        affine = sem("affine", 3 * KD)
        h_done = sem("h_done", 3)
        h_ready = sem("h_ready", 3 * KD)
        up_free = sem("up_free", 2 * FT)
        silu_ready = sem("silu_ready", 2 * FT)
        g_hi_done = sem("g_hi_done", 2 * FT)
        g_ready = sem("g_ready", 2 * FT)
        z_copied = sem("z_copied", 22)
        rope_ready = sem("rope_ready", 2 * HEADS)
        pool_in = sem("pool_in", 1)
        pool_mixed = sem("pool_mixed", 2)
        small_done = sem("small_done", 4)
        conv_done = sem("conv_done", 2)
        conv_mean = sem("conv_mean", 1)
        conv_cent = sem("conv_cent", 2)
        conv_sqd = sem("conv_sqd", 2)
        conv_var = sem("conv_var", 1)
        conv_std = sem("conv_std", 1)
        conv_nrm = sem("conv_nrm", 2)
        conv_act = sem("conv_act", 2)
        conv_pwd = sem("conv_pwd", 2)
        ret_s = sem("ret_s", 3 * HEADS)
        ret_p = sem("ret_p", 3 * HEADS)
        ret_o = sem("ret_o", HEADS)
        ret_oc = sem("ret_oc", HEADS)
        ret_mean = sem("ret_mean", HEADS)
        ret_cent = sem("ret_cent", HEADS)
        ret_sqd = sem("ret_sqd", HEADS)
        ret_var = sem("ret_var", HEADS)
        ret_std = sem("ret_std", HEADS)
        ret_done = sem("ret_done", 1)
        mix_hi = sem("mix_hi", KD)
        mix_ready = sem("mix_ready", KD)
        x_ready = sem("x_ready")
        z2_copied = sem("z2_copied")
        at_s = sem("at_s")
        at_max = sem("at_max")
        at_exp = sem("at_exp")
        at_norm = sem("at_norm")
        at_t = sem("at_t")
        at_tc = sem("at_tc")
        at_o = sem("at_o")
        at_done = sem("at_done")
        gate_ready = sem("gate_ready")
        gate_log = sem("gate_log")
        gate_cum = sem("gate_cum")
        gate_exp = sem("gate_exp")
        gla_in = sem("gla_in")
        gla_s = sem("gla_s")
        gla_kt = sem("gla_kt")
        gla_att = sem("gla_att")
        gla_ktc = sem("gla_ktc")
        gla_ds = sem("gla_ds")
        gla_state = sem("gla_state")
        gla_o = sem("gla_o")
        gla_sqd = sem("gla_sqd")
        gla_var = sem("gla_var")
        gla_std = sem("gla_std")
        gla_done = sem("gla_done")
        c_sqd = sem("c_sqd")
        c_var = sem("c_var")
        c_std = sem("c_std")
        c_nrm = sem("c_nrm")
        c_hi = sem("c_hi")
        c_ready = sem("c_ready")
        qd_ready = sem("qd_ready")
        qd_copied = sem("qd_copied")
        qd_roped = sem("qd_roped")
        kn_ready = sem("kn_ready")
        kn_copied = sem("kn_copied")
        vd_ready = sem("vd_ready")
        vd_copied = sem("vd_copied")
        kpe_roped = sem("kpe_roped")
        kd_ready = sem("kd_ready")
        out_t = sem("out_t")
        out_c = sem("out_c")
        stored = sem("stored")
        dve_seq = sem("dve_seq", DVE_LINKS)
        act_seq = sem("act_seq")
        block = ctx.enter_context(nc.Block())

        def hs(buf, k, lo=0, n=T):
            return buf[:, k * T + lo:k * T + lo + n]

        def half(buf, hd, lo, n):
            return buf[64 * (hd % 2):64 * (hd % 2) + 64, hd // 2, lo:lo + n]

        def xk(k):
            return h[:, k, META:T]

        UNITS = [(t, j) for j in range(4) for t in range(2)]
        QK = range(6, 14)
        VALUES = range(14, 18)
        EVEN_TOKEN = (8, 9, 10, 11, 16, 17, 18, 19)
        ODD_TOKEN = (5,)

        @block.sync
        def _(sp):
            st = Stream()

            def load(src, blocks, ahead, pairs=0):
                slot = st.slot(ahead)
                sp.wait_ge(w_ready, st.value(ahead, pairs, 1))
                sp.dma_start(raw[:, slot, 0:blocks * P], src).then_inc(loaded[slot], 16)

            def ffn(i):
                for name, n, blocks in (("up_w", FT, UP_BLOCKS), ("down_w", KD, DOWN_BLOCKS)):
                    src = a[name].rearrange("f c p n -> (f c) p n")
                    with sp.Fori(0, n // 2) as c:
                        for j in range(2):
                            load(src[bass.ds(c * 2 + i * n + j, 1)].rearrange("a p n -> (a p) n"), blocks, j, c)
                    st.c += n

            def straight(chunks):
                for i, (src, blocks) in enumerate(chunks):
                    load(src, blocks, i)
                st.c += len(chunks)

            with sp.Fori(0, LAYERS) as l:
                st.enter(l)
                ffn(l * 2)
                src = a["in_w"][bass.ds(l, 1)].rearrange("a c p n -> (a c) p n")
                straight([(src[c, :, 0:n * KD * P], n * KD) for c, n in enumerate(IN_GROUPS)])
                src = a["out_w"][bass.ds(l, 1)].rearrange("a c p n -> (a c) p n")
                straight([(src[c], 2 * KD) for c in range(OUT_CHUNKS)])
                ffn(l * 2 + 1)
            st.leave()
            straight([(a["even_w"][c, :, 0:n * KD * P], n * KD) for c, n in enumerate(EVEN_GROUPS)])
            straight([(a["out_w"][2, c], 2 * KD) for c in range(OUT_CHUNKS)])
            ffn(4)
            straight([(a["odd_w"][c, :, 0:n * KD * P], n * KD) for c, n in enumerate(ODD_GROUPS)])
            straight([(a["uq_w"][c], 12) for c in range(2)] + [(a["ukv_w"], 16)])
            straight([(a["out_w"][3, c], 2 * KD) for c in range(OUT_CHUNKS)])
            ffn(5)
            for t in range(2):
                sp.wait_ge(out_c, KD * (t + 1))
                sp.dma_start(a["out"][t * P:(t + 1) * P, :], x_tok[:, t, :]).then_inc(stored, 16)
            sp.wait_ge(stored, 32)

        @block.gpsimd
        def _(pool):
            seen = Seen(per_layer)
            pool.dma_start(x_tok[0:META, 0, :], a["meta"]).then_inc(x_loaded, 16)
            pool.dma_start(x_tok[META:P, 0, :], a["x"][0:P - META, :]).then_inc(x_loaded, 16)
            pool.dma_start(x_tok[:, 1, :], a["x"][P - META:2 * P - META, :]).then_inc(x_loaded, 16)
            pool.dma_start(x_tok[0:META, 2, :], a["x"][2 * P - META:SEQ, :]).then_inc(x_loaded, 16)
            pool.dma_start(ident[:], a["ident"]).then_inc(x_loaded, 16)
            for dst, name in ((vec, "vec"), (uvec, "uvec"), (decay, "decay"), (rope_cos, "rope_cos"),
                              (rope_sin, "rope_sin"), (inv_count, "inv_count"), (sinks, "sinks")):
                pool.dma_start(dst[:], a[name]).then_inc(consts_loaded, 16)
            with pool.Fori(0, LAYERS) as l:
                seen.enter(l)
                pool.wait_ge(h_ready, l * (3 * KD) + KD)
                pool.dma_start(mixw[:], a["mixw"][bass.ds(l, 1)].rearrange("a p b n -> (a p) b n"))\
                    .then_inc(mixw_loaded, 16)
            pool.wait_ge(h_ready, KD + (LAYERS - 1) * 3 * KD + 2 * KD)
            for dst, name in ((rel_a, "rel_a"), (logc, "logc"), (rel_c, "rel_c"), (mask_d, "mask_d"),
                              (tril, "tril"), (scan_m, "scan_m"), (gup, "gup"), (rcos, "rcos"), (rsin, "rsin")):
                pool.dma_start(dst[:], a[name]).then_inc(tables_loaded, 16)

        @block.tensor
        def _(pe):
            seen, st = Seen(per_layer), Stream()

            def mm3(out, w, x, first, last):
                pe.matmul(out, w[0], x[0], start=first, stop=False)
                pe.matmul(out, w[0], x[1], start=False, stop=False)
                return pe.matmul(out, w[1], x[0], start=False, stop=last)

            def wpair(slot, b, n=1):
                return w_hi[:, slot, b * P:(b + n) * P], w_lo[:, slot, b * P:(b + n) * P]

            def hpair(k, lo=0, n=T):
                return hs(h_hi, k, lo, n), hs(h_lo, k, lo, n)

            def chunk_is_split(ahead, pairs=0):
                return st.value(ahead, pairs, 3)

            def squares_sum(n=T):
                for k in range(KD):
                    pe.wait_ge(squared, seen.next(squared))
                    last = pe.matmul(ps[7][:, 0:n], ones[:], sq[:, k, 0:n], start=k == 0, stop=k == KD - 1)
                last.then_inc(var_ready, 1)

            def tile_sum(m, n, first=False, stop=False):
                if isinstance(m, int):
                    tile, square = y[:, m, 0:n], sq[:, m, 0:n]
                else:
                    tile = y[:, bass.ds(m, 1), 0:n].rearrange("p a n -> p (a n)")
                    square = sq[:, bass.ds(m, 1), 0:n].rearrange("p a n -> p (a n)")
                if n == T:
                    pe.wait_ge(y_ready, seen.at(y_ready, m + 1))
                    last = pe.matmul(ps[6][:, 0:n], ones[:], tile, start=first, stop=stop)
                else:
                    pe.wait_ge(squared, seen.at(squared, m + 1))
                    last = pe.matmul(ps[7][:, 0:n], ones[:], square, start=first, stop=stop)
                if stop:
                    last.then_inc(mean_ready if n == T else var_ready, 1)
                    seen.skip(y_ready, KD)
                    if n < T:
                        seen.skip(squared, KD)

            def first_chunk(tiles, banks, n, slot):
                for k in range(KD):
                    pe.wait_ge(h_ready, seen.next(h_ready))
                    lasts = [mm3(bank[:, 0:n], wpair(slot, e * KD + k), hpair(k, 0, n), k == 0, k == KD - 1)
                             for e, bank in zip(range(tiles), banks)]
                return lasts

            def ffn(n=T):
                def up(i, j):
                    slot = st.slot(j)
                    pe.wait_ge(w_ready, chunk_is_split(j, i))
                    pe.wait_ge(up_free, seen.at(up_free, i * 2 + (j + 1)))
                    if isinstance(i, int) and (i, j) == (0, 0):
                        last = first_chunk(2, ps[0:2], n, slot)[-1]
                    else:
                        for e in range(2):
                            for k in range(KD):
                                last = mm3(ps[2 * j + e][:, 0:n], wpair(slot, e * KD + k), hpair(k, 0, n),
                                           k == 0, k == KD - 1)
                    last.then_inc(chunk_used, 1)

                def down(i, j):
                    slot = st.slot(j)
                    pe.wait_ge(w_ready, chunk_is_split(j, i))
                    pe.wait_ge(y_ready, seen.at(y_ready, i * 2 + (j - 1)))
                    if isinstance(i, int) and (i, j) == (0, 0):
                        pe.wait_ge(g_ready, seen.at(g_ready, FT - 2))
                    for k in range(FT):
                        if isinstance(i, int) and (i, j, k) == (0, 0, FT - 2):
                            pe.wait_ge(g_ready, seen.at(g_ready, FT))
                        last = mm3(ps[4 + j][:, 0:n], wpair(slot, k), (g_hi[:, k, 0:n], g_lo[:, k, 0:n]),
                                   k == 0, k == FT - 1)
                    last.then_inc(chunk_used, 1)
                    if j == 1 or not isinstance(i, int):
                        tile_sum(i * 2 + (j - 1), n, first=isinstance(i, int))

                up(0, 0)
                up(0, 1)
                with pe.Fori(1, FT // 2) as i:
                    up(i, 0)
                    up(i, 1)
                st.c += FT
                seen.skip(up_free, FT)
                down(0, 0)
                down(0, 1)
                with pe.Fori(1, KD // 2) as i:
                    down(i, 0)
                    down(i, 1)
                st.c += KD
                seen.skip(g_ready, FT)
                tile_sum(KD - 1, n, stop=True)

            def project_out(n=T):
                pe.wait_ge(mix_ready, seen.next(mix_ready, KD))
                for c in range(OUT_CHUNKS):
                    pe.wait_ge(w_ready, chunk_is_split(c))
                    for e in range(2):
                        pe.wait_ge(y_ready, seen.at(y_ready, 2 * c + e - 1))
                        for k in range(KD):
                            last = mm3(ps[4 + e][:, 0:n], wpair(st.slot(c), e * KD + k),
                                       (g_hi[:, k, 0:n], g_lo[:, k, 0:n]), k == 0, k == KD - 1)
                        last.then_inc(chunk_used if e else tile_ready, 1)
                        if 2 * c + e:
                            tile_sum(2 * c + e - 1, n, first=2 * c + e == 1)
                st.c += OUT_CHUNKS
                tile_sum(KD - 1, n, stop=True)

            def in_tiles(sizes, by_token, token_tiles, copied, n):
                z = 0
                for c, tiles in enumerate(sizes):
                    pe.wait_ge(w_ready, chunk_is_split(c))
                    if c == 0:
                        for e, last in enumerate(first_chunk(tiles, ps, n, st.slot(c))):
                            last.then_inc(chunk_used if e == tiles - 1 else tile_ready, 1)
                        z = tiles
                        continue
                    for e in range(tiles):
                        bank = ps[z % 4]
                        if z >= 4:
                            pe.wait_ge(copied, seen.at(copied, z - 3))
                        if z in by_token:
                            for t in range(token_tiles):
                                for k in range(KD):
                                    last = mm3(bank[:, t * P:(t + 1) * P], hpair(k, t * P, P),
                                               wpair(st.slot(c), e * KD + k), k == 0, k == KD - 1)
                        else:
                            for k in range(KD):
                                last = mm3(bank[:, 0:n], wpair(st.slot(c), e * KD + k), hpair(k, 0, n),
                                           k == 0, k == KD - 1)
                        last.then_inc(chunk_used if e == tiles - 1 else tile_ready, 1)
                        z += 1
                st.c += len(sizes)
                pe.wait_ge(copied, seen.next(copied, z))

            pe.wait_ge(x_loaded, 80)
            for k in range(KD):
                if k >= 4:
                    pe.wait_ge(y_ready, k - 3)
                for t, (lo, m) in enumerate(KTOK):
                    last = pe.transpose(ps[k % 4][:, lo:lo + m], x_tok[0:m, t, k * P:(k + 1) * P], ident[0:m, 0:m])
                last.then_inc(xT_ready, 1)
            pe.wait_ge(consts_set, 1)
            for k in range(KD):
                tile_sum(k, T, k == 0, k == KD - 1)
            squares_sum()

            with pe.Fori(0, LAYERS) as l:
                seen.enter(l)
                st.enter(l)
                ffn()
                squares_sum()
                in_tiles(IN_GROUPS, VALUES, 3, z_copied, T)
                pe.wait_ge(mixw_loaded, seen.next(mixw_loaded, 16))
                pe.wait_ge(pool_in, seen.next(pool_in))
                for j in range(2):
                    pe.matmul(ps[j][:, 0:T], mixw[:, j, :], pool_y[:, j, :], start=True, stop=True)\
                        .then_inc(pool_mixed, 1)
                for j in range(2):
                    pe.wait_ge(conv_done, seen.next(conv_done))
                    last = pe.matmul(ps[6][:, 0:T], ones[:], conv_y[:, j, :], start=j == 0, stop=j == 1)
                last.then_inc(conv_mean, 1)
                for j in range(2):
                    pe.wait_ge(conv_sqd, seen.next(conv_sqd))
                    last = pe.matmul(ps[7][:, 0:T], ones[:], conv_sq[:, j, :], start=j == 0, stop=j == 1)
                last.then_inc(conv_var, 1)
                pe.wait_ge(rope_ready, seen.next(rope_ready, 2 * HEADS))
                pe.wait_ge(small_done, seen.next(small_done, 2))

                def values(hd):
                    for t, (lo, m) in enumerate(KTOK):
                        pe.wait_ge(ret_p, seen.at(ret_p, 3 * hd + t + 1))
                        last = pe.matmul(ps[4 + hd % 2][:, 0:T], v_tok[0:m, t, hd * P:(hd + 1) * P],
                                         pT[0:m, hd % 2, t, :], start=t == 0, stop=t == 2)
                    last.then_inc(ret_o, 1)

                for hd in range(HEADS + 1):
                    if hd < HEADS:
                        for t, (lo, m) in enumerate(KTOK):
                            n = 3 * hd + t
                            if n >= 4:
                                pe.wait_ge(ret_p, seen.at(ret_p, n - 3))
                            pe.matmul(ps[n % 4][0:m, 0:T], kT[:, hd, lo:lo + m], qT[:, hd, :],
                                      start=True, stop=True).then_inc(ret_s, 1)
                    if hd >= 3:
                        pe.wait_ge(ret_oc, seen.at(ret_oc, hd - 2))
                    if hd >= 1:
                        values(hd - 1)
                seen.skip(ret_p, 3 * HEADS)
                for hd in range(HEADS):
                    pe.wait_ge(ret_oc, seen.next(ret_oc))
                    pe.matmul(ps[hd][:, 0:T], ones[:], o_c[:, hd, :], start=True, stop=True).then_inc(ret_mean, 1)
                pe.wait_ge(conv_act, seen.next(conv_act, 2))
                for j in range(2):
                    for k in range(2):
                        last = pe.matmul(ps[6 + j][:, 0:T], mixw[:, 2 + 2 * k + j, :], conv_y[:, k, :],
                                         start=k == 0, stop=k == 1)
                    last.then_inc(conv_pwd, 1)
                pe.wait_ge(small_done, seen.next(small_done, 2))
                for hd in range(HEADS):
                    pe.wait_ge(ret_sqd, seen.next(ret_sqd))
                    pe.matmul(ps[4 + hd][:, 0:T], ones[:], o_sq[:, hd, :], start=True, stop=True)\
                        .then_inc(ret_var, 1)
                project_out()
                squares_sum()
                ffn()
                squares_sum()
            seen.leave()
            st.leave()

            def attention(q, k, v):
                def scores(u):
                    t, j = UNITS[u]
                    for e in range(2):
                        last = pe.matmul(ps[2 * (u % 2) + e][:, 0:P * (t + 1)], q(2 * j + e, t),
                                         k(2 * j + e, t), start=True, stop=True)
                    last.then_inc(at_s, 1)

                def turn(u):
                    t, j = UNITS[u]
                    pe.wait_ge(at_norm, seen.next(at_norm))
                    for e in range(2):
                        for kt in range(t + 1):
                            last = pe.transpose(ps[4 + u % 2][:, (2 * e + kt) * P:(2 * e + kt + 1) * P],
                                                att_p[:, u % 2, e, 1 + kt * P:1 + (kt + 1) * P], ident[:])
                    last.then_inc(at_t, 1)

                def values(u):
                    t, j = UNITS[u]
                    pe.wait_ge(at_tc, seen.next(at_tc))
                    if u >= 2:
                        pe.wait_ge(at_done, seen.at(at_done, u - 1))
                    for e in range(2):
                        for kt in range(t + 1):
                            last = pe.matmul(ps[6 + u % 2][64 * e:64 * e + 64, 0:P], v(2 * j + e, kt),
                                             att_pT[:, u % 2, 2 * e + kt, :], start=kt == 0, stop=kt == t)
                    last.then_inc(at_o, 1)

                for u in range(len(UNITS) + 2):
                    if u < len(UNITS):
                        scores(u)
                    if 1 <= u <= len(UNITS):
                        turn(u - 1)
                    if u >= 2:
                        values(u - 2)
                pe.wait_ge(at_done, seen.next(at_done, len(UNITS)))

            pe.wait_ge(tables_loaded, 16 * 9)
            seen.skip(h_ready, KD)
            squares_sum(S)
            in_tiles(EVEN_GROUPS, EVEN_TOKEN, 2, z2_copied, S)
            for j in range(2):
                last = pe.matmul(ps[6 + j][:, 0:S], gup[0:16, j, :], gb[0:16, :], start=True, stop=True)
            last.then_inc(gate_ready, 1)
            attention(lambda hd, t: half(qa, hd, t * P, P), lambda hd, t: half(ka, hd, 0, P * (t + 1)),
                      lambda hd, kt: va[:, kt, hd * 64:hd * 64 + 64])
            pe.wait_ge(gla_in, 1)
            for t in range(2):
                for hd in range(4):
                    last = pe.matmul(ps[2 * (hd % 2) + t][:, (hd // 2) * P:(hd // 2 + 1) * P], half(kb, hd, t * P, P),
                                     half(qb, hd, t * P, P), start=True, stop=True)
            last.then_inc(gla_s, 1)
            for t in range(2):
                for j in range(2):
                    last = pe.transpose(ps[7][:, (2 * t + j) * P:(2 * t + j + 1) * P],
                                        khat[:, j, t * P:(t + 1) * P], ident[:])
            last.then_inc(gla_kt, 1)
            pe.wait_ge(gla_ktc, 1)
            for n in range(3):
                r = 64 * (n % 2)
                for hd in range(4):
                    e = 64 * (hd % 2)
                    last = pe.matmul(ps[4 + n][e:e + 64, (hd // 2) * P:(hd // 2 + 1) * P],
                                     k_tok[r:r + 64, n // 2, hd // 2, e:e + 64],
                                     vb[r:r + 64, n // 2, hd * P:(hd + 1) * P], start=True, stop=True)
            last.then_inc(gla_ds, 1)
            pe.wait_ge(gla_att, 1)
            pe.wait_ge(gla_state, 1)
            for hd in range(4):
                bank = ps[4 + hd]
                for t in range(2):
                    o = t * P
                    pe.matmul(bank[:, o:o + P], vb[:, t, hd * P:(hd + 1) * P], att[:, t, hd, :],
                              start=True, stop=False)
                    across = (1,) if t == 0 else (2, 3)
                    for n in across:
                        o = 64 * n
                        last = pe.matmul(bank[:, o:o + 64], half(state[:, n - 1], hd, 0, P),
                                         half(qhat, hd, 64 * n, 64), start=False, stop=n == across[-1])
            last.then_inc(gla_o, 1)
            for hd in range(4):
                pe.wait_ge(gla_sqd, hd + 1)
                pe.matmul(ps[hd][:, 0:S], ones[:], g_sq[:, hd, :], start=True, stop=True).then_inc(gla_var, 1)
            project_out(S)
            squares_sum(S)
            ffn(S)

            squares_sum(S)
            in_tiles(ODD_GROUPS, ODD_TOKEN, 2, z2_copied, S)
            attention(lambda hd, t: half(qc, hd, t * P, P),
                      lambda hd, t: kdup[64 * (hd % 2):64 * (hd % 2) + 64, hd // 4, 0:P * (t + 1)],
                      lambda hd, kt: vc[:, kt, (hd // 4) * 64:(hd // 4) * 64 + 64])
            for g, n in enumerate((3, 2)):
                pe.wait_ge(c_sqd, g + 1)
                for k in range(n):
                    last = pe.matmul(ps[6 + g][:, 0:S], ones[:], c_sq[:, k, :], start=k == 0, stop=k == n - 1)
                last.then_inc(c_var, 1)
            pe.wait_ge(c_ready, 5)
            for c in range(2):
                pe.wait_ge(w_ready, chunk_is_split(c))
                for e in range(4):
                    z = 4 * c + e
                    if z >= 4:
                        pe.wait_ge(qd_copied, z - 3)
                    for k in range(3):
                        last = mm3(ps[z % 4][:, 0:S], wpair(st.slot(c), 3 * e + k), hpair(k, 0, S), k == 0, k == 2)
                    last.then_inc(chunk_used if e == 3 else qd_ready, 1)
            pe.wait_ge(w_ready, chunk_is_split(2))
            for j in range(4):
                if j >= 2:
                    pe.wait_ge(kn_copied, j - 1)
                for k in range(2):
                    last = mm3(ps[4 + j % 2][:, 0:S], wpair(st.slot(2), 8 * k + j), hpair(3 + k, 0, S), k == 0, k == 1)
                last.then_inc(kn_ready, 1)
            for t in range(2):
                for k in range(2):
                    last = mm3(ps[6 + t][:, 0:512], hpair(3 + k, t * P, P), wpair(st.slot(2), 8 * k + 4, 4),
                               k == 0, k == 1)
                last.then_inc(chunk_used if t else vd_ready, 1)
            st.c += 3
            pe.wait_ge(qd_roped, 8)
            pe.wait_ge(kn_copied, 4)
            pe.wait_ge(vd_copied, 2)
            pe.wait_ge(kd_ready, 1)
            attention(lambda hd, t: qd[0:96, hd, t * P:(t + 1) * P], lambda hd, t: kd[0:96, hd, 0:P * (t + 1)],
                      lambda hd, kt: vd[:, kt, hd * 64:hd * 64 + 64])
            project_out(S)
            squares_sum(S)
            ffn(S)
            pe.wait_ge(x_ready, 3 * KD)
            pe.wait_ge(x_ready, 4 * KD)
            for t in range(2):
                for k in range(KD):
                    n = t * KD + k
                    if n >= 8:
                        pe.wait_ge(out_c, n - 7)
                    pe.transpose(ps[n % 8][:, 0:P], h[:, k, META + t * P:META + (t + 1) * P], ident[:])\
                        .then_inc(out_t, 1)

        @block.scalar
        def _(act):
            seen, st = Seen(per_layer), Stream()

            def split_next(blocks, pairs=0, ahead=1):
                if blocks:
                    slot = st.slot(ahead)
                    act.wait_ge(loaded[slot], st.loads(ahead, pairs))
                    act.wait_ge(chunk_used, st.value(ahead, pairs))
                    act.activation(w_hi[:, slot, 0:blocks * P], raw[:, slot, 0:blocks * P], ACT.Copy)\
                        .then_inc(w_hi_done, 1)

            def vcol(l, col):
                return vec[:, bass.ds(l, 1), col:col + 1].rearrange("p a b -> p (a b)")

            def squares(source, ready, n):
                for k in range(KD):
                    if ready is not None:
                        act.wait_ge(ready, seen.next(ready))
                    act.activation(sq[:, k, 0:n], source(k), ACT.Square).then_inc(squared, 1)

            def deviation(n):
                act.wait_ge(var_ready, seen.next(var_ready))
                act.activation(std[:, 0:n], ps[7][:, 0:n], ACT.Sqrt, scale=1.0 / D,
                               bias=eps[:, 0:1] if n == T else eps[:, 1:2]).then_inc(std_ready, 1)

            def layer_norm(bias, early):
                split_next(early)
                squares(lambda k: y[:, k, :], centered, T)
                deviation(T)
                for k in range(KD):
                    act.wait_ge(normed, seen.next(normed))
                    act.activation(hs(h_hi, k), y[:, k, :], ACT.Identity, bias=bias(k)).then_inc(affine, 1)
                for k in range(KD):
                    last = act.activation(h[:, k, :], y[:, k, :], ACT.Identity, bias=bias(k))
                last.then_inc(h_done, 1)

            def pre_norm(ready):
                squares(xk, ready, S)
                deviation(S)
                for k in range(KD):
                    act.wait_ge(normed, seen.next(normed))
                    act.activation(hs(h_hi, k, 0, S), y[:, k, 0:S], ACT.Copy).then_inc(affine, 1)

            def post_norm(early):
                split_next(early)
                deviation(S)
                seen.skip(normed, KD)

            def square_tile(m):
                act.wait_ge(y_ready, seen.at(y_ready, m + 1))
                f = bass.ds(m, 1)
                act.activation(sq[:, f, 0:S], y[:, f, 0:S], ACT.Square).then_inc(squared, 1)

            def ffn(after, n=T):
                def up(i, j, last):
                    if not (isinstance(i, int) and (i, j) == (0, 0)):
                        split_next(DOWN_BLOCKS if last else UP_BLOCKS, i, j + 1)
                    act.wait_ge(chunk_used, st.value(j, i, 2))
                    act.activation(sig[:, j, 0:n], ps[2 * j][:, 0:n], ACT.Silu).then_inc(silu_ready, 1)

                def down(i, j, last):
                    split_next(after if last else DOWN_BLOCKS, i, j + 1)
                    if n < T:
                        square_tile(i * 2 + j)

                pairs_of(act, FT, up)
                st.c += FT
                pairs_of(act, KD, down)
                st.c += KD
                seen.skip(y_ready, KD)

            def tile_is_ready(ahead, e, tiles):
                if e == tiles - 1:
                    act.wait_ge(chunk_used, st.value(ahead, 0, 2))
                else:
                    act.wait_ge(tile_ready, seen.next(tile_ready))

            def in_tiles(sizes, after, copy):
                z = 0
                for c, tiles in enumerate(sizes):
                    if c:
                        split_next(sizes[c + 1] * KD if c + 1 < len(sizes) else after, 0, c + 1)
                    for e in range(tiles):
                        tile_is_ready(c, e, tiles)
                        copy(z, ps[z % 4])
                        z += 1
                st.c += len(sizes)

            def mix_split(k, n):
                act.activation(g_hi[:, k, 0:n], y[:, k, 0:n], ACT.Copy).then_inc(mix_hi, 1)

            def project_out(n=T):
                for c in range(OUT_CHUNKS):
                    split_next(2 * KD if c + 1 < OUT_CHUNKS else UP_BLOCKS, 0, c + 1)
                    if n < T:
                        square_tile(2 * c)
                        square_tile(2 * c + 1)
                seen.skip(tile_ready, OUT_CHUNKS)
                seen.skip(y_ready, KD)
                st.c += OUT_CHUNKS

            seen.skip(y_ready, KD)
            act.wait_ge(loaded[0], 16)
            act.activation(w_hi[:, 0, 0:UP_BLOCKS * P], raw[:, 0, 0:UP_BLOCKS * P], ACT.Copy)\
                .then_inc(w_hi_done, 1)
            act.wait_ge(consts_loaded, 16 * 7)
            act.wait_ge(consts_set, 1)
            layer_norm(lambda k: uvec[:, U_INB + k:U_INB + k + 1], UP_BLOCKS)
            with act.Fori(0, LAYERS) as l:
                seen.enter(l)
                st.enter(l)
                ffn(IN_GROUPS[0] * KD)
                layer_norm(lambda k: vcol(l, V_LN + 8 + k), IN_GROUPS[1] * KD)

                def copy(z, bank):
                    if z < 2:
                        last = act.activation(xpad[:, z, 16:16 + T], bank[:, 0:T], ACT.Copy)
                    elif z < 4:
                        last = act.activation(ca[:, z - 2, :], bank[:, 0:T], ACT.Copy)
                    elif z < 6:
                        last = act.activation(cg[:, z - 4, :], bank[:, 0:T], ACT.Sigmoid)
                    elif z in QK:
                        i = z - QK[0]
                        if i >= 2:
                            act.wait_ge(rope_ready, seen.at(rope_ready, i - 1))
                        act.activation(qk_raw[:, i % 2, :], bank[:, 0:T], ACT.Copy)
                        act.activation(qk_swap[0:64, i % 2, :], bank[64:128, 0:T], ACT.Copy)
                        last = act.activation(qk_swap[64:128, i % 2, :], bank[0:64, 0:T], ACT.Copy)
                    elif z in VALUES:
                        i = z - VALUES[0]
                        last = act.activation(v_tok[:, :, i * P:(i + 1) * P],
                                              bank[:, 0:3 * P].rearrange("p (t n) -> p t n", t=3), ACT.Copy)
                    else:
                        last = act.activation(gate_s[:, z - 18, :], bank[:, 0:T], ACT.Silu)
                    last.then_inc(z_copied, 1)

                in_tiles(IN_GROUPS, 2 * KD, copy)
                for j in range(2):
                    act.wait_ge(pool_mixed, seen.next(pool_mixed))
                    act.activation(y[:, j, :], ps[j][:, 0:T], ACT.Identity, scale=vcol(l, V_PSC + j))\
                        .then_inc(small_done, 1)
                for j in range(2):
                    act.wait_ge(conv_cent, seen.next(conv_cent))
                    act.activation(conv_sq[:, j, :], conv_y[:, j, :], ACT.Square).then_inc(conv_sqd, 1)
                act.wait_ge(conv_var, seen.next(conv_var))
                act.activation(std[:], ps[7][:, 0:T], ACT.Sqrt, scale=1.0 / (2 * P), bias=eps[:, 0:1])\
                    .then_inc(conv_std, 1)
                for j in range(2):
                    act.wait_ge(conv_nrm, seen.next(conv_nrm))
                    act.activation(conv_y[:, j, :], conv_y[:, j, :], ACT.Silu, scale=vcol(l, V_CG + j),
                                   bias=vcol(l, V_CB + j)).then_inc(conv_act, 1)
                for j in range(2):
                    act.wait_ge(conv_pwd, seen.next(conv_pwd))
                    act.activation(y[:, 2 + j, :], ps[6 + j][:, 0:T], ACT.Copy).then_inc(small_done, 1)
                for hd in range(HEADS):
                    act.wait_ge(ret_cent, seen.next(ret_cent))
                    act.activation(o_sq[:, hd, :], o_c[:, hd, :], ACT.Square).then_inc(ret_sqd, 1)
                for hd in range(HEADS):
                    act.wait_ge(ret_var, seen.next(ret_var))
                    act.activation(o_std[:, hd, :], ps[4 + hd][:, 0:T], ACT.Sqrt, scale=1.0 / P,
                                   bias=eps[:, 0:1]).then_inc(ret_std, 1)
                act.wait_ge(small_done, seen.next(small_done, 4))
                for k in range(4):
                    mix_split(k, T)
                act.wait_ge(ret_done, seen.next(ret_done))
                for k in range(4, KD):
                    mix_split(k, T)
                project_out()
                layer_norm(lambda k: vcol(l, V_LN + 24 + k), UP_BLOCKS)
                ffn(UP_BLOCKS)
                layer_norm(lambda k: vcol(l, V_LN + 40 + k), UP_BLOCKS)
            seen.leave()
            st.leave()

            def attention(low):
                def exps(u):
                    t, j = UNITS[u]
                    act.wait_ge(at_max, seen.next(at_max))
                    for e in range(2):
                        last = act.activation(att_p[:, u % 2, e, low:1 + P * (t + 1)],
                                              att_s[:, u % 2, e, low:1 + P * (t + 1)], ACT.Exp,
                                              bias=att_max[:, u % 2, e:e + 1], accum_out=att_sum[:, u % 2, e:e + 1])
                    last.then_inc(at_exp, 1)

                def copy_turned(u):
                    t, j = UNITS[u]
                    act.wait_ge(at_t, seen.next(at_t))
                    if t:
                        last = act.activation(att_pT[:, u % 2].rearrange("p a n -> p (a n)"), ps[4 + u % 2][:, :],
                                              ACT.Copy)
                    else:
                        last = act.activation(att_pT[:, u % 2, 0:3:2, :],
                                              ps[4 + u % 2][:, :].rearrange("p (a n) -> p a n", n=P)[:, 0:3:2, :],
                                              ACT.Copy)
                    last.then_inc(at_tc, 1)

                def copy_out(u):
                    t, j = UNITS[u]
                    act.wait_ge(at_o, seen.next(at_o))
                    act.activation(y[:, first + j, t * P:(t + 1) * P], ps[6 + u % 2][:, 0:P], ACT.Copy)\
                        .then_inc(at_done, 1)

                first = out_tile[0]
                for u in range(len(UNITS) + 2):
                    if u < len(UNITS):
                        exps(u)
                    if 1 <= u <= len(UNITS):
                        copy_turned(u - 1)
                    if u >= 2:
                        copy_out(u - 2)
                seen.skip(at_done, len(UNITS))

            out_tile = [0]
            act.wait_ge(h_done, 1 + 3 * LAYERS)
            pre_norm(None)
            EIGHTH = 64 ** -0.5

            def copy(z, bank):
                if z < 4:
                    last = act.activation(qa[:, z, :], bank[:, 0:S], ACT.Copy, scale=EIGHTH)
                elif z < 8:
                    last = act.activation(ka[:, z - 4, :], bank[:, 0:S], ACT.Copy)
                elif z in EVEN_TOKEN:
                    dst, i = (va, z - 8) if z < 12 else (vb, z - 16)
                    last = act.activation(dst[:, :, i * P:(i + 1) * P],
                                          bank[:, 0:2 * P].rearrange("p (t n) -> p t n", t=2), ACT.Copy)
                elif z < 14:
                    last = act.activation(qb[:, z - 12, :], bank[:, 0:S], ACT.Copy, scale=EIGHTH)
                elif z < 16:
                    last = act.activation(kb[:, z - 14, :], bank[:, 0:S], ACT.Copy)
                elif z < 24:
                    last = act.activation(rb[:, z - 20, :], bank[:, 0:S], ACT.Silu)
                else:
                    last = act.activation(gb[0:16, :], bank[0:16, 0:S], ACT.Copy)
                last.then_inc(z2_copied, 1)

            in_tiles(EVEN_GROUPS, 2 * KD, copy)
            act.wait_ge(gate_ready, 1)
            for j in range(2):
                last = act.activation(zb[:, j, :], ps[6 + j][:, 0:S], ACT.Abs, bias=uvec[:, U_GATEB + j:U_GATEB + j + 1])
            last.then_inc(act_seq, 1)
            act.wait_ge(act_seq, 1)
            act.activation(zb[:], zb[:], ACT.Exp, scale=-1.0).then_inc(act_seq, 1)
            act.wait_ge(act_seq, 2)
            act.activation(zb[:], zb[:], ACT.Ln, bias=1.0).then_inc(gate_log, 1)
            act.wait_ge(gate_cum, 1)
            act.activation(za[:], dmid[:], ACT.Exp)
            act.activation(zb[:], dmid[:], ACT.Exp, scale=-1.0)
            act.activation(qhat[:], bc[:], ACT.Exp)
            act.activation(khat[:], dlast[:], ACT.Exp).then_inc(gate_exp, 1)
            attention(1)
            act.wait_ge(gla_kt, 1)
            act.activation(k_tok[:].rearrange("p t j n -> p (t j n)"), ps[7][:, :], ACT.Copy).then_inc(gla_ktc, 1)
            act.wait_ge(gla_o, 1)
            for hd in range(4):
                act.activation(g_sq[:, hd, :], ps[4 + hd][:, 0:S], ACT.Square)\
                    .then_inc(gla_sqd, 1)
            for hd in range(4):
                act.wait_ge(gla_var, hd + 1)
                act.activation(g_std[:, hd, :], ps[hd][:, 0:S], ACT.Sqrt, scale=1.0 / P, bias=eps[:, 1:2])\
                    .then_inc(gla_std, 1)
            act.wait_ge(at_done, seen.at(at_done, 0))
            for k in range(4):
                mix_split(k, S)
            act.wait_ge(gla_done, 1)
            for k in range(4, KD):
                mix_split(k, S)
            project_out(S)
            post_norm(UP_BLOCKS)
            pre_norm(x_ready)
            ffn(ODD_GROUPS[0] * KD, S)
            post_norm(ODD_GROUPS[1] * KD)

            pre_norm(x_ready)
            SCALE_D = 96 ** -0.5

            def copy(z, bank):
                if z < 4:
                    last = act.activation(qc[:, z, :], bank[:, 0:S], ACT.Copy, scale=EIGHTH)
                elif z == 4:
                    for kv in range(2):
                        for e in range(2):
                            last = act.activation(kdup[64 * e:64 * e + 64, kv, :], bank[64 * kv:64 * kv + 64, 0:S],
                                                  ACT.Copy)
                elif z == 5:
                    last = act.activation(vc[:].rearrange("p t n -> p (t n)"), bank[:, 0:2 * P], ACT.Copy)
                elif z < 11:
                    last = act.activation(cqkv[:, z - 6, :], bank[:, 0:S], ACT.Copy)
                else:
                    act.activation(rt[64:96, 0, :], bank[64:96, 0:S], ACT.Copy)
                    last = act.activation(rt[64:96, 1, :], bank[96:128, 0:S], ACT.Copy)
                last.then_inc(z2_copied, 1)

            in_tiles(ODD_GROUPS, 12, copy)
            seen.skip(z2_copied, 25 + 12)
            attention(0)
            act.wait_ge(z2_copied, 25 + 12)
            for g, (k0, n, width) in enumerate(((0, 3, 384), (3, 2, 256))):
                for k in range(n):
                    last = act.activation(c_sq[:, k, :], cqkv[:, k0 + k, :], ACT.Square)
                last.then_inc(c_sqd, 1)
                act.wait_ge(c_var, g + 1)
                if g:
                    act.wait_ge(c_nrm, 3)
                act.activation(std[:, 0:S], ps[6 + g][:, 0:S], ACT.Sqrt, scale=1.0 / width, bias=eps[:, 1:2])\
                    .then_inc(c_std, 1)
                for k in range(n):
                    act.wait_ge(c_nrm, k0 + k + 1)
                    act.activation(hs(h_hi, k0 + k, 0, S), cqkv[:, k0 + k, :], ACT.Copy).then_inc(c_hi, 1)
            for c in range(2):
                split_next((12, 16)[c], 0, c + 1)
                for e in range(4):
                    z = 4 * c + e
                    if e == 3:
                        act.wait_ge(chunk_used, st.value(c, 0, 2))
                    else:
                        act.wait_ge(qd_ready, 3 * c + e + 1)
                    if z < 2:
                        act.wait_ge(kd_ready, 1)
                    else:
                        act.wait_ge(qd_roped, z - 1)
                    act.activation(qd[0:96, z, :], ps[z % 4][0:96, 0:S], ACT.Copy, scale=SCALE_D)
                    act.activation(rt[64:96, z % 2, :], ps[z % 4][96:128, 0:S], ACT.Copy, scale=SCALE_D)\
                        .then_inc(qd_copied, 1)
            split_next(2 * KD, 0, 3)
            for j in range(4):
                act.wait_ge(kn_ready, j + 1)
                act.activation(kd[0:64, 2 * j, :], ps[4 + j % 2][0:64, 0:S], ACT.Copy)
                act.activation(kd[0:64, 2 * j + 1, :], ps[4 + j % 2][64:128, 0:S], ACT.Copy).then_inc(kn_copied, 1)
            for t in range(2):
                if t:
                    act.wait_ge(chunk_used, st.value(2, 0, 2))
                else:
                    act.wait_ge(vd_ready, 1)
                act.activation(vd[:, t, :], ps[6 + t][:, :], ACT.Copy).then_inc(vd_copied, 1)
            st.c += 3
            out_tile[0] = 4
            attention(1)
            act.wait_ge(at_done, seen.at(at_done, 0))
            for k in range(KD):
                mix_split(k, S)
            project_out(S)
            post_norm(UP_BLOCKS)
            pre_norm(x_ready)
            ffn(0, S)
            post_norm(0)

        @block.vector
        def _(dve):
            seen, st = Seen(per_layer), Stream()

            def link(ins):
                ins.then_inc(dve_seq, 1)
                dve.wait_ge(dve_seq, seen.next(dve_seq))

            def split_next(blocks, pairs=0, ahead=1):
                if blocks:
                    slot = st.slot(ahead)
                    dve.wait_ge(w_hi_done, st.value(ahead, pairs, 1))
                    dve.tensor_tensor(w_lo[:, slot, 0:blocks * P], raw[:, slot, 0:blocks * P],
                                      w_hi[:, slot, 0:blocks * P].bitcast(F32), ALU.subtract).then_inc(w_ready, 1)

            def vcol(l, col):
                return vec[:, bass.ds(l, 1), col:col + 1].rearrange("p a b -> p (a b)")

            def inverse_std(n):
                dve.wait_ge(std_ready, seen.next(std_ready))
                link(dve.reciprocal(rstd[:, 0:n], std[:, 0:n]))

            def layer_norm(gain, bias, early):
                dve.wait_ge(mean_ready, seen.next(mean_ready))
                for k in range(KD):
                    dve.scalar_tensor_tensor(y[:, k, :], ps[6][:, 0:T], -1.0 / D, y[:, k, :], ALU.mult, ALU.add)\
                        .then_inc(centered, 1)
                split_next(early)
                inverse_std(T)
                for k in range(KD + 1):
                    if k < KD:
                        dve.scalar_tensor_tensor(y[:, k, :], y[:, k, :], gain(k), rstd[:], ALU.mult, ALU.mult)\
                            .then_inc(normed, 1)
                    if k:
                        dve.wait_ge(affine, seen.next(affine))
                        dve.scalar_tensor_tensor(hs(h_lo, k - 1), y[:, k - 1, :], bias(k - 1),
                                                 hs(h_hi, k - 1).bitcast(F32), ALU.add, ALU.subtract)\
                            .then_inc(h_ready, 1)
                seen.skip(normed, KD)

            def scaled(k, source, col):
                dve.scalar_tensor_tensor(y[:, k, 0:S], source, uvec[:, col + k:col + k + 1], rstd[:, 0:S],
                                         ALU.mult, ALU.mult).then_inc(normed, 1)

            def pre_norm(col):
                inverse_std(S)
                for k in range(KD + 1):
                    if k < KD:
                        scaled(k, xk(k), col)
                    if k:
                        dve.wait_ge(affine, seen.next(affine))
                        dve.tensor_tensor(hs(h_lo, k - 1, 0, S), y[:, k - 1, 0:S],
                                          hs(h_hi, k - 1, 0, S).bitcast(F32), ALU.subtract).then_inc(h_ready, 1)
                seen.skip(normed, KD)

            def post_norm(col, early):
                split_next(early)
                inverse_std(S)
                for k in range(KD + 1):
                    if k < KD:
                        scaled(k, y[:, k, 0:S], col)
                    if k:
                        dve.wait_ge(normed, seen.next(normed))
                        dve.tensor_tensor(xk(k - 1), xk(k - 1), y[:, k - 1, 0:S], ALU.add).then_inc(x_ready, 1)

            def take_tile(m, bank, first_block):
                if first_block:
                    dve.wait_ge(h_done, seen.at(h_done, 0))
                    ins = dve.scalar_tensor_tensor(y[:, m, :].rearrange("p a n -> p (a n)"),
                                                   h[:, m, :].rearrange("p a n -> p (a n)"), ALPHA,
                                                   bank[:, 0:T], ALU.mult, ALU.add)
                else:
                    ins = dve.tensor_copy(y[:, m, 0:S].rearrange("p a n -> p (a n)"), bank[:, 0:S])
                ins.then_inc(y_ready, 1)

            def ffn(after, first_block=True):
                n = T if first_block else S

                def up(i, j, last):
                    if not (isinstance(i, int) and (i, j) == (0, 0)):
                        split_next(DOWN_BLOCKS if last else UP_BLOCKS, i, j + 1)
                    dve.wait_ge(silu_ready, seen.at(silu_ready, i * 2 + (j + 1)))
                    dve.scalar_tensor_tensor(gf[:, j, 0:n], sig[:, j, 0:n], 0.5 if first_block else 1.0,
                                             ps[2 * j + 1][:, 0:n], ALU.mult, ALU.mult).then_inc(up_free, 1)
                    dve.wait_ge(up_free, seen.at(up_free, i * 2 + (j + 1)))
                    f = bass.ds(i * 2 + j, 1)
                    hi = g_hi[:, f, 0:n].rearrange("p a n -> p (a n)")
                    dve.tensor_copy(hi, gf[:, j, 0:n]).then_inc(g_hi_done, 1)
                    dve.wait_ge(g_hi_done, seen.at(g_hi_done, i * 2 + (j + 1)))
                    dve.tensor_tensor(g_lo[:, f, 0:n].rearrange("p a n -> p (a n)"), gf[:, j, 0:n],
                                      hi.bitcast(F32), ALU.subtract).then_inc(g_ready, 1)

                def down(i, j, last):
                    split_next(after if last else DOWN_BLOCKS, i, j + 1)
                    dve.wait_ge(chunk_used, st.value(j, i, 2))
                    take_tile(bass.ds(i * 2 + j, 1), ps[4 + j], first_block)

                pairs_of(dve, FT, up)
                for s in (silu_ready, up_free, g_hi_done):
                    seen.skip(s, FT)
                st.c += FT
                if first_block:
                    seen.skip(h_done, 1)
                pairs_of(dve, KD, down)
                st.c += KD

            def project_out(first_block):
                for c in range(OUT_CHUNKS):
                    split_next(2 * KD if c + 1 < OUT_CHUNKS else UP_BLOCKS, 0, c + 1)
                    dve.wait_ge(tile_ready, seen.next(tile_ready))
                    take_tile(bass.ds(2 * c, 1), ps[4], first_block)
                    dve.wait_ge(chunk_used, st.value(c, 0, 2))
                    take_tile(bass.ds(2 * c + 1, 1), ps[5], first_block)
                st.c += OUT_CHUNKS

            def mix_split(n):
                for k in range(KD):
                    dve.wait_ge(mix_hi, seen.next(mix_hi))
                    dve.tensor_tensor(g_lo[:, k, 0:n], y[:, k, 0:n], g_hi[:, k, 0:n].bitcast(F32), ALU.subtract)\
                        .then_inc(mix_ready, 1)

            dve.memset(eps[:, 0:1], LN_EPS).then_inc(w_ready, 2)
            dve.memset(eps[:, 1:2], RMS_EPS).then_inc(chunk_used, 1)
            dve.memset(hs(h_hi, KD, 0, P).bitcast(F32), 0.0).then_inc(up_free, 2)
            dve.memset(hs(h_lo, KD, 0, P).bitcast(F32), 0.0)
            dve.memset(ones[:], 1.0).then_inc(consts_set, 1)
            seen.skip(up_free, 2)
            for k in range(KD):
                dve.wait_ge(xT_ready, k + 1)
                dve.tensor_copy(y[:, k, :], ps[k % 4][:, 0:T]).then_inc(y_ready, 1)
            split_next(UP_BLOCKS, 0, 0)
            dve.wait_ge(consts_loaded, 16 * 7)
            layer_norm(lambda k: uvec[:, U_ING + k:U_ING + k + 1], lambda k: uvec[:, U_INB + k:U_INB + k + 1],
                       UP_BLOCKS)
            with dve.Fori(0, LAYERS) as l:
                seen.enter(l)
                st.enter(l)
                def norm(i, early):
                    layer_norm(lambda k: vcol(l, V_LN + 16 * i + k), lambda k: vcol(l, V_LN + 16 * i + 8 + k), early)

                ffn(IN_GROUPS[0] * KD)
                norm(0, IN_GROUPS[1] * KD)
                dve.memset(xpad[:, :, 0:16], 0.0)
                link(dve.memset(upad[:, :, 0:TAPS - 1], 0.0))

                def pool_windows():
                    W = 16 + T
                    src = xpad
                    for i, w in enumerate((1, 2, 4, 8)):
                        dst = win[i % 3]
                        link(dve.tensor_tensor(dst[:, :, 2 * w - 1:W], src[:, :, 2 * w - 1:W],
                                               src[:, :, w - 1:W - w], ALU.add))
                        r, j = 64 * (i % 2), i // 2
                        last = dve.tensor_tensor(pool_y[r:r + 64, j, :], dst[r:r + 64, j, 16:W],
                                                 inv_count[r:r + 64, j, :], ALU.mult)
                        src = dst
                    link(last)
                    dve.tensor_tensor(pool_y[:], pool_y[:], xpad[:, :, 16:W], ALU.subtract).then_inc(pool_in, 1)

                def conv_tap(i):
                    for j in range(2):
                        u, w = upad[:, j, i:i + T], vcol(l, V_DW + j * TAPS + i)
                        if i == 0:
                            ins = dve.tensor_scalar(conv_y[:, j, :], u, w, vcol(l, V_CDB + j), ALU.mult, ALU.add)
                        else:
                            ins = dve.scalar_tensor_tensor(conv_y[:, j, :], u, w, conv_y[:, j, :], ALU.mult, ALU.add)
                        if i == TAPS - 1:
                            ins.then_inc(conv_done, 1)
                    if i < TAPS - 1:
                        link(ins)

                def rope(i):
                    dst = (qT if i < HEADS else kT)[:, i % HEADS, :]
                    dve.tensor_tensor(qk_raw[:, i % 2, :], qk_raw[:, i % 2, :], rope_cos[:], ALU.mult)
                    link(dve.tensor_tensor(qk_swap[:, i % 2, :], qk_swap[:, i % 2, :], rope_sin[:], ALU.mult))
                    dve.tensor_tensor(dst, qk_raw[:, i % 2, :], qk_swap[:, i % 2, :], ALU.add)\
                        .then_inc(rope_ready, 1)

                z, tap = 0, 0
                for c, tiles in enumerate(IN_GROUPS):
                    if c:
                        split_next(IN_GROUPS[c + 1] * KD if c + 1 < len(IN_GROUPS) else 2 * KD, 0, c + 1)
                    if c < 7:
                        dve.wait_ge(z_copied, seen.at(z_copied, z + tiles))
                    if c == 0:
                        pool_windows()
                    elif c == 2:
                        link(dve.tensor_tensor(upad[:, :, TAPS - 1:], ca[:], cg[:], ALU.mult))
                    elif c < 7 and c > 2:
                        rope(z - QK[0])
                        rope(z + 1 - QK[0])
                    if c >= 2:
                        for _ in range(3 if c < 7 else 4):
                            if tap < TAPS:
                                conv_tap(tap)
                                tap += 1
                    z += tiles
                while tap < TAPS:
                    conv_tap(tap)
                    tap += 1
                seen.skip(z_copied, 22)
                seen.skip(tile_ready, 10)
                st.c += len(IN_GROUPS)
                dve.wait_ge(conv_mean, seen.next(conv_mean))
                for j in range(2):
                    dve.scalar_tensor_tensor(conv_y[:, j, :], ps[6][:, 0:T], -1.0 / (2 * P), conv_y[:, j, :],
                                             ALU.mult, ALU.add).then_inc(conv_cent, 1)
                dve.wait_ge(conv_std, seen.next(conv_std))
                link(dve.reciprocal(rstd[:], std[:]))
                for j in range(2):
                    dve.tensor_tensor(conv_y[:, j, :], conv_y[:, j, :], rstd[:], ALU.mult).then_inc(conv_nrm, 1)
                for hd in range(HEADS + 1):
                    if hd < HEADS:
                        for t, (lo, m) in enumerate(KTOK):
                            dve.wait_ge(ret_s, seen.next(ret_s))
                            dve.tensor_tensor(pT[0:m, hd % 2, t, :], ps[(3 * hd + t) % 4][0:m, 0:T],
                                              decay[0:m, t, hd, :], ALU.mult).then_inc(ret_p, 1)
                    if hd >= 1:
                        dve.wait_ge(ret_o, seen.next(ret_o))
                        dve.tensor_copy(o_c[:, hd - 1, :], ps[4 + (hd - 1) % 2][:, 0:T]).then_inc(ret_oc, 1)
                for hd in range(HEADS):
                    dve.wait_ge(ret_mean, seen.next(ret_mean))
                    dve.scalar_tensor_tensor(o_c[:, hd, :], ps[hd][:, 0:T], -1.0 / P, o_c[:, hd, :],
                                             ALU.mult, ALU.add).then_inc(ret_cent, 1)
                dve.wait_ge(ret_std, seen.next(ret_std, HEADS))
                dve.wait_ge(h_done, seen.next(h_done))
                link(dve.reciprocal(o_rstd[:], o_std[:]))
                link(dve.tensor_tensor(o_c[:], o_c[:], o_rstd[:], ALU.mult))
                for hd in range(HEADS):
                    last = dve.scalar_tensor_tensor(y[:, 4 + hd, :], o_c[:, hd, :], vcol(l, V_GN + hd),
                                                    gate_s[:, hd, :], ALU.mult, ALU.mult)
                last.then_inc(ret_done, 1)
                mix_split(T)
                project_out(True)
                norm(1, UP_BLOCKS)
                ffn(UP_BLOCKS)
                norm(2, UP_BLOCKS)
                assert seen.n[dve_seq.name] - seen.before[dve_seq.name] == DVE_LINKS
            seen.leave()
            st.leave()

            def attention(low, add_bias):
                def logits(u):
                    t, j = UNITS[u]
                    b, keys = u % 2, P * (t + 1)
                    dve.wait_ge(at_s, seen.next(at_s))
                    if low == 0:
                        dve.tensor_copy(att_s[:, b, :, 0], sinks[:, 2 * j:2 * j + 2])
                    link(add_bias(b, t, j, keys))
                    dve.tensor_reduce(att_max[:, b, :], att_s[:, b, :, low:1 + keys], AX.X, ALU.max, negate=True)\
                        .then_inc(at_max, 1)

                def divide(u):
                    t, j = UNITS[u]
                    b, keys = u % 2, P * (t + 1)
                    dve.wait_ge(at_exp, seen.next(at_exp))
                    link(dve.reciprocal(att_inv[:, b, :], att_sum[:, b, :]))
                    for e in range(2):
                        last = dve.tensor_scalar(att_p[:, b, e, 1:1 + keys], att_p[:, b, e, 1:1 + keys],
                                                 att_inv[:, b, e:e + 1], None, ALU.mult)
                    last.then_inc(at_norm, 1)

                for u in range(len(UNITS) + 1):
                    if u < len(UNITS):
                        logits(u)
                    if u >= 1:
                        divide(u - 1)

            def sloped(rel):
                def add(b, t, j, keys):
                    for e in range(2):
                        last = dve.scalar_tensor_tensor(att_s[:, b, e, 1:1 + keys], rel[:, t, 0:keys],
                                                        2.0 ** -(2 * j + e + 1), ps[2 * b + e][:, 0:keys],
                                                        ALU.mult, ALU.add)
                    return last
                return add

            def dilated(b, t, j, keys):
                link(sloped(rel_a)(b, t, j, keys))
                for e in range(2):
                    last = dve.tensor_tensor(att_s[:, b, e, 1:1 + keys], att_s[:, b, e, 1:1 + keys],
                                             logc[:, t, 0:keys], ALU.add)
                return last

            def causal(b, t, j, keys):
                for e in range(2):
                    last = dve.tensor_tensor(att_s[:, b, e, 1:1 + keys], ps[2 * b + e][:, 0:keys],
                                             mask_d[:, t, 0:keys], ALU.add)
                return last

            def in_stream(sizes, after):
                for c in range(1, len(sizes)):
                    split_next(sizes[c + 1] * KD if c + 1 < len(sizes) else after, 0, c + 1)
                st.c += len(sizes)

            dve.wait_ge(tables_loaded, 16 * 9)
            dve.wait_ge(h_done, 1 + 3 * LAYERS)
            pre_norm(U_RMS)
            in_stream(EVEN_GROUPS, 2 * KD)
            seen.skip(tile_ready, 12)
            dve.wait_ge(gate_log, 1)
            for j in range(2):
                last = dve.tensor_scalar(za[:, j, :], ps[6 + j][:, 0:S], uvec[:, U_GATEB + j:U_GATEB + j + 1], 0.0,
                                         ALU.add, ALU.min)
            link(last)
            link(dve.tensor_tensor(za[:], za[:], zb[:], ALU.subtract))
            for j in range(2):
                last = dve.tensor_tensor_scan(bc[:, j, :], scan_m[:], za[:, j, :], 0.0, ALU.mult, ALU.add)
            link(last)
            link(dve.tensor_scalar(bc[:], bc[:], 1.0 / 16.0, None, ALU.mult))
            for j in range(2):
                by_chunk = bc[:, j, :].rearrange("p (c i) -> p c i", i=64)
                dve.tensor_tensor(dmid[:, j, :].rearrange("p (c i) -> p c i", i=64), by_chunk,
                                  by_chunk[:, :, 31:32].broadcast_to([P, 4, 64]), ALU.subtract)
                last = dve.tensor_tensor(dlast[:, j, :].rearrange("p (c i) -> p c i", i=64),
                                         by_chunk[:, :, 63:64].broadcast_to([P, 4, 64]), by_chunk, ALU.subtract)
            last.then_inc(gate_cum, 1)
            dve.wait_ge(gate_exp, 1)
            link(dve.memset(att[:], 0.0))
            link(dve.tensor_copy(dec[:], qhat[:].rearrange("p j (c i) -> p j c i", i=64)[:, :, :, 63]))
            dve.tensor_tensor(qhat[:], qhat[:], qb[:], ALU.mult)
            link(dve.tensor_tensor(khat[:], khat[:], kb[:], ALU.mult))
            dve.tensor_tensor(qb[:], qb[:], za[:], ALU.mult)
            dve.tensor_tensor(kb[:], kb[:], zb[:], ALU.mult).then_inc(gla_in, 1)
            attention(1, dilated)
            dve.wait_ge(gla_s, 1)
            for t in range(2):
                for hd in range(4):
                    last = dve.copy_predicated(att[:, t, hd, :], tril[:].bitcast(I32),
                                               ps[2 * (hd % 2) + t][:, (hd // 2) * P:(hd // 2 + 1) * P])
            last.then_inc(gla_att, 1)
            dve.wait_ge(gla_ds, 1)
            link(dve.tensor_copy(state[:, 0].rearrange("p j n -> p (j n)"), ps[4][:, 0:2 * P]))
            for n in (1, 2):
                for j in range(2):
                    last = dve.scalar_tensor_tensor(state[:, n, j, :], state[:, n - 1, j, :], dec[:, j, n:n + 1],
                                                    ps[4 + n][:, j * P:(j + 1) * P], ALU.mult, ALU.add)
                if n == 1:
                    link(last)
                else:
                    last.then_inc(gla_state, 1)
            dve.wait_ge(gla_std, 4)
            link(dve.reciprocal(g_std[:], g_std[:]))
            for hd in range(4):
                last = dve.scalar_tensor_tensor(y[:, 4 + hd, 0:S], ps[4 + hd][:, 0:S],
                                                uvec[:, U_GLAN:U_GLAN + 1], g_std[:, hd, :], ALU.mult, ALU.mult)
            link(last)
            dve.tensor_tensor(y[:, 4:8, 0:S], y[:, 4:8, 0:S], rb[:], ALU.mult).then_inc(gla_done, 1)
            mix_split(S)
            project_out(False)
            post_norm(U_RMS + 8, UP_BLOCKS)
            pre_norm(U_RMS + 16)
            ffn(ODD_GROUPS[0] * KD, False)
            post_norm(U_RMS + 24, ODD_GROUPS[1] * KD)

            pre_norm(U_RMS + 32)
            in_stream(ODD_GROUPS, 12)
            seen.skip(tile_ready, 6)
            dve.wait_ge(z2_copied, 25 + 12)
            dve.tensor_tensor(rt[64:96, 0, :], rt[64:96, 0, :], rcos[64:96, :], ALU.mult)
            link(dve.tensor_tensor(rt[64:96, 1, :], rt[64:96, 1, :], rsin[64:96, :], ALU.mult))
            for hd in range(8):
                last = dve.tensor_tensor(kd[64:96, hd, :], rt[64:96, 0, :], rt[64:96, 1, :], ALU.add)
            last.then_inc(kd_ready, 1)
            attention(0, sloped(rel_c))
            for g, (k0, n, col) in enumerate(((0, 3, U_QN), (3, 2, U_KVN))):
                dve.wait_ge(c_std, g + 1)
                link(dve.reciprocal(rstd[:, 0:S], std[:, 0:S]))
                for k in range(n):
                    dve.scalar_tensor_tensor(cqkv[:, k0 + k, :], cqkv[:, k0 + k, :], uvec[:, col + k:col + k + 1],
                                             rstd[:, 0:S], ALU.mult, ALU.mult).then_inc(c_nrm, 1)
                for k in range(n):
                    dve.wait_ge(c_hi, k0 + k + 1)
                    dve.tensor_tensor(hs(h_lo, k0 + k, 0, S), cqkv[:, k0 + k, :],
                                      hs(h_hi, k0 + k, 0, S).bitcast(F32), ALU.subtract).then_inc(c_ready, 1)
            for c in range(2):
                split_next((12, 16)[c], 0, c + 1)
                for z in range(4 * c, 4 * c + 4):
                    dve.wait_ge(qd_copied, z + 1)
                    dve.tensor_tensor(qd[64:96, z, :], qd[64:96, z, :], rcos[64:96, :], ALU.mult)
                    link(dve.tensor_tensor(rt[64:96, z % 2, :], rt[64:96, z % 2, :], rsin[64:96, :], ALU.mult))
                    dve.tensor_tensor(qd[64:96, z, :], qd[64:96, z, :], rt[64:96, z % 2, :], ALU.add)\
                        .then_inc(qd_roped, 1)
            split_next(2 * KD, 0, 3)
            st.c += 3
            attention(1, causal)
            mix_split(S)
            project_out(False)
            post_norm(U_RMS + 40, UP_BLOCKS)
            pre_norm(U_RMS + 48)
            ffn(0, False)
            post_norm(U_RMS + 56, 0)
            for n in range(2 * KD):
                t, k = n // KD, n % KD
                dve.wait_ge(out_t, n + 1)
                dve.tensor_copy(x_tok[:, t, k * P:(k + 1) * P], ps[n % 8][:, 0:P]).then_inc(out_c, 1)


def tables():
    f8 = np.float64
    t = {}
    t["ident"] = np.eye(P)
    gamma = 1.0 - 2.0 ** (-5.0 - np.arange(HEADS, dtype=f8))
    pos = np.arange(T)
    chunk = (pos + (-META) % 64) // 64
    dist = np.abs(pos[:, None] - pos[None, :])
    seen = chunk[:, None] <= chunk[None, :]
    d = np.where(seen[None], gamma[:, None, None] ** dist[None], 0.0) * P ** -0.5
    dk = np.zeros((P, 3, HEADS, T))
    for i, (lo, m) in enumerate(KTOK):
        dk[0:m, i] = d[:, lo:lo + m, :].transpose(1, 0, 2)
    t["decay"] = dk
    inv = (10000.0 ** (-np.arange(0, P, 2, dtype=np.float32) / np.float32(P))).astype(np.float32)
    ang = (np.arange(T, dtype=np.float32)[:, None] * inv[None, :]).T.astype(f8)
    t["rope_cos"] = np.concatenate([np.cos(ang), np.cos(ang)])
    t["rope_sin"] = np.concatenate([-np.sin(ang), np.sin(ang)])
    ic = np.zeros((P, 2, T))
    for g, w in enumerate((2, 4, 8, 16)):
        ic[64 * (g % 2):64 * (g % 2) + 64, g // 2] = 1.0 / np.minimum(pos + 1, w)
    t["inv_count"] = ic
    rel = np.arange(SEQ)[:, None] - np.arange(SEQ)[None, :]
    count = ((rel >= 0) & (rel <= 128)) * 1 + ((rel >= 0) & (rel % 4 == 0)) * 1 + ((rel >= 0) & (rel % 16 == 0)) * 1

    def by_tile(m):
        return m.reshape(2, P, SEQ).transpose(1, 0, 2)

    t["rel_a"] = by_tile(np.where(count > 0, -rel, -1e30))
    t["logc"] = by_tile(np.log(np.maximum(count, 1)))
    t["rel_c"] = by_tile(np.where((rel >= 0) & (rel <= 127), -rel, -1e30))
    t["mask_d"] = by_tile(np.where(rel >= 0, 0.0, -1e30))
    i = np.arange(P)
    t["tril"] = (i[:, None] <= i[None, :]) & (i[:, None] // 64 == i[None, :] // 64)
    t["scan_m"] = np.tile(np.arange(SEQ) % 64 != 0, (P, 1))
    half = 16
    freqs = (10000.0 ** (-np.arange(half, dtype=np.float32) / np.float32(half))).astype(np.float32)
    ang = (np.arange(SEQ, dtype=np.float32)[:, None] * freqs[None, :]).T.astype(f8)
    c, s = np.zeros((P, SEQ)), np.zeros((P, SEQ))
    c[64:96] = np.concatenate([np.cos(ang), np.cos(ang)])
    s[64:96] = np.concatenate([-np.sin(ang), np.sin(ang)])
    t["rcos"], t["rsin"] = c, s
    return {k: np.ascontiguousarray(v, dtype=np.float32) for k, v in t.items()}


def blocks(w, cols=P):
    k, n = w.shape
    return w.reshape(k // P, P, n // cols, cols).transpose(2, 1, 0, 3)


def padded(w, k, n):
    out = np.zeros((k, n), w.dtype)
    out[:w.shape[0], :w.shape[1]] = w
    return out


def tiles_to_chunks(w, per):
    b = blocks(w)
    n = -(-b.shape[0] // per)
    out = np.zeros((n * per,) + b.shape[1:], w.dtype)
    out[:b.shape[0]] = b
    out = out.reshape(n, per, P, -1).transpose(0, 2, 1, 3)
    return out.reshape(n, P, -1)


def up_layout(gate, up):
    f = FT * P
    g, u = blocks(padded(gate, D, f)), blocks(padded(up, D, f))
    return np.stack([g, u], axis=2).reshape(FT, P, UP_BLOCKS * P)


def down_layout(w):
    return blocks(padded(w, FT * P, D)).reshape(KD, P, DOWN_BLOCKS * P)


def columns(v):
    return v.reshape(-1, P).T


def lay_out(i):
    a = {}
    dff = i["ffn1_w2"].shape[1]
    up, down = [], []
    for l in range(LAYERS):
        for n in ("ffn1", "ffn2"):
            w = i[n + "_w13"][l]
            up.append(up_layout(w[:, :dff], w[:, dff:]))
            down.append(down_layout(i[n + "_w2"][l]))
    for l in range(2):
        up.append(up_layout(i["ffn_w_gate_2"][l], i["ffn_w_up_2"][l]))
        down.append(down_layout(i["ffn_w_down_2"][l]))
    a["up_w"], a["down_w"] = np.stack(up), np.stack(down)
    ins = []
    for l in range(LAYERS):
        b = blocks(i["w_in"][l])
        buf = np.zeros((len(IN_GROUPS), P, 2 * KD * P), np.float32)
        z = 0
        for c, n in enumerate(IN_GROUPS):
            buf[c, :, :n * KD * P] = b[z:z + n].transpose(1, 0, 2, 3).reshape(P, -1)
            z += n
        ins.append(buf)
    a["in_w"] = np.stack(ins)
    outs = [i["w_out"][0], i["w_out"][1], i["ab_w_out_2"][0], i["cd_w_out_2"][0]]
    a["out_w"] = np.stack([tiles_to_chunks(w, 2) for w in outs])
    a["even_w"] = tiles_to_chunks(padded(i["ab_w_in_2"][0], D, 25 * P), 2)
    w = i["cd_w_in_2"][0]
    odd = np.zeros((D, 12 * P), np.float32)
    odd[:, :1408] = w[:, :1408]
    odd[:, 1408 + 64:1408 + 96] = w[:, 1408:1440]
    odd[:, 1408 + 96:1408 + 112] = w[:, 1424:1440]
    odd[:, 1408 + 112:1408 + 128] = w[:, 1408:1424]
    a["odd_w"] = tiles_to_chunks(odd, 2)
    w = i["mla_w_uq_2"][0].reshape(384, 8, 96)
    w = np.concatenate([w, w[:, :, 80:96], w[:, :, 64:80]], axis=2).reshape(384, 8 * P)
    a["uq_w"] = blocks(w).reshape(2, 4, P, 3 * P).transpose(0, 2, 1, 3).reshape(2, P, 12 * P)
    w = i["mla_w_ukv_2"][0].reshape(256, 8, 2, 64)
    w = w.transpose(0, 2, 1, 3).reshape(2, P, 1024)
    a["ukv_w"] = w.transpose(1, 0, 2).reshape(P, 2048)
    mixw = np.zeros((LAYERS, P, 6, P), np.float32)
    for l in range(LAYERS):
        for g in range(4):
            r = 64 * (g % 2)
            mixw[l, r:r + 64, g // 2, r:r + 64] = i["pool_w"][l, g]
        mixw[l, :, 2:6] = i["conv_pw"][l].reshape(2, P, 2, P).transpose(1, 0, 2, 3).reshape(P, 4, P)
    a["mixw"] = mixw
    v = np.zeros((P, LAYERS, NV), np.float32)
    for l in range(LAYERS):
        for n in range(3):
            v[:, l, 16 * n:16 * n + 8] = columns(i["ln_g"][l, n])
            v[:, l, 16 * n + 8:16 * n + 16] = columns(i["ln_b"][l, n])
        for col, name, n in ((V_PSC, "pool_scale", 2), (V_CDB, "conv_db", 2), (V_CG, "conv_ln_g", 2),
                             (V_CB, "conv_ln_b", 2), (V_GN, "ret_gn_g", 4)):
            v[:, l, col:col + n] = columns(i[name][l])
        v[:, l, V_DW:] = i["conv_dw"][l].reshape(TAPS, 2, P).transpose(2, 1, 0).reshape(P, 2 * TAPS)
    a["vec"] = v
    u = np.zeros((P, NU), np.float32)
    u[:, U_ING:U_ING + 8] = columns(i["ln_in_g"])
    u[:, U_INB:U_INB + 8] = columns(i["ln_in_b"])
    for l in range(2):
        for n, name in enumerate(("norm_mix_pre_2", "norm_mix_post_2", "norm_ffn_pre_2", "norm_ffn_post_2")):
            c = U_RMS + 32 * l + 8 * n
            u[:, c:c + 8] = columns(i[name][l])
    u[:, U_GATEB:U_GATEB + 2] = columns(i["gla_b_gate_2"][0])
    u[:, U_GLAN] = i["gla_norm_2"][0]
    u[:, U_QN:U_QN + 3] = columns(i["mla_q_norm_2"][0])
    u[:, U_KVN:U_KVN + 2] = columns(i["mla_kv_norm_2"][0])
    a["uvec"] = u
    a["sinks"] = np.tile(i["swa_sinks_2"][0], (P, 1))
    gup = np.zeros((P, 2, P), np.float32)
    gup[0:16] = i["gla_w_gate_up_2"][0].reshape(16, 2, P)
    a["gup"] = gup
    a["x"], a["meta"] = i["x"][0], i["meta"]
    return {k: np.ascontiguousarray(w) for k, w in a.items()}


def kernel(**inputs):
    import concourse.bacc as bacc
    from concourse.bass_utils import run_bass_kernel_spmd

    arrays = lay_out({k: np.asarray(v) for k, v in inputs.items()})
    arrays.update(tables())
    nc = bacc.Bacc("TRN2", target_bir_lowering=False, num_devices=1)
    arrays = {f"in_{k}": v for k, v in arrays.items()}
    a = {k[3:]: nc.dram_tensor(k, v.shape, F32, kind="ExternalInput").ap() for k, v in arrays.items()}
    a["out"] = nc.dram_tensor("out", (SEQ, D), F32, kind="ExternalOutput").ap()
    forward(nc, a)
    r = run_bass_kernel_spmd(nc, [arrays], core_ids=[0])
    return r.results[0]["out"].reshape(1, SEQ, D)
```

```python
from contextlib import ExitStack

import numpy as np

import concourse.bass as bass
from concourse import mybir

F32 = mybir.dt.float32
F32R = mybir.dt.float32r
I32 = mybir.dt.int32
ALU = mybir.AluOpType
ACT = mybir.ActivationFunctionType
AX = mybir.AxisListType

P = 128
D = 1024
KD = D // P
META = 16
SEQ = 256
T = META + SEQ
LAYERS = 2
FT = 22
ALPHA = (2.0 * LAYERS) ** 0.25
LN_EPS = 1e-5
RMS_EPS = 1e-6
HEADS = 4
TAPS = 31
KTOK = [(0, 128), (128, 128), (256, 16)]
UP_BLOCKS = 2 * KD
DOWN_BLOCKS = FT
SLOT = DOWN_BLOCKS * P
FFN_CHUNKS = FT + KD
IN_GROUPS = [2] * 10 + [1] * 2
OUT_CHUNKS = KD // 2
EVEN_GROUPS = [2] * 12 + [1]
ODD_GROUPS = [2] * 6
EVEN_ORDER = [0, 4, 8, 24, 1, 5, 9, 12, 2, 6, 10, 13, 3, 7, 11, 14, 15, 16, 17, 18, 19, 20, 21, 22, 23]
ODD_ORDER = [6, 7, 8, 9, 10, 11, 4, 5, 0, 1, 2, 3]
LAYER_CHUNKS = 2 * FFN_CHUNKS + len(IN_GROUPS) + OUT_CHUNKS
V_LN, V_PSC, V_CDB, V_CG, V_CB, V_GN, V_DW = 0, 48, 50, 52, 54, 56, 60
DVE_LINKS = 51
NV = V_DW + 2 * TAPS
U_ING, U_INB, U_RMS, U_GATEB, U_GLAN, U_QN, U_KVN = 0, 8, 16, 80, 82, 83, 86
NU = 88


class Seen:

    def __init__(self, per_layer):
        self.n, self.per, self.layer = {}, per_layer, None

    def at(self, sem, ahead):
        v = self.n.get(sem.name, 0) + ahead
        return v if self.layer is None else self.layer * self.per[sem.name] + v

    def skip(self, sem, by):
        self.n[sem.name] = self.n.get(sem.name, 0) + by

    def next(self, sem, by=1):
        self.skip(sem, by)
        return self.at(sem, 0)

    def enter(self, layer):
        self.layer, self.before = layer, dict(self.n)

    def leave(self):
        self.layer = None
        self.n = {s: self.before.get(s, 0) + LAYERS * self.per[s] for s in self.per}


class Stream:

    def __init__(self):
        self.c, self.layer = 0, None

    def value(self, ahead, pairs=0, plus=0):
        v = pairs * 2 + (self.c + ahead + plus)
        return v if self.layer is None else self.layer * LAYER_CHUNKS + v

    def loads(self, ahead, pairs=0):
        v = pairs * 16 + ((self.c + ahead) // 2 + 1) * 16
        return v if self.layer is None else self.layer * (8 * LAYER_CHUNKS) + v

    def slot(self, ahead):
        return (self.c + ahead) % 2

    def enter(self, layer):
        assert self.c == 0
        self.layer = layer

    def leave(self):
        assert self.c == LAYER_CHUNKS
        self.layer, self.c = None, LAYERS * LAYER_CHUNKS


def region(*spans):
    spans = [list(s) for s in spans]

    def take(size):
        size = -(-size // 32) * 32
        for s in spans:
            if s[1] - s[0] >= size:
                s[0] += size
                return s[0] - size
        raise AssertionError((size, spans))

    take.spans = spans
    return take


def pairs_of(eng, n, step):
    for j in range(2):
        step(0, j, False)
    with eng.Fori(1, n // 2 - 1) as i:
        for j in range(2):
            step(i, j, False)
    for j in range(2):
        step(n // 2 - 1, j, j == 1)


def forward(nc, a):
    with ExitStack() as ctx:
        cursor = [-(-nc.sbuf_base // 32) * 32]
        limit = nc.sbuf_usable_end
        T4 = T * 4
        S = SEQ

        def place(name, shape, dt=F32, offset=None):
            if offset is None:
                offset = cursor[0]
                cursor[0] += -(-int(np.prod(shape[1:])) * 4 // 32) * 32
                assert cursor[0] <= limit, (name, cursor[0], limit)
            return nc.alloc_sbuf_tensor_at(name, list(shape), dt, offset=offset)

        def placer(take):
            return lambda name, shape, dt=F32: place(name, shape, dt, take(int(np.prod(shape[1:])) * 4))

        raw = place("raw", [P, 2, SLOT])
        w_hi = place("w_hi", [P, 2, SLOT], F32R)
        w_lo = place("w_lo", [P, 2, SLOT], F32R)
        h = place("h", [P, KD, T])
        h_hi = place("h_hi", [P, KD * T + P], F32R)
        h_lo = place("h_lo", [P, KD * T + P], F32R)
        y = place("y", [P, KD, T])
        sq_at = cursor[0]
        sq = place("sq", [P, KD, T])
        ghi_at = cursor[0]
        g_hi = place("g_hi", [P, FT, T], F32R)
        glo_at = cursor[0]
        g_lo = place("g_lo", [P, FT, T], F32R)
        g_end = cursor[0]
        ones = place("ones", [P, P])
        ident = place("ident", [P, P])
        vec = place("vec", [P, LAYERS, NV])
        uvec = place("uvec", [P, NU])
        sinks = place("sinks", [P, 8])
        eps = place("eps", [P, 2])
        std = place("std", [P, T])
        rstd = place("rstd", [P, T])
        sig = place("sig", [P, 2, T])
        gf = place("gf", [P, 2, T])
        decay_at = cursor[0]
        decay = place("decay", [P, 3, HEADS, T])
        rope_cos = place("rope_cos", [P, T])
        rope_sin = place("rope_sin", [P, T])
        inv_count = place("inv_count", [P, 2, T])
        mixw = place("mixw", [P, 6, P])
        rest_at = cursor[0]

        spans = ((ghi_at + KD * T4, glo_at), (glo_at + KD * T4, g_end), (rest_at, limit))
        one = placer(region(*spans))
        xpad = one("xpad", [P, 2, 16 + T])
        upad = one("upad", [P, 2, TAPS - 1 + T])
        ca = one("ca", [P, 2, T])
        cg = one("cg", [P, 2, T])
        qk_raw = one("qk_raw", [P, 2, T])
        qk_swap = one("qk_swap", [P, 2, T])
        qT = one("qT", [P, HEADS, T])
        kT = one("kT", [P, HEADS, T])
        v_tok = one("v_tok", [P, 3, HEADS * P])
        gate_s = one("gate_s", [P, HEADS, T])
        conv_y = one("conv_y", [P, 2, T])
        conv_sq = one("conv_sq", [P, 2, T])
        pool_y = one("pool_y", [P, 2, T])
        o_c = one("o_c", [P, HEADS, T])
        o_rstd = one("o_rstd", [P, HEADS, T])
        win = [place(f"win{i}", [P, 2, 16 + T], offset=sq_at + i * 2 * (16 + T) * 4) for i in range(3)]
        pT = place("pT", [P, 2, 3, T], offset=sq_at)
        o_sq = place("o_sq", [P, HEADS, T], offset=sq_at)
        o_std = place("o_std", [P, HEADS, T], offset=sq_at + HEADS * T4)
        x_tok = place("x_tok", [P, 3, D], offset=ghi_at)

        table = placer(region((decay_at, rest_at)))
        rel_a = table("rel_a", [P, 2, S])
        logc = table("logc", [P, 2, S])
        rel_c = table("rel_c", [P, 2, S])
        mask_d = table("mask_d", [P, 2, S])
        tril = table("tril", [P, P])
        scan_m = table("scan_m", [P, S])
        gup = table("gup", [P, 2, P])
        rcos = table("rcos", [P, S])
        rsin = table("rsin", [P, S])
        both_at = region(*spans)
        both = placer(both_at)
        att_s = both("att_s", [P, 2, 2, S + 1])
        att_p = both("att_p", [P, 2, 2, S + 1])
        att_pT = both("att_pT", [P, 2, 4, P])
        att_max = both("att_max", [P, 2, 2])
        att_sum = both("att_sum", [P, 2, 2])
        att_inv = both("att_inv", [P, 2, 2])
        even = placer(region(*both_at.spans))
        odd = placer(region(*both_at.spans))
        qa = even("qa", [P, 4, S])
        ka = even("ka", [P, 4, S])
        va = even("va", [P, 2, 512])
        qb = even("qb", [P, 2, S])
        kb = even("kb", [P, 2, S])
        vb = even("vb", [P, 2, 512])
        rb = even("rb", [P, 4, S])
        gb = even("gb", [P, S])
        bc = even("bc", [P, 2, S])
        khat = even("khat", [P, 2, S])
        qhat = even("qhat", [P, 2, S])
        att = even("att", [P, 2, 4, P])
        za = place("za", [P, 2, S], offset=sq_at)
        zb = place("zb", [P, 2, S], offset=sq_at + 2048)
        dmid = place("dmid", [P, 2, S], offset=sq_at + 4096)
        dlast = place("dlast", [P, 2, S], offset=sq_at + 6144)
        k_tok = place("k_tok", [P, 2, 2, P], offset=sq_at)
        state = place("state", [P, 3, 2, P], offset=sq_at + 2048)
        dec = place("dec", [P, 2, 4], offset=sq_at + 5120)
        g_sq = place("g_sq", [P, 4, S], offset=sq_at)
        g_std = place("g_std", [P, 4, S], offset=sq_at + 4096)
        qc = odd("qc", [P, 4, S])
        kdup = odd("kdup", [P, 2, S])
        vc = odd("vc", [P, 2, P])
        qd = odd("qd", [P, 8, S])
        kd = odd("kd", [P, 8, S])
        vd = odd("vd", [P, 2, 512])
        rt = odd("rt", [P, 2, S])
        cqkv = place("cqkv", [P, 5, S], offset=sq_at)

        ps = [ctx.enter_context(nc.psum_tensor(f"bank{i}", [P, 512], F32)) for i in range(8)]

        per_layer = {}

        def sem(name, in_layer=0):
            s = ctx.enter_context(nc.semaphore(name))
            per_layer[s.name] = in_layer
            return s

        loaded = [sem(f"raw_loaded{i}") for i in range(2)]
        w_hi_done = sem("w_hi_done")
        w_ready = sem("w_ready")
        chunk_used = sem("chunk_used")
        tile_ready = sem("tile_ready", 10 + OUT_CHUNKS)
        x_loaded = sem("x_loaded")
        consts_loaded = sem("consts_loaded")
        consts_set = sem("consts_set")
        tables_loaded = sem("tables_loaded")
        mixw_loaded = sem("mixw_loaded", 16)
        xT_ready = sem("xT_ready")
        y_ready = sem("y_ready", 3 * KD)
        mean_ready = sem("mean_ready", 3)
        centered = sem("centered", 3 * KD)
        squared = sem("squared", 3 * KD)
        var_ready = sem("var_ready", 3)
        std_ready = sem("std_ready", 3)
        normed = sem("normed", 3 * KD)
        affine = sem("affine", 3 * KD)
        h_done = sem("h_done", 3)
        h_ready = sem("h_ready", 3 * KD)
        up_free = sem("up_free", 2 * FT)
        silu_ready = sem("silu_ready", 2 * FT)
        g_hi_done = sem("g_hi_done", 2 * FT)
        g_ready = sem("g_ready", 2 * FT)
        z_copied = sem("z_copied", 22)
        rope_ready = sem("rope_ready", 2 * HEADS)
        pool_in = sem("pool_in", 1)
        pool_mixed = sem("pool_mixed", 2)
        small_done = sem("small_done", 4)
        conv_done = sem("conv_done", 2)
        conv_mean = sem("conv_mean", 1)
        conv_cent = sem("conv_cent", 2)
        conv_sqd = sem("conv_sqd", 2)
        conv_var = sem("conv_var", 1)
        conv_std = sem("conv_std", 1)
        conv_nrm = sem("conv_nrm", 2)
        conv_act = sem("conv_act", 2)
        conv_pwd = sem("conv_pwd", 2)
        ret_s = sem("ret_s", 3 * HEADS)
        ret_p = sem("ret_p", 3 * HEADS)
        ret_o = sem("ret_o", HEADS)
        ret_oc = sem("ret_oc", HEADS)
        ret_mean = sem("ret_mean", HEADS)
        ret_cent = sem("ret_cent", HEADS)
        ret_sqd = sem("ret_sqd", HEADS)
        ret_var = sem("ret_var", HEADS)
        ret_std = sem("ret_std", HEADS)
        ret_done = sem("ret_done", 1)
        mix_hi = sem("mix_hi", KD)
        mix_ready = sem("mix_ready", KD)
        x_ready = sem("x_ready")
        z2_copied = sem("z2_copied")
        at_s = sem("at_s")
        at_max = sem("at_max")
        at_exp = sem("at_exp")
        at_inv = sem("at_inv")
        at_norm = sem("at_norm")
        at_t = sem("at_t")
        at_tc = sem("at_tc")
        at_o = sem("at_o")
        at_done = sem("at_done")
        gate_ready = sem("gate_ready")
        gate_log = sem("gate_log")
        gate_cum = sem("gate_cum")
        gate_exp = sem("gate_exp")
        gla_in = sem("gla_in")
        gla_s = sem("gla_s")
        gla_kt = sem("gla_kt")
        gla_att = sem("gla_att")
        gla_ktc = sem("gla_ktc")
        gla_ds = sem("gla_ds")
        gla_state = sem("gla_state")
        gla_o = sem("gla_o")
        gla_sqd = sem("gla_sqd")
        gla_var = sem("gla_var")
        gla_std = sem("gla_std")
        gla_done = sem("gla_done")
        c_sqd = sem("c_sqd")
        c_var = sem("c_var")
        c_std = sem("c_std")
        c_nrm = sem("c_nrm")
        c_hi = sem("c_hi")
        c_ready = sem("c_ready")
        qd_ready = sem("qd_ready")
        qd_copied = sem("qd_copied")
        qd_roped = sem("qd_roped")
        kn_ready = sem("kn_ready")
        kn_copied = sem("kn_copied")
        vd_ready = sem("vd_ready")
        vd_copied = sem("vd_copied")
        kd_ready = sem("kd_ready")
        out_t = sem("out_t")
        out_c = sem("out_c")
        stored = sem("stored")
        dve_seq = sem("dve_seq", DVE_LINKS)
        act_seq = sem("act_seq")
        block = ctx.enter_context(nc.Block())

        def hs(buf, k, lo=0, n=T):
            return buf[:, k * T + lo:k * T + lo + n]

        def half(buf, hd, lo, n):
            return buf[64 * (hd % 2):64 * (hd % 2) + 64, hd // 2, lo:lo + n]

        def xk(k):
            return h[:, k, META:T]

        UNITS = [(t, j) for j in range(4) for t in range(2)]
        UN = len(UNITS)

        def unit_banks(u, start):
            return ps[0:4] if u >= start and u % 2 else ps[4:8]

        def same_banks(u, start):
            v = u - 1 if u <= start else u - 2
            return v if v >= 0 and unit_banks(v, start)[0] is unit_banks(u, start)[0] else None

        QK = range(6, 14)
        VALUES = range(14, 18)
        EVEN_TOKEN = (8, 9, 10, 11, 16, 17, 18, 19)
        ODD_TOKEN = (5,)

        @block.sync
        def _(sp):
            st = Stream()

            def load(src, blocks, ahead, pairs=0):
                slot = st.slot(ahead)
                sp.wait_ge(w_ready, st.value(ahead, pairs, 1))
                sp.dma_start(raw[:, slot, 0:blocks * P], src).then_inc(loaded[slot], 16)

            def ffn(i):
                for name, n, blocks in (("up_w", FT, UP_BLOCKS), ("down_w", KD, DOWN_BLOCKS)):
                    src = a[name].rearrange("f c p n -> (f c) p n")
                    with sp.Fori(0, n // 2) as c:
                        for j in range(2):
                            load(src[bass.ds(c * 2 + i * n + j, 1)].rearrange("a p n -> (a p) n"), blocks, j, c)
                    st.c += n

            def straight(chunks):
                for i, (src, blocks) in enumerate(chunks):
                    load(src, blocks, i)
                st.c += len(chunks)

            with sp.Fori(0, LAYERS) as l:
                st.enter(l)
                ffn(l * 2)
                src = a["in_w"][bass.ds(l, 1)].rearrange("a c p n -> (a c) p n")
                straight([(src[c, :, 0:n * KD * P], n * KD) for c, n in enumerate(IN_GROUPS)])
                src = a["out_w"][bass.ds(l, 1)].rearrange("a c p n -> (a c) p n")
                straight([(src[c], 2 * KD) for c in range(OUT_CHUNKS)])
                ffn(l * 2 + 1)
            st.leave()
            straight([(a["even_w"][c, :, 0:n * KD * P], n * KD) for c, n in enumerate(EVEN_GROUPS)])
            straight([(a["out_w"][2, c], 2 * KD) for c in range(OUT_CHUNKS)])
            ffn(4)
            straight([(a["odd_w"][c, :, 0:n * KD * P], n * KD) for c, n in enumerate(ODD_GROUPS)])
            straight([(a["ukv_w"], 16)] + [(a["uq_w"][c], 12) for c in range(2)])
            straight([(a["out_w"][3, c], 2 * KD) for c in range(OUT_CHUNKS)])
            ffn(5)
            for t in range(2):
                sp.wait_ge(out_c, KD * (t + 1))
                sp.dma_start(a["out"][t * P:(t + 1) * P, :], x_tok[:, t, :]).then_inc(stored, 16)
            sp.wait_ge(stored, 32)

        @block.gpsimd
        def _(pool):
            seen = Seen(per_layer)
            pool.dma_start(x_tok[0:META, 0, :], a["meta"]).then_inc(x_loaded, 16)
            pool.dma_start(x_tok[META:P, 0, :], a["x"][0:P - META, :]).then_inc(x_loaded, 16)
            pool.dma_start(x_tok[:, 1, :], a["x"][P - META:2 * P - META, :]).then_inc(x_loaded, 16)
            pool.dma_start(x_tok[0:META, 2, :], a["x"][2 * P - META:SEQ, :]).then_inc(x_loaded, 16)
            pool.dma_start(ident[:], a["ident"]).then_inc(x_loaded, 16)
            for dst, name in ((vec, "vec"), (uvec, "uvec"), (decay, "decay"), (rope_cos, "rope_cos"),
                              (rope_sin, "rope_sin"), (inv_count, "inv_count"), (sinks, "sinks")):
                pool.dma_start(dst[:], a[name]).then_inc(consts_loaded, 16)
            with pool.Fori(0, LAYERS) as l:
                seen.enter(l)
                pool.wait_ge(h_ready, l * (3 * KD) + KD)
                pool.dma_start(mixw[:], a["mixw"][bass.ds(l, 1)].rearrange("a p b n -> (a p) b n"))\
                    .then_inc(mixw_loaded, 16)
            pool.wait_ge(h_ready, KD + (LAYERS - 1) * 3 * KD + 2 * KD)
            for dst, name in ((rel_a, "rel_a"), (logc, "logc"), (rel_c, "rel_c"), (mask_d, "mask_d"),
                              (tril, "tril"), (scan_m, "scan_m"), (gup, "gup"), (rcos, "rcos"), (rsin, "rsin")):
                pool.dma_start(dst[:], a[name]).then_inc(tables_loaded, 16)
            for u in range(3 * UN):
                t, b = UNITS[u % UN][0], u % 2
                pool.wait_ge(at_inv, u + 1)
                for e in range(2):
                    last = pool.tensor_scalar(att_p[:, b, e, 1:1 + P * (t + 1)], att_p[:, b, e, 1:1 + P * (t + 1)],
                                              att_inv[:, b, e:e + 1], None, ALU.mult)
                last.then_inc(at_norm, 1)

        @block.tensor
        def _(pe):
            seen, st = Seen(per_layer), Stream()

            def mm3(out, w, x, first, last):
                pe.matmul(out, w[0], x[0], start=first, stop=False)
                pe.matmul(out, w[0], x[1], start=False, stop=False)
                return pe.matmul(out, w[1], x[0], start=False, stop=last)

            def wpair(slot, b, n=1):
                return w_hi[:, slot, b * P:(b + n) * P], w_lo[:, slot, b * P:(b + n) * P]

            def hpair(k, lo=0, n=T):
                return hs(h_hi, k, lo, n), hs(h_lo, k, lo, n)

            def chunk_is_split(ahead, pairs=0):
                return st.value(ahead, pairs, 3)

            def squares_sum(n=T):
                for k in range(KD):
                    pe.wait_ge(squared, seen.next(squared))
                    last = pe.matmul(ps[7][:, 0:n], ones[:], sq[:, k, 0:n], start=k == 0, stop=k == KD - 1)
                last.then_inc(var_ready, 1)

            def tile_sum(m, n, first=False, stop=False):
                if isinstance(m, int):
                    tile, square = y[:, m, 0:n], sq[:, m, 0:n]
                else:
                    tile = y[:, bass.ds(m, 1), 0:n].rearrange("p a n -> p (a n)")
                    square = sq[:, bass.ds(m, 1), 0:n].rearrange("p a n -> p (a n)")
                if n == T:
                    pe.wait_ge(y_ready, seen.at(y_ready, m + 1))
                    last = pe.matmul(ps[6][:, 0:n], ones[:], tile, start=first, stop=stop)
                else:
                    pe.wait_ge(squared, seen.at(squared, m + 1))
                    last = pe.matmul(ps[7][:, 0:n], ones[:], square, start=first, stop=stop)
                if stop:
                    last.then_inc(mean_ready if n == T else var_ready, 1)
                    seen.skip(y_ready, KD)
                    if n < T:
                        seen.skip(squared, KD)

            def first_chunk(tiles, banks, n, slot):
                for k in range(KD):
                    pe.wait_ge(h_ready, seen.next(h_ready))
                    lasts = [mm3(bank[:, 0:n], wpair(slot, e * KD + k), hpair(k, 0, n), k == 0, k == KD - 1)
                             for e, bank in zip(range(tiles), banks)]
                return lasts

            def ffn(n=T):
                def up(i, j):
                    slot = st.slot(j)
                    pe.wait_ge(w_ready, chunk_is_split(j, i))
                    pe.wait_ge(up_free, seen.at(up_free, i * 2 + (j + 1)))
                    if isinstance(i, int) and (i, j) == (0, 0):
                        last = first_chunk(2, ps[0:2], n, slot)[-1]
                    else:
                        for e in range(2):
                            for k in range(KD):
                                last = mm3(ps[2 * j + e][:, 0:n], wpair(slot, e * KD + k), hpair(k, 0, n),
                                           k == 0, k == KD - 1)
                    last.then_inc(chunk_used, 1)

                def down(i, j):
                    slot = st.slot(j)
                    pe.wait_ge(w_ready, chunk_is_split(j, i))
                    pe.wait_ge(y_ready, seen.at(y_ready, i * 2 + (j - 1)))
                    if isinstance(i, int) and (i, j) == (0, 0):
                        pe.wait_ge(g_ready, seen.at(g_ready, FT - 2))
                    for k in range(FT):
                        if isinstance(i, int) and (i, j, k) == (0, 0, FT - 2):
                            pe.wait_ge(g_ready, seen.at(g_ready, FT))
                        last = mm3(ps[4 + j][:, 0:n], wpair(slot, k), (g_hi[:, k, 0:n], g_lo[:, k, 0:n]),
                                   k == 0, k == FT - 1)
                    last.then_inc(chunk_used, 1)
                    if j == 1 or not isinstance(i, int):
                        tile_sum(i * 2 + (j - 1), n, first=isinstance(i, int))

                up(0, 0)
                up(0, 1)
                with pe.Fori(1, FT // 2) as i:
                    up(i, 0)
                    up(i, 1)
                st.c += FT
                seen.skip(up_free, FT)
                down(0, 0)
                down(0, 1)
                with pe.Fori(1, KD // 2) as i:
                    down(i, 0)
                    down(i, 1)
                st.c += KD
                seen.skip(g_ready, FT)
                tile_sum(KD - 1, n, stop=True)

            def project_out(n=T):
                pe.wait_ge(mix_ready, seen.next(mix_ready, KD))
                for c in range(OUT_CHUNKS):
                    pe.wait_ge(w_ready, chunk_is_split(c))
                    for e in range(2):
                        pe.wait_ge(y_ready, seen.at(y_ready, 2 * c + e - 1))
                        for k in range(KD):
                            last = mm3(ps[4 + e][:, 0:n], wpair(st.slot(c), e * KD + k),
                                       (g_hi[:, k, 0:n], g_lo[:, k, 0:n]), k == 0, k == KD - 1)
                        last.then_inc(chunk_used if e else tile_ready, 1)
                        if 2 * c + e:
                            tile_sum(2 * c + e - 1, n, first=2 * c + e == 1)
                st.c += OUT_CHUNKS
                tile_sum(KD - 1, n, stop=True)

            def in_tiles(sizes, order, by_token, token_tiles, banks, copied, n, between):
                z = 0
                for c, tiles in enumerate(sizes):
                    pe.wait_ge(w_ready, chunk_is_split(c))
                    if c == 0:
                        lasts = first_chunk(tiles, ps, n, st.slot(c))
                    for e in range(tiles):
                        bank = ps[z % banks]
                        if z >= banks:
                            pe.wait_ge(copied, seen.at(copied, z - banks + 1))
                        if c == 0:
                            last = lasts[e]
                        elif order[z] in by_token:
                            for t in range(token_tiles):
                                for k in range(KD):
                                    last = mm3(bank[:, t * P:(t + 1) * P], hpair(k, t * P, P),
                                               wpair(st.slot(c), e * KD + k), k == 0, k == KD - 1)
                        else:
                            for k in range(KD):
                                last = mm3(bank[:, 0:n], wpair(st.slot(c), e * KD + k), hpair(k, 0, n),
                                           k == 0, k == KD - 1)
                        last.then_inc(chunk_used if e == tiles - 1 else tile_ready, 1)
                        z += 1
                    between(c)
                st.c += len(sizes)
                pe.wait_ge(copied, seen.next(copied, z))

            pe.wait_ge(x_loaded, 80)
            for k in range(KD):
                if k >= 4:
                    pe.wait_ge(y_ready, k - 3)
                for t, (lo, m) in enumerate(KTOK):
                    last = pe.transpose(ps[k % 4][:, lo:lo + m], x_tok[0:m, t, k * P:(k + 1) * P], ident[0:m, 0:m])
                last.then_inc(xT_ready, 1)
            pe.wait_ge(consts_set, 1)
            for k in range(KD):
                tile_sum(k, T, k == 0, k == KD - 1)
            squares_sum()

            with pe.Fori(0, LAYERS) as l:
                seen.enter(l)
                st.enter(l)
                ffn()
                squares_sum()
                in_tiles(IN_GROUPS, range(22), VALUES, 3, 4, z_copied, T, lambda c: None)
                pe.wait_ge(mixw_loaded, seen.next(mixw_loaded, 16))
                pe.wait_ge(pool_in, seen.next(pool_in))
                for j in range(2):
                    pe.matmul(ps[j][:, 0:T], mixw[:, j, :], pool_y[:, j, :], start=True, stop=True)\
                        .then_inc(pool_mixed, 1)
                for j in range(2):
                    pe.wait_ge(conv_done, seen.next(conv_done))
                    last = pe.matmul(ps[6][:, 0:T], ones[:], conv_y[:, j, :], start=j == 0, stop=j == 1)
                last.then_inc(conv_mean, 1)
                for j in range(2):
                    pe.wait_ge(conv_sqd, seen.next(conv_sqd))
                    last = pe.matmul(ps[7][:, 0:T], ones[:], conv_sq[:, j, :], start=j == 0, stop=j == 1)
                last.then_inc(conv_var, 1)
                pe.wait_ge(rope_ready, seen.next(rope_ready, 2 * HEADS))
                pe.wait_ge(small_done, seen.next(small_done, 2))

                def values(hd):
                    for t, (lo, m) in enumerate(KTOK):
                        pe.wait_ge(ret_p, seen.at(ret_p, 3 * hd + t + 1))
                        last = pe.matmul(ps[4 + hd % 2][:, 0:T], v_tok[0:m, t, hd * P:(hd + 1) * P],
                                         pT[0:m, hd % 2, t, :], start=t == 0, stop=t == 2)
                    last.then_inc(ret_o, 1)

                for hd in range(HEADS + 1):
                    if hd < HEADS:
                        for t, (lo, m) in enumerate(KTOK):
                            n = 3 * hd + t
                            if n >= 4:
                                pe.wait_ge(ret_p, seen.at(ret_p, n - 3))
                            pe.matmul(ps[n % 4][0:m, 0:T], kT[:, hd, lo:lo + m], qT[:, hd, :],
                                      start=True, stop=True).then_inc(ret_s, 1)
                    if hd >= 3:
                        pe.wait_ge(ret_oc, seen.at(ret_oc, hd - 2))
                    if hd >= 1:
                        values(hd - 1)
                seen.skip(ret_p, 3 * HEADS)
                for hd in range(HEADS):
                    pe.wait_ge(ret_oc, seen.next(ret_oc))
                    pe.matmul(ps[hd][:, 0:T], ones[:], o_c[:, hd, :], start=True, stop=True).then_inc(ret_mean, 1)
                pe.wait_ge(conv_act, seen.next(conv_act, 2))
                for j in range(2):
                    for k in range(2):
                        last = pe.matmul(ps[6 + j][:, 0:T], mixw[:, 2 + 2 * k + j, :], conv_y[:, k, :],
                                         start=k == 0, stop=k == 1)
                    last.then_inc(conv_pwd, 1)
                pe.wait_ge(small_done, seen.next(small_done, 2))
                for hd in range(HEADS):
                    pe.wait_ge(ret_sqd, seen.next(ret_sqd))
                    pe.matmul(ps[4 + hd][:, 0:T], ones[:], o_sq[:, hd, :], start=True, stop=True)\
                        .then_inc(ret_var, 1)
                project_out()
                squares_sum()
                ffn()
                squares_sum()
            seen.leave()
            st.leave()

            def attention(u, units, start, base, q, k, v, ready, v_ready):
                if u < units:
                    t, j = UNITS[u % UN]
                    before = same_banks(u, start)
                    ready(u)
                    if before is not None:
                        pe.wait_ge(at_max, base + before + 1)
                    for e in range(2):
                        last = pe.matmul(unit_banks(u, start)[e][:, 0:P * (t + 1)], q(u, 2 * j + e, t),
                                         k(u, 2 * j + e, t), start=True, stop=True)
                    last.then_inc(at_s, 1)
                if 0 <= u - 3 < units:
                    u -= 3
                    t, j = UNITS[u % UN]
                    before = same_banks(u, start)
                    v_ready(u)
                    pe.wait_ge(at_tc, base + u + 1)
                    if before is not None:
                        pe.wait_ge(at_done, base + before + 1)
                    for e in range(2):
                        for kt in range(t + 1):
                            last = pe.matmul(unit_banks(u, start)[3][64 * e:64 * e + 64, 0:P], v(u, 2 * j + e, kt),
                                             att_pT[:, u % 2, 2 * e + kt, :], start=kt == 0, stop=kt == t)
                    last.then_inc(at_o, 1)
                    u += 3
                if 0 <= u - 2 < units:
                    u -= 2
                    t, j = UNITS[u % UN]
                    before = same_banks(u, start)
                    pe.wait_ge(at_norm, base + u + 1)
                    if before is not None:
                        pe.wait_ge(at_tc, base + before + 1)
                    for e in range(2):
                        for kt in range(t + 1):
                            last = pe.transpose(unit_banks(u, start)[2][:, (2 * e + kt) * P:(2 * e + kt + 1) * P],
                                                att_p[:, u % 2, e, 1 + kt * P:1 + (kt + 1) * P], ident[:])
                    last.then_inc(at_t, 1)

            pe.wait_ge(tables_loaded, 16 * 9)
            seen.skip(h_ready, KD)
            squares_sum(S)

            def step_a(u):
                attention(u, UN, UN, 0, lambda u, hd, t: half(qa, hd, t * P, P),
                          lambda u, hd, t: half(ka, hd, 0, P * (t + 1)),
                          lambda u, hd, kt: va[:, kt, hd * 64:hd * 64 + 64],
                          lambda u: pe.wait_ge(z2_copied, 4 * (u // 2) + 2),
                          lambda u: pe.wait_ge(z2_copied, 4 * (u // 2) + 3))

            def between(c):
                if c == 2:
                    pe.wait_ge(z2_copied, 4)
                    for j in range(2):
                        last = pe.matmul(ps[3][:, j * S:(j + 1) * S], gup[0:16, j, :], gb[0:16, :],
                                         start=True, stop=True)
                    last.then_inc(gate_ready, 1)
                if 1 <= c < UN + 4:
                    step_a(c - 1)

            in_tiles(EVEN_GROUPS, EVEN_ORDER, EVEN_TOKEN, 2, 3, z2_copied, S, between)
            pe.wait_ge(at_done, UN)
            pe.wait_ge(gla_in, 1)
            for t in range(2):
                for hd in range(4):
                    last = pe.matmul(ps[2 * (hd % 2) + t][:, (hd // 2) * P:(hd // 2 + 1) * P], half(kb, hd, t * P, P),
                                     half(qb, hd, t * P, P), start=True, stop=True)
            last.then_inc(gla_s, 1)
            for t in range(2):
                for j in range(2):
                    last = pe.transpose(ps[7][:, (2 * t + j) * P:(2 * t + j + 1) * P],
                                        khat[:, j, t * P:(t + 1) * P], ident[:])
            last.then_inc(gla_kt, 1)
            pe.wait_ge(gla_ktc, 1)
            for n in range(3):
                r = 64 * (n % 2)
                for hd in range(4):
                    e = 64 * (hd % 2)
                    last = pe.matmul(ps[4 + n][e:e + 64, (hd // 2) * P:(hd // 2 + 1) * P],
                                     k_tok[r:r + 64, n // 2, hd // 2, e:e + 64],
                                     vb[r:r + 64, n // 2, hd * P:(hd + 1) * P], start=True, stop=True)
            last.then_inc(gla_ds, 1)
            pe.wait_ge(gla_att, 1)
            pe.wait_ge(gla_state, 1)
            for hd in range(4):
                bank = ps[4 + hd]
                for t in range(2):
                    o = t * P
                    pe.matmul(bank[:, o:o + P], vb[:, t, hd * P:(hd + 1) * P], att[:, t, hd, :],
                              start=True, stop=False)
                    across = (1,) if t == 0 else (2, 3)
                    for n in across:
                        o = 64 * n
                        last = pe.matmul(bank[:, o:o + 64], half(state[:, n - 1], hd, 0, P),
                                         half(qhat, hd, 64 * n, 64), start=False, stop=n == across[-1])
            last.then_inc(gla_o, 1)
            for hd in range(4):
                pe.wait_ge(gla_sqd, hd + 1)
                pe.matmul(ps[hd][:, 0:S], ones[:], g_sq[:, hd, :], start=True, stop=True).then_inc(gla_var, 1)
            project_out(S)
            squares_sum(S)
            ffn(S)

            squares_sum(S)

            def step_cd(u):
                def ready(u):
                    if u < UN:
                        pe.wait_ge(z2_copied, 25 + 8 + u // 2 + 1)
                    else:
                        pe.wait_ge(qd_roped, 2 * (u % UN // 2) + 2)
                        pe.wait_ge(kd_ready, 1)

                attention(u, 2 * UN, UN, UN,
                          lambda u, hd, t: half(qc, hd, t * P, P) if u < UN else qd[0:96, hd, t * P:(t + 1) * P],
                          lambda u, hd, t: kdup[64 * (hd % 2):64 * (hd % 2) + 64, hd // 4, 0:P * (t + 1)]
                          if u < UN else kd[0:96, hd, 0:P * (t + 1)],
                          lambda u, hd, kt: vc[:, kt, (hd // 4) * 64:(hd // 4) * 64 + 64]
                          if u < UN else vd[:, kt, hd * 64:hd * 64 + 64], ready, lambda u: None)

            def between(c):
                if c == 3:
                    for g, (k0, n) in enumerate(((0, 3), (3, 2))):
                        pe.wait_ge(c_sqd, g + 1)
                        for k in range(n):
                            last = pe.matmul(ps[6 + g][:, 0:S], ones[:], y[:, k0 + k, 0:S],
                                             start=k == 0, stop=k == n - 1)
                        last.then_inc(c_var, 1)
                if c >= 4:
                    step_cd(c - 4)

            in_tiles(ODD_GROUPS, ODD_ORDER, ODD_TOKEN, 2, 3, z2_copied, S, between)

            def latent(k, lo, n):
                return g_hi[:, k, lo:lo + n], g_lo[:, k, lo:lo + n]

            pe.wait_ge(w_ready, chunk_is_split(0))
            pe.wait_ge(c_ready, 5)
            for j in range(4):
                if j >= 2:
                    pe.wait_ge(kn_copied, j - 1)
                for k in range(2):
                    last = mm3(ps[j % 2][:, 0:S], wpair(st.slot(0), 8 * k + j), latent(3 + k, 0, S), k == 0, k == 1)
                last.then_inc(kn_ready, 1)
            step_cd(2)
            for t in range(2):
                for k in range(2):
                    last = mm3(ps[2 + t][:, 0:512], latent(3 + k, t * P, P), wpair(st.slot(0), 8 * k + 4, 4),
                               k == 0, k == 1)
                last.then_inc(chunk_used if t else vd_ready, 1)
            step_cd(3)
            pe.wait_ge(kn_copied, 4)
            pe.wait_ge(vd_copied, 2)
            for c in range(2):
                pe.wait_ge(w_ready, chunk_is_split(1 + c))
                for e in range(4):
                    z = 4 * c + e
                    if z >= 4:
                        pe.wait_ge(qd_copied, z - 3)
                    for k in range(3):
                        last = mm3(ps[z % 4][:, 0:S], wpair(st.slot(1 + c), 3 * e + k), latent(k, 0, S),
                                   k == 0, k == 2)
                    last.then_inc(chunk_used if e == 3 else qd_ready, 1)
                    if e % 2:
                        step_cd(4 + z // 2)
            st.c += 3
            pe.wait_ge(qd_copied, 8)
            for u in range(UN, 2 * UN + 3):
                step_cd(u)
            project_out(S)
            squares_sum(S)
            ffn(S)
            pe.wait_ge(x_ready, 3 * KD)
            pe.wait_ge(x_ready, 4 * KD)
            for t in range(2):
                for k in range(KD):
                    n = t * KD + k
                    if n >= 8:
                        pe.wait_ge(out_c, n - 7)
                    pe.transpose(ps[n % 8][:, 0:P], h[:, k, META + t * P:META + (t + 1) * P], ident[:])\
                        .then_inc(out_t, 1)

        @block.scalar
        def _(act):
            seen, st = Seen(per_layer), Stream()

            def split_next(blocks, pairs=0, ahead=1):
                if blocks:
                    slot = st.slot(ahead)
                    act.wait_ge(loaded[slot], st.loads(ahead, pairs))
                    act.wait_ge(chunk_used, st.value(ahead, pairs))
                    act.activation(w_hi[:, slot, 0:blocks * P], raw[:, slot, 0:blocks * P], ACT.Copy)\
                        .then_inc(w_hi_done, 1)

            def vcol(l, col):
                return vec[:, bass.ds(l, 1), col:col + 1].rearrange("p a b -> p (a b)")

            def squares(source, ready, n):
                for k in range(KD):
                    if ready is not None:
                        act.wait_ge(ready, seen.next(ready))
                    act.activation(sq[:, k, 0:n], source(k), ACT.Square).then_inc(squared, 1)

            def deviation(n):
                act.wait_ge(var_ready, seen.next(var_ready))
                act.activation(std[:, 0:n], ps[7][:, 0:n], ACT.Sqrt, scale=1.0 / D,
                               bias=eps[:, 0:1] if n == T else eps[:, 1:2]).then_inc(std_ready, 1)

            def layer_norm(bias, early):
                split_next(early)
                squares(lambda k: y[:, k, :], centered, T)
                deviation(T)
                for k in range(KD):
                    act.wait_ge(normed, seen.next(normed))
                    act.activation(hs(h_hi, k), y[:, k, :], ACT.Identity, bias=bias(k)).then_inc(affine, 1)
                for k in range(KD):
                    last = act.activation(h[:, k, :], y[:, k, :], ACT.Identity, bias=bias(k))
                last.then_inc(h_done, 1)

            def pre_norm(ready):
                squares(xk, ready, S)
                deviation(S)
                for k in range(KD):
                    act.wait_ge(normed, seen.next(normed))
                    act.activation(hs(h_hi, k, 0, S), y[:, k, 0:S], ACT.Copy).then_inc(affine, 1)

            def post_norm(early):
                split_next(early)
                deviation(S)
                seen.skip(normed, KD)

            def square_tile(m):
                act.wait_ge(y_ready, seen.at(y_ready, m + 1))
                f = bass.ds(m, 1)
                act.activation(sq[:, f, 0:S], y[:, f, 0:S], ACT.Square).then_inc(squared, 1)

            def ffn(after, n=T):
                def up(i, j, last):
                    if not (isinstance(i, int) and (i, j) == (0, 0)):
                        split_next(DOWN_BLOCKS if last else UP_BLOCKS, i, j + 1)
                    act.wait_ge(chunk_used, st.value(j, i, 2))
                    act.activation(sig[:, j, 0:n], ps[2 * j][:, 0:n], ACT.Silu).then_inc(silu_ready, 1)

                def down(i, j, last):
                    split_next(after if last else DOWN_BLOCKS, i, j + 1)
                    if n < T:
                        square_tile(i * 2 + j)

                pairs_of(act, FT, up)
                st.c += FT
                pairs_of(act, KD, down)
                st.c += KD
                seen.skip(y_ready, KD)

            def tile_is_ready(ahead, e, tiles):
                if e == tiles - 1:
                    act.wait_ge(chunk_used, st.value(ahead, 0, 2))
                else:
                    act.wait_ge(tile_ready, seen.next(tile_ready))

            def in_tiles(sizes, order, banks, after, copy, before=lambda c: None):
                z = 0
                for c, tiles in enumerate(sizes):
                    if c:
                        split_next(sizes[c + 1] * KD if c + 1 < len(sizes) else after, 0, c + 1)
                    before(c)
                    for e in range(tiles):
                        tile_is_ready(c, e, tiles)
                        copy(order[z], ps[z % banks])
                        z += 1
                st.c += len(sizes)

            def mix_split(k, n):
                act.activation(g_hi[:, k, 0:n], y[:, k, 0:n], ACT.Copy).then_inc(mix_hi, 1)

            def project_out(n=T):
                for c in range(OUT_CHUNKS):
                    split_next(2 * KD if c + 1 < OUT_CHUNKS else UP_BLOCKS, 0, c + 1)
                    if n < T:
                        square_tile(2 * c)
                        square_tile(2 * c + 1)
                seen.skip(tile_ready, OUT_CHUNKS)
                seen.skip(y_ready, KD)
                st.c += OUT_CHUNKS

            seen.skip(y_ready, KD)
            act.wait_ge(loaded[0], 16)
            act.activation(w_hi[:, 0, 0:UP_BLOCKS * P], raw[:, 0, 0:UP_BLOCKS * P], ACT.Copy)\
                .then_inc(w_hi_done, 1)
            act.wait_ge(consts_loaded, 16 * 7)
            act.wait_ge(consts_set, 1)
            layer_norm(lambda k: uvec[:, U_INB + k:U_INB + k + 1], UP_BLOCKS)
            with act.Fori(0, LAYERS) as l:
                seen.enter(l)
                st.enter(l)
                ffn(IN_GROUPS[0] * KD)
                layer_norm(lambda k: vcol(l, V_LN + 8 + k), IN_GROUPS[1] * KD)

                def copy(z, bank):
                    if z < 2:
                        last = act.activation(xpad[:, z, 16:16 + T], bank[:, 0:T], ACT.Copy)
                    elif z < 4:
                        last = act.activation(ca[:, z - 2, :], bank[:, 0:T], ACT.Copy)
                    elif z < 6:
                        last = act.activation(cg[:, z - 4, :], bank[:, 0:T], ACT.Sigmoid)
                    elif z in QK:
                        i = z - QK[0]
                        if i >= 2:
                            act.wait_ge(rope_ready, seen.at(rope_ready, i - 1))
                        act.activation(qk_raw[:, i % 2, :], bank[:, 0:T], ACT.Copy)
                        act.activation(qk_swap[0:64, i % 2, :], bank[64:128, 0:T], ACT.Copy)
                        last = act.activation(qk_swap[64:128, i % 2, :], bank[0:64, 0:T], ACT.Copy)
                    elif z in VALUES:
                        i = z - VALUES[0]
                        last = act.activation(v_tok[:, :, i * P:(i + 1) * P],
                                              bank[:, 0:3 * P].rearrange("p (t n) -> p t n", t=3), ACT.Copy)
                    else:
                        last = act.activation(gate_s[:, z - 18, :], bank[:, 0:T], ACT.Silu)
                    last.then_inc(z_copied, 1)

                in_tiles(IN_GROUPS, range(22), 4, 2 * KD, copy)
                for j in range(2):
                    act.wait_ge(pool_mixed, seen.next(pool_mixed))
                    act.activation(y[:, j, :], ps[j][:, 0:T], ACT.Identity, scale=vcol(l, V_PSC + j))\
                        .then_inc(small_done, 1)
                for j in range(2):
                    act.wait_ge(conv_cent, seen.next(conv_cent))
                    act.activation(conv_sq[:, j, :], conv_y[:, j, :], ACT.Square).then_inc(conv_sqd, 1)
                act.wait_ge(conv_var, seen.next(conv_var))
                act.activation(std[:], ps[7][:, 0:T], ACT.Sqrt, scale=1.0 / (2 * P), bias=eps[:, 0:1])\
                    .then_inc(conv_std, 1)
                for j in range(2):
                    act.wait_ge(conv_nrm, seen.next(conv_nrm))
                    act.activation(conv_y[:, j, :], conv_y[:, j, :], ACT.Silu, scale=vcol(l, V_CG + j),
                                   bias=vcol(l, V_CB + j)).then_inc(conv_act, 1)
                for j in range(2):
                    act.wait_ge(conv_pwd, seen.next(conv_pwd))
                    act.activation(y[:, 2 + j, :], ps[6 + j][:, 0:T], ACT.Copy).then_inc(small_done, 1)
                for hd in range(HEADS):
                    act.wait_ge(ret_cent, seen.next(ret_cent))
                    act.activation(o_sq[:, hd, :], o_c[:, hd, :], ACT.Square).then_inc(ret_sqd, 1)
                for hd in range(HEADS):
                    act.wait_ge(ret_var, seen.next(ret_var))
                    act.activation(o_std[:, hd, :], ps[4 + hd][:, 0:T], ACT.Sqrt, scale=1.0 / P,
                                   bias=eps[:, 0:1]).then_inc(ret_std, 1)
                act.wait_ge(small_done, seen.next(small_done, 4))
                for k in range(4):
                    mix_split(k, T)
                act.wait_ge(ret_done, seen.next(ret_done))
                for k in range(4, KD):
                    mix_split(k, T)
                project_out()
                layer_norm(lambda k: vcol(l, V_LN + 24 + k), UP_BLOCKS)
                ffn(UP_BLOCKS)
                layer_norm(lambda k: vcol(l, V_LN + 40 + k), UP_BLOCKS)
            seen.leave()
            st.leave()

            def attention(u, units, start, base, low, tile):
                if 0 <= u - 2 < units:
                    v = u - 2
                    bank = unit_banks(v, start)[2]
                    act.wait_ge(at_t, base + v + 1)
                    if UNITS[v % UN][0]:
                        last = act.activation(att_pT[:, v % 2].rearrange("p a n -> p (a n)"), bank[:, :], ACT.Copy)
                    else:
                        last = act.activation(att_pT[:, v % 2, 0:3:2, :],
                                              bank[:, :].rearrange("p (a n) -> p a n", n=P)[:, 0:3:2, :], ACT.Copy)
                    last.then_inc(at_tc, 1)
                if u < units:
                    t, j = UNITS[u % UN]
                    act.wait_ge(at_max, base + u + 1)
                    for e in range(2):
                        last = act.activation(att_p[:, u % 2, e, low(u):1 + P * (t + 1)],
                                              att_s[:, u % 2, e, low(u):1 + P * (t + 1)], ACT.Exp,
                                              bias=att_max[:, u % 2, e:e + 1], accum_out=att_sum[:, u % 2, e:e + 1])
                    last.then_inc(at_exp, 1)
                if 0 <= u - 3 < units:
                    v = u - 3
                    t, j = UNITS[v % UN]
                    act.wait_ge(at_o, base + v + 1)
                    act.activation(y[:, tile(v) + j, t * P:(t + 1) * P], unit_banks(v, start)[3][:, 0:P], ACT.Copy)\
                        .then_inc(at_done, 1)

            act.wait_ge(h_done, 1 + 3 * LAYERS)
            pre_norm(None)
            EIGHTH = 64 ** -0.5

            def copy(z, bank):
                if z < 4:
                    last = act.activation(qa[:, z, :], bank[:, 0:S], ACT.Copy, scale=EIGHTH)
                elif z < 8:
                    last = act.activation(ka[:, z - 4, :], bank[:, 0:S], ACT.Copy)
                elif z in EVEN_TOKEN:
                    dst, i = (va, z - 8) if z < 12 else (vb, z - 16)
                    last = act.activation(dst[:, :, i * P:(i + 1) * P],
                                          bank[:, 0:2 * P].rearrange("p (t n) -> p t n", t=2), ACT.Copy)
                elif z < 14:
                    last = act.activation(qb[:, z - 12, :], bank[:, 0:S], ACT.Copy, scale=EIGHTH)
                elif z < 16:
                    last = act.activation(kb[:, z - 14, :], bank[:, 0:S], ACT.Copy)
                elif z < 24:
                    last = act.activation(rb[:, z - 20, :], bank[:, 0:S], ACT.Silu)
                else:
                    last = act.activation(gb[0:16, :], bank[0:16, 0:S], ACT.Copy)
                last.then_inc(z2_copied, 1)

            def before(c):
                if 2 <= c < UN + 5:
                    attention(c - 2, UN, UN, 0, lambda u: 1, lambda u: 0)
                if c == 4:
                    act.wait_ge(gate_ready, 1)
                    for j in range(2):
                        last = act.activation(zb[:, j, :], ps[3][:, j * S:(j + 1) * S], ACT.Abs,
                                              bias=uvec[:, U_GATEB + j:U_GATEB + j + 1])
                    last.then_inc(act_seq, 1)
                    act.wait_ge(act_seq, 1)
                    act.activation(zb[:], zb[:], ACT.Exp, scale=-1.0).then_inc(act_seq, 1)
                    act.wait_ge(act_seq, 2)
                    act.activation(zb[:], zb[:], ACT.Ln, bias=1.0).then_inc(gate_log, 1)
                if c == 7:
                    act.wait_ge(gate_cum, 1)
                    act.activation(za[:], dmid[:], ACT.Exp)
                    act.activation(zb[:], dmid[:], ACT.Exp, scale=-1.0)
                    act.activation(qhat[:], bc[:], ACT.Exp)
                    act.activation(khat[:], dlast[:], ACT.Exp).then_inc(gate_exp, 1)

            in_tiles(EVEN_GROUPS, EVEN_ORDER, 3, 2 * KD, copy, before)
            act.wait_ge(gla_kt, 1)
            act.activation(k_tok[:].rearrange("p t j n -> p (t j n)"), ps[7][:, :], ACT.Copy).then_inc(gla_ktc, 1)
            act.wait_ge(gla_o, 1)
            for hd in range(4):
                act.activation(g_sq[:, hd, :], ps[4 + hd][:, 0:S], ACT.Square)\
                    .then_inc(gla_sqd, 1)
            for hd in range(4):
                act.wait_ge(gla_var, hd + 1)
                act.activation(g_std[:, hd, :], ps[hd][:, 0:S], ACT.Sqrt, scale=1.0 / P, bias=eps[:, 1:2])\
                    .then_inc(gla_std, 1)
            act.wait_ge(at_done, UN)
            for k in range(4):
                mix_split(k, S)
            act.wait_ge(gla_done, 1)
            for k in range(4, KD):
                mix_split(k, S)
            project_out(S)
            post_norm(UP_BLOCKS)
            pre_norm(x_ready)
            ffn(ODD_GROUPS[0] * KD, S)
            post_norm(ODD_GROUPS[1] * KD)

            pre_norm(x_ready)
            SCALE_D = 96 ** -0.5

            def copy(z, bank):
                if z < 4:
                    last = act.activation(qc[:, z, :], bank[:, 0:S], ACT.Copy, scale=EIGHTH)
                elif z == 4:
                    for kv in range(2):
                        for e in range(2):
                            last = act.activation(kdup[64 * e:64 * e + 64, kv, :], bank[64 * kv:64 * kv + 64, 0:S],
                                                  ACT.Copy)
                elif z == 5:
                    last = act.activation(vc[:].rearrange("p t n -> p (t n)"), bank[:, 0:2 * P], ACT.Copy)
                elif z < 11:
                    last = act.activation(cqkv[:, z - 6, :], bank[:, 0:S], ACT.Copy)
                else:
                    act.activation(rt[64:96, 0, :], bank[64:96, 0:S], ACT.Copy)
                    last = act.activation(rt[64:96, 1, :], bank[96:128, 0:S], ACT.Copy)
                last.then_inc(z2_copied, 1)

            seen.skip(z2_copied, 25)

            def step_cd(u):
                attention(u, 2 * UN, UN, UN, lambda u: 0 if u < UN else 1, lambda u: 0 if u < UN else 4)

            def before(c):
                if c == 3:
                    act.wait_ge(z2_copied, 25 + 6)
                    for k in range(5):
                        last = act.activation(y[:, k, 0:S], cqkv[:, k, :], ACT.Square)
                        if k in (2, 4):
                            last.then_inc(c_sqd, 1)
                elif c == 4:
                    for g, width in enumerate((384, 256)):
                        act.wait_ge(c_var, g + 1)
                        act.activation(sig[:, g, 0:S], ps[6 + g][:, 0:S], ACT.Sqrt, scale=1.0 / width,
                                       bias=eps[:, 1:2]).then_inc(c_std, 1)
                elif c == 5:
                    for k in range(5):
                        act.wait_ge(c_nrm, k + 1)
                        act.activation(g_hi[:, k, 0:S], cqkv[:, k, :], ACT.Copy).then_inc(c_hi, 1)
                    step_cd(0)

            in_tiles(ODD_GROUPS, ODD_ORDER, 3, 16, copy, before)
            split_next(12, 0, 1)
            step_cd(1)
            for j in range(4):
                act.wait_ge(kn_ready, j + 1)
                act.activation(kd[0:64, 2 * j, :], ps[j % 2][0:64, 0:S], ACT.Copy)
                act.activation(kd[0:64, 2 * j + 1, :], ps[j % 2][64:128, 0:S], ACT.Copy).then_inc(kn_copied, 1)
            step_cd(2)
            for t in range(2):
                if t:
                    act.wait_ge(chunk_used, st.value(0, 0, 2))
                else:
                    act.wait_ge(vd_ready, 1)
                act.activation(vd[:, t, :], ps[2 + t][:, :], ACT.Copy).then_inc(vd_copied, 1)
            split_next(12, 0, 2)
            step_cd(3)
            for c in range(2):
                if c:
                    split_next(2 * KD, 0, 3)
                    step_cd(5)
                for e in range(4):
                    z = 4 * c + e
                    if e == 3:
                        act.wait_ge(chunk_used, st.value(1 + c, 0, 2))
                    else:
                        act.wait_ge(qd_ready, 3 * c + e + 1)
                    if z < 2:
                        act.wait_ge(kd_ready, 1)
                    else:
                        act.wait_ge(qd_roped, z - 1)
                    act.activation(qd[0:96, z, :], ps[z % 4][0:96, 0:S], ACT.Copy, scale=SCALE_D)
                    act.activation(rt[64:96, z % 2, :], ps[z % 4][96:128, 0:S], ACT.Copy, scale=SCALE_D)\
                        .then_inc(qd_copied, 1)
                    if e == 1:
                        step_cd(4 + 2 * c)
            st.c += 3
            for u in range(UN - 1, 2 * UN + 3):
                step_cd(u)
            act.wait_ge(at_done, 3 * UN)
            for k in range(KD):
                mix_split(k, S)
            project_out(S)
            post_norm(UP_BLOCKS)
            pre_norm(x_ready)
            ffn(0, S)
            post_norm(0)

        @block.vector
        def _(dve):
            seen, st = Seen(per_layer), Stream()

            def link(ins):
                ins.then_inc(dve_seq, 1)
                dve.wait_ge(dve_seq, seen.next(dve_seq))

            def split_next(blocks, pairs=0, ahead=1):
                if blocks:
                    slot = st.slot(ahead)
                    dve.wait_ge(w_hi_done, st.value(ahead, pairs, 1))
                    dve.tensor_tensor(w_lo[:, slot, 0:blocks * P], raw[:, slot, 0:blocks * P],
                                      w_hi[:, slot, 0:blocks * P].bitcast(F32), ALU.subtract).then_inc(w_ready, 1)

            def vcol(l, col):
                return vec[:, bass.ds(l, 1), col:col + 1].rearrange("p a b -> p (a b)")

            def inverse_std(n):
                dve.wait_ge(std_ready, seen.next(std_ready))
                link(dve.reciprocal(rstd[:, 0:n], std[:, 0:n]))

            def layer_norm(gain, bias, early):
                dve.wait_ge(mean_ready, seen.next(mean_ready))
                for k in range(KD):
                    dve.scalar_tensor_tensor(y[:, k, :], ps[6][:, 0:T], -1.0 / D, y[:, k, :], ALU.mult, ALU.add)\
                        .then_inc(centered, 1)
                split_next(early)
                inverse_std(T)
                for k in range(KD + 1):
                    if k < KD:
                        dve.scalar_tensor_tensor(y[:, k, :], y[:, k, :], gain(k), rstd[:], ALU.mult, ALU.mult)\
                            .then_inc(normed, 1)
                    if k:
                        dve.wait_ge(affine, seen.next(affine))
                        dve.scalar_tensor_tensor(hs(h_lo, k - 1), y[:, k - 1, :], bias(k - 1),
                                                 hs(h_hi, k - 1).bitcast(F32), ALU.add, ALU.subtract)\
                            .then_inc(h_ready, 1)
                seen.skip(normed, KD)

            def scaled(k, source, col):
                dve.scalar_tensor_tensor(y[:, k, 0:S], source, uvec[:, col + k:col + k + 1], rstd[:, 0:S],
                                         ALU.mult, ALU.mult).then_inc(normed, 1)

            def pre_norm(col):
                inverse_std(S)
                for k in range(KD + 1):
                    if k < KD:
                        scaled(k, xk(k), col)
                    if k:
                        dve.wait_ge(affine, seen.next(affine))
                        dve.tensor_tensor(hs(h_lo, k - 1, 0, S), y[:, k - 1, 0:S],
                                          hs(h_hi, k - 1, 0, S).bitcast(F32), ALU.subtract).then_inc(h_ready, 1)
                seen.skip(normed, KD)

            def post_norm(col, early):
                split_next(early)
                inverse_std(S)
                for k in range(KD + 1):
                    if k < KD:
                        scaled(k, y[:, k, 0:S], col)
                    if k:
                        dve.wait_ge(normed, seen.next(normed))
                        dve.tensor_tensor(xk(k - 1), xk(k - 1), y[:, k - 1, 0:S], ALU.add).then_inc(x_ready, 1)

            def take_tile(m, bank, first_block):
                if first_block:
                    dve.wait_ge(h_done, seen.at(h_done, 0))
                    ins = dve.scalar_tensor_tensor(y[:, m, :].rearrange("p a n -> p (a n)"),
                                                   h[:, m, :].rearrange("p a n -> p (a n)"), ALPHA,
                                                   bank[:, 0:T], ALU.mult, ALU.add)
                else:
                    ins = dve.tensor_copy(y[:, m, 0:S].rearrange("p a n -> p (a n)"), bank[:, 0:S])
                ins.then_inc(y_ready, 1)

            def ffn(after, first_block=True):
                n = T if first_block else S

                def up(i, j, last):
                    if not (isinstance(i, int) and (i, j) == (0, 0)):
                        split_next(DOWN_BLOCKS if last else UP_BLOCKS, i, j + 1)
                    dve.wait_ge(silu_ready, seen.at(silu_ready, i * 2 + (j + 1)))
                    dve.scalar_tensor_tensor(gf[:, j, 0:n], sig[:, j, 0:n], 0.5 if first_block else 1.0,
                                             ps[2 * j + 1][:, 0:n], ALU.mult, ALU.mult).then_inc(up_free, 1)
                    dve.wait_ge(up_free, seen.at(up_free, i * 2 + (j + 1)))
                    f = bass.ds(i * 2 + j, 1)
                    hi = g_hi[:, f, 0:n].rearrange("p a n -> p (a n)")
                    dve.tensor_copy(hi, gf[:, j, 0:n]).then_inc(g_hi_done, 1)
                    dve.wait_ge(g_hi_done, seen.at(g_hi_done, i * 2 + (j + 1)))
                    dve.tensor_tensor(g_lo[:, f, 0:n].rearrange("p a n -> p (a n)"), gf[:, j, 0:n],
                                      hi.bitcast(F32), ALU.subtract).then_inc(g_ready, 1)

                def down(i, j, last):
                    split_next(after if last else DOWN_BLOCKS, i, j + 1)
                    dve.wait_ge(chunk_used, st.value(j, i, 2))
                    take_tile(bass.ds(i * 2 + j, 1), ps[4 + j], first_block)

                pairs_of(dve, FT, up)
                for s in (silu_ready, up_free, g_hi_done):
                    seen.skip(s, FT)
                st.c += FT
                if first_block:
                    seen.skip(h_done, 1)
                pairs_of(dve, KD, down)
                st.c += KD

            def project_out(first_block):
                for c in range(OUT_CHUNKS):
                    split_next(2 * KD if c + 1 < OUT_CHUNKS else UP_BLOCKS, 0, c + 1)
                    dve.wait_ge(tile_ready, seen.next(tile_ready))
                    take_tile(bass.ds(2 * c, 1), ps[4], first_block)
                    dve.wait_ge(chunk_used, st.value(c, 0, 2))
                    take_tile(bass.ds(2 * c + 1, 1), ps[5], first_block)
                st.c += OUT_CHUNKS

            def mix_split(n):
                for k in range(KD):
                    dve.wait_ge(mix_hi, seen.next(mix_hi))
                    dve.tensor_tensor(g_lo[:, k, 0:n], y[:, k, 0:n], g_hi[:, k, 0:n].bitcast(F32), ALU.subtract)\
                        .then_inc(mix_ready, 1)

            dve.memset(eps[:, 0:1], LN_EPS).then_inc(w_ready, 2)
            dve.memset(eps[:, 1:2], RMS_EPS).then_inc(chunk_used, 1)
            dve.memset(hs(h_hi, KD, 0, P).bitcast(F32), 0.0).then_inc(up_free, 2)
            dve.memset(hs(h_lo, KD, 0, P).bitcast(F32), 0.0)
            dve.memset(ones[:], 1.0).then_inc(consts_set, 1)
            seen.skip(up_free, 2)
            for k in range(KD):
                dve.wait_ge(xT_ready, k + 1)
                dve.tensor_copy(y[:, k, :], ps[k % 4][:, 0:T]).then_inc(y_ready, 1)
            split_next(UP_BLOCKS, 0, 0)
            dve.wait_ge(consts_loaded, 16 * 7)
            layer_norm(lambda k: uvec[:, U_ING + k:U_ING + k + 1], lambda k: uvec[:, U_INB + k:U_INB + k + 1],
                       UP_BLOCKS)
            with dve.Fori(0, LAYERS) as l:
                seen.enter(l)
                st.enter(l)
                def norm(i, early):
                    layer_norm(lambda k: vcol(l, V_LN + 16 * i + k), lambda k: vcol(l, V_LN + 16 * i + 8 + k), early)

                ffn(IN_GROUPS[0] * KD)
                norm(0, IN_GROUPS[1] * KD)
                dve.memset(xpad[:, :, 0:16], 0.0)
                link(dve.memset(upad[:, :, 0:TAPS - 1], 0.0))

                def pool_windows():
                    W = 16 + T
                    src = xpad
                    for i, w in enumerate((1, 2, 4, 8)):
                        dst = win[i % 3]
                        link(dve.tensor_tensor(dst[:, :, 2 * w - 1:W], src[:, :, 2 * w - 1:W],
                                               src[:, :, w - 1:W - w], ALU.add))
                        r, j = 64 * (i % 2), i // 2
                        last = dve.tensor_tensor(pool_y[r:r + 64, j, :], dst[r:r + 64, j, 16:W],
                                                 inv_count[r:r + 64, j, :], ALU.mult)
                        src = dst
                    link(last)
                    dve.tensor_tensor(pool_y[:], pool_y[:], xpad[:, :, 16:W], ALU.subtract).then_inc(pool_in, 1)

                def conv_tap(i):
                    for j in range(2):
                        u, w = upad[:, j, i:i + T], vcol(l, V_DW + j * TAPS + i)
                        if i == 0:
                            ins = dve.tensor_scalar(conv_y[:, j, :], u, w, vcol(l, V_CDB + j), ALU.mult, ALU.add)
                        else:
                            ins = dve.scalar_tensor_tensor(conv_y[:, j, :], u, w, conv_y[:, j, :], ALU.mult, ALU.add)
                        if i == TAPS - 1:
                            ins.then_inc(conv_done, 1)
                    if i < TAPS - 1:
                        link(ins)

                def rope(i):
                    dst = (qT if i < HEADS else kT)[:, i % HEADS, :]
                    dve.tensor_tensor(qk_raw[:, i % 2, :], qk_raw[:, i % 2, :], rope_cos[:], ALU.mult)
                    link(dve.tensor_tensor(qk_swap[:, i % 2, :], qk_swap[:, i % 2, :], rope_sin[:], ALU.mult))
                    dve.tensor_tensor(dst, qk_raw[:, i % 2, :], qk_swap[:, i % 2, :], ALU.add)\
                        .then_inc(rope_ready, 1)

                z, tap = 0, 0
                for c, tiles in enumerate(IN_GROUPS):
                    if c:
                        split_next(IN_GROUPS[c + 1] * KD if c + 1 < len(IN_GROUPS) else 2 * KD, 0, c + 1)
                    if c < 7:
                        dve.wait_ge(z_copied, seen.at(z_copied, z + tiles))
                    if c == 0:
                        pool_windows()
                    elif c == 2:
                        link(dve.tensor_tensor(upad[:, :, TAPS - 1:], ca[:], cg[:], ALU.mult))
                    elif c < 7 and c > 2:
                        rope(z - QK[0])
                        rope(z + 1 - QK[0])
                    if c >= 2:
                        for _ in range(3 if c < 7 else 4):
                            if tap < TAPS:
                                conv_tap(tap)
                                tap += 1
                    z += tiles
                while tap < TAPS:
                    conv_tap(tap)
                    tap += 1
                seen.skip(z_copied, 22)
                seen.skip(tile_ready, 10)
                st.c += len(IN_GROUPS)
                dve.wait_ge(conv_mean, seen.next(conv_mean))
                for j in range(2):
                    dve.scalar_tensor_tensor(conv_y[:, j, :], ps[6][:, 0:T], -1.0 / (2 * P), conv_y[:, j, :],
                                             ALU.mult, ALU.add).then_inc(conv_cent, 1)
                dve.wait_ge(conv_std, seen.next(conv_std))
                link(dve.reciprocal(rstd[:], std[:]))
                for j in range(2):
                    dve.tensor_tensor(conv_y[:, j, :], conv_y[:, j, :], rstd[:], ALU.mult).then_inc(conv_nrm, 1)
                for hd in range(HEADS + 1):
                    if hd < HEADS:
                        for t, (lo, m) in enumerate(KTOK):
                            dve.wait_ge(ret_s, seen.next(ret_s))
                            dve.tensor_tensor(pT[0:m, hd % 2, t, :], ps[(3 * hd + t) % 4][0:m, 0:T],
                                              decay[0:m, t, hd, :], ALU.mult).then_inc(ret_p, 1)
                    if hd >= 1:
                        dve.wait_ge(ret_o, seen.next(ret_o))
                        dve.tensor_copy(o_c[:, hd - 1, :], ps[4 + (hd - 1) % 2][:, 0:T]).then_inc(ret_oc, 1)
                for hd in range(HEADS):
                    dve.wait_ge(ret_mean, seen.next(ret_mean))
                    dve.scalar_tensor_tensor(o_c[:, hd, :], ps[hd][:, 0:T], -1.0 / P, o_c[:, hd, :],
                                             ALU.mult, ALU.add).then_inc(ret_cent, 1)
                dve.wait_ge(ret_std, seen.next(ret_std, HEADS))
                dve.wait_ge(h_done, seen.next(h_done))
                link(dve.reciprocal(o_rstd[:], o_std[:]))
                link(dve.tensor_tensor(o_c[:], o_c[:], o_rstd[:], ALU.mult))
                for hd in range(HEADS):
                    last = dve.scalar_tensor_tensor(y[:, 4 + hd, :], o_c[:, hd, :], vcol(l, V_GN + hd),
                                                    gate_s[:, hd, :], ALU.mult, ALU.mult)
                last.then_inc(ret_done, 1)
                mix_split(T)
                project_out(True)
                norm(1, UP_BLOCKS)
                ffn(UP_BLOCKS)
                norm(2, UP_BLOCKS)
                assert seen.n[dve_seq.name] - seen.before[dve_seq.name] == DVE_LINKS
            seen.leave()
            st.leave()

            def logits(u, low, add_bias):
                t, j = UNITS[u % UN]
                b, keys = u % 2, P * (t + 1)
                dve.wait_ge(at_s, u + 1)
                if u >= 2:
                    dve.wait_ge(at_exp, u - 1)
                if low == 0:
                    dve.tensor_copy(att_s[:, b, :, 0], sinks[:, 2 * j:2 * j + 2])
                start = UN if u < UN else 2 * UN
                link(add_bias(unit_banks(u, start), b, t, j, keys))
                dve.tensor_reduce(att_max[:, b, :], att_s[:, b, :, low:1 + keys], AX.X, ALU.max, negate=True)\
                    .then_inc(at_max, 1)

            def inverse(u):
                dve.wait_ge(at_exp, u + 1)
                dve.reciprocal(att_inv[:, u % 2, :], att_sum[:, u % 2, :]).then_inc(at_inv, 1)

            def sloped(rel):
                def add(banks, b, t, j, keys):
                    for e in range(2):
                        last = dve.scalar_tensor_tensor(att_s[:, b, e, 1:1 + keys], rel[:, t, 0:keys],
                                                        2.0 ** -(2 * j + e + 1), banks[e][:, 0:keys],
                                                        ALU.mult, ALU.add)
                    return last
                return add

            def dilated(banks, b, t, j, keys):
                link(sloped(rel_a)(banks, b, t, j, keys))
                for e in range(2):
                    last = dve.tensor_tensor(att_s[:, b, e, 1:1 + keys], att_s[:, b, e, 1:1 + keys],
                                             logc[:, t, 0:keys], ALU.add)
                return last

            def causal(banks, b, t, j, keys):
                for e in range(2):
                    last = dve.tensor_tensor(att_s[:, b, e, 1:1 + keys], banks[e][:, 0:keys],
                                             mask_d[:, t, 0:keys], ALU.add)
                return last

            def in_stream(sizes, after, before, then):
                for c in range(len(sizes)):
                    before(c)
                    if c:
                        split_next(sizes[c + 1] * KD if c + 1 < len(sizes) else after, 0, c + 1)
                    then(c)
                st.c += len(sizes)

            dve.wait_ge(tables_loaded, 16 * 9)
            dve.wait_ge(h_done, 1 + 3 * LAYERS)
            pre_norm(U_RMS)

            def before(c):
                if 2 <= c < UN + 2:
                    logits(c - 2, 1, dilated)
                if 3 <= c < UN + 3:
                    inverse(c - 3)

            def then(c):
                if c == 5:
                    dve.wait_ge(gate_log, 1)
                    for j in range(2):
                        last = dve.tensor_scalar(za[:, j, :], ps[3][:, j * S:(j + 1) * S],
                                                 uvec[:, U_GATEB + j:U_GATEB + j + 1], 0.0, ALU.add, ALU.min)
                    link(last)
                    link(dve.tensor_tensor(za[:], za[:], zb[:], ALU.subtract))
                    for j in range(2):
                        last = dve.tensor_tensor_scan(bc[:, j, :], scan_m[:], za[:, j, :], 0.0, ALU.mult, ALU.add)
                    link(last)
                elif c == 6:
                    link(dve.tensor_scalar(bc[:], bc[:], 1.0 / 16.0, None, ALU.mult))
                    for j in range(2):
                        by_chunk = bc[:, j, :].rearrange("p (c i) -> p c i", i=64)
                        dve.tensor_tensor(dmid[:, j, :].rearrange("p (c i) -> p c i", i=64), by_chunk,
                                          by_chunk[:, :, 31:32].broadcast_to([P, 4, 64]), ALU.subtract)
                        last = dve.tensor_tensor(dlast[:, j, :].rearrange("p (c i) -> p c i", i=64),
                                                 by_chunk[:, :, 63:64].broadcast_to([P, 4, 64]), by_chunk,
                                                 ALU.subtract)
                    last.then_inc(gate_cum, 1)
                elif c == 10:
                    dve.wait_ge(z2_copied, 17)
                    gla_inputs()

            def gla_inputs():
                dve.wait_ge(gate_exp, 1)
                link(dve.memset(att[:], 0.0))
                link(dve.tensor_copy(dec[:], qhat[:].rearrange("p j (c i) -> p j c i", i=64)[:, :, :, 63]))
                dve.tensor_tensor(qhat[:], qhat[:], qb[:], ALU.mult)
                link(dve.tensor_tensor(khat[:], khat[:], kb[:], ALU.mult))
                dve.tensor_tensor(qb[:], qb[:], za[:], ALU.mult)
                dve.tensor_tensor(kb[:], kb[:], zb[:], ALU.mult).then_inc(gla_in, 1)

            in_stream(EVEN_GROUPS, 2 * KD, before, then)
            seen.skip(tile_ready, 12)
            dve.wait_ge(gla_s, 1)
            for t in range(2):
                for hd in range(4):
                    last = dve.copy_predicated(att[:, t, hd, :], tril[:].bitcast(I32),
                                               ps[2 * (hd % 2) + t][:, (hd // 2) * P:(hd // 2 + 1) * P])
            last.then_inc(gla_att, 1)
            dve.wait_ge(gla_ds, 1)
            link(dve.tensor_copy(state[:, 0].rearrange("p j n -> p (j n)"), ps[4][:, 0:2 * P]))
            for n in (1, 2):
                for j in range(2):
                    last = dve.scalar_tensor_tensor(state[:, n, j, :], state[:, n - 1, j, :], dec[:, j, n:n + 1],
                                                    ps[4 + n][:, j * P:(j + 1) * P], ALU.mult, ALU.add)
                if n == 1:
                    link(last)
                else:
                    last.then_inc(gla_state, 1)
            dve.wait_ge(gla_std, 4)
            link(dve.reciprocal(g_std[:], g_std[:]))
            for hd in range(4):
                last = dve.scalar_tensor_tensor(y[:, 4 + hd, 0:S], ps[4 + hd][:, 0:S],
                                                uvec[:, U_GLAN:U_GLAN + 1], g_std[:, hd, :], ALU.mult, ALU.mult)
            link(last)
            dve.tensor_tensor(y[:, 4:8, 0:S], y[:, 4:8, 0:S], rb[:], ALU.mult).then_inc(gla_done, 1)
            mix_split(S)
            project_out(False)
            post_norm(U_RMS + 8, UP_BLOCKS)
            pre_norm(U_RMS + 16)
            ffn(ODD_GROUPS[0] * KD, False)
            post_norm(U_RMS + 24, ODD_GROUPS[1] * KD)

            pre_norm(U_RMS + 32)

            def step_cd(u):
                if u < 2 * UN:
                    logits(UN + u, 0 if u < UN else 1, sloped(rel_c) if u < UN else causal)
                if u >= 1:
                    inverse(UN + u - 1)

            def before(c):
                if c == 5:
                    step_cd(0)

            def then(c):
                if c == 3:
                    dve.wait_ge(z2_copied, 25 + 6)
                    dve.tensor_tensor(rt[64:96, 0, :], rt[64:96, 0, :], rcos[64:96, :], ALU.mult)
                    link(dve.tensor_tensor(rt[64:96, 1, :], rt[64:96, 1, :], rsin[64:96, :], ALU.mult))
                    for hd in range(8):
                        last = dve.tensor_tensor(kd[64:96, hd, :], rt[64:96, 0, :], rt[64:96, 1, :], ALU.add)
                    last.then_inc(kd_ready, 1)
                elif c == 4:
                    dve.wait_ge(c_std, 2)
                    link(dve.reciprocal(gf[:, :, 0:S], sig[:, :, 0:S]))
                    for k in range(5):
                        g, col = (0, U_QN + k) if k < 3 else (1, U_KVN + k - 3)
                        dve.scalar_tensor_tensor(cqkv[:, k, :], cqkv[:, k, :], uvec[:, col:col + 1],
                                                 gf[:, g, 0:S], ALU.mult, ALU.mult).then_inc(c_nrm, 1)
                elif c == 5:
                    for k in range(5):
                        dve.wait_ge(c_hi, k + 1)
                        dve.tensor_tensor(g_lo[:, k, 0:S], cqkv[:, k, :], g_hi[:, k, 0:S].bitcast(F32),
                                          ALU.subtract).then_inc(c_ready, 1)

            in_stream(ODD_GROUPS, 16, before, then)
            seen.skip(tile_ready, 6)
            step_cd(1)
            split_next(12, 0, 1)
            step_cd(2)
            split_next(12, 0, 2)
            step_cd(3)
            for z in range(8):
                if z == 4:
                    split_next(2 * KD, 0, 3)
                    step_cd(5)
                dve.wait_ge(qd_copied, z + 1)
                dve.tensor_tensor(qd[64:96, z, :], qd[64:96, z, :], rcos[64:96, :], ALU.mult)
                link(dve.tensor_tensor(rt[64:96, z % 2, :], rt[64:96, z % 2, :], rsin[64:96, :], ALU.mult))
                dve.tensor_tensor(qd[64:96, z, :], qd[64:96, z, :], rt[64:96, z % 2, :], ALU.add)\
                    .then_inc(qd_roped, 1)
                if z in (1, 5):
                    step_cd(4 + z // 2)
            st.c += 3
            for u in range(UN - 1, 2 * UN + 1):
                step_cd(u)
            mix_split(S)
            project_out(False)
            post_norm(U_RMS + 40, UP_BLOCKS)
            pre_norm(U_RMS + 48)
            ffn(0, False)
            post_norm(U_RMS + 56, 0)
            for n in range(2 * KD):
                t, k = n // KD, n % KD
                dve.wait_ge(out_t, n + 1)
                dve.tensor_copy(x_tok[:, t, k * P:(k + 1) * P], ps[n % 8][:, 0:P]).then_inc(out_c, 1)


def tables():
    f8 = np.float64
    t = {}
    t["ident"] = np.eye(P)
    gamma = 1.0 - 2.0 ** (-5.0 - np.arange(HEADS, dtype=f8))
    pos = np.arange(T)
    chunk = (pos + (-META) % 64) // 64
    dist = np.abs(pos[:, None] - pos[None, :])
    seen = chunk[:, None] <= chunk[None, :]
    d = np.where(seen[None], gamma[:, None, None] ** dist[None], 0.0) * P ** -0.5
    dk = np.zeros((P, 3, HEADS, T))
    for i, (lo, m) in enumerate(KTOK):
        dk[0:m, i] = d[:, lo:lo + m, :].transpose(1, 0, 2)
    t["decay"] = dk
    inv = (10000.0 ** (-np.arange(0, P, 2, dtype=np.float32) / np.float32(P))).astype(np.float32)
    ang = (np.arange(T, dtype=np.float32)[:, None] * inv[None, :]).T.astype(f8)
    t["rope_cos"] = np.concatenate([np.cos(ang), np.cos(ang)])
    t["rope_sin"] = np.concatenate([-np.sin(ang), np.sin(ang)])
    ic = np.zeros((P, 2, T))
    for g, w in enumerate((2, 4, 8, 16)):
        ic[64 * (g % 2):64 * (g % 2) + 64, g // 2] = 1.0 / np.minimum(pos + 1, w)
    t["inv_count"] = ic
    rel = np.arange(SEQ)[:, None] - np.arange(SEQ)[None, :]
    count = ((rel >= 0) & (rel <= 128)) * 1 + ((rel >= 0) & (rel % 4 == 0)) * 1 + ((rel >= 0) & (rel % 16 == 0)) * 1

    def by_tile(m):
        return m.reshape(2, P, SEQ).transpose(1, 0, 2)

    t["rel_a"] = by_tile(np.where(count > 0, -rel, -1e30))
    t["logc"] = by_tile(np.log(np.maximum(count, 1)))
    t["rel_c"] = by_tile(np.where((rel >= 0) & (rel <= 127), -rel, -1e30))
    t["mask_d"] = by_tile(np.where(rel >= 0, 0.0, -1e30))
    i = np.arange(P)
    t["tril"] = (i[:, None] <= i[None, :]) & (i[:, None] // 64 == i[None, :] // 64)
    t["scan_m"] = np.tile(np.arange(SEQ) % 64 != 0, (P, 1))
    half = 16
    freqs = (10000.0 ** (-np.arange(half, dtype=np.float32) / np.float32(half))).astype(np.float32)
    ang = (np.arange(SEQ, dtype=np.float32)[:, None] * freqs[None, :]).T.astype(f8)
    c, s = np.zeros((P, SEQ)), np.zeros((P, SEQ))
    c[64:96] = np.concatenate([np.cos(ang), np.cos(ang)])
    s[64:96] = np.concatenate([-np.sin(ang), np.sin(ang)])
    t["rcos"], t["rsin"] = c, s
    return {k: np.ascontiguousarray(v, dtype=np.float32) for k, v in t.items()}


def blocks(w, cols=P):
    k, n = w.shape
    return w.reshape(k // P, P, n // cols, cols).transpose(2, 1, 0, 3)


def padded(w, k, n):
    out = np.zeros((k, n), w.dtype)
    out[:w.shape[0], :w.shape[1]] = w
    return out


def tiles_to_chunks(w, per, order=None):
    b = blocks(w)
    if order is not None:
        b = b[order]
    n = -(-b.shape[0] // per)
    out = np.zeros((n * per,) + b.shape[1:], w.dtype)
    out[:b.shape[0]] = b
    out = out.reshape(n, per, P, -1).transpose(0, 2, 1, 3)
    return out.reshape(n, P, -1)


def up_layout(gate, up):
    f = FT * P
    g, u = blocks(padded(gate, D, f)), blocks(padded(up, D, f))
    return np.stack([g, u], axis=2).reshape(FT, P, UP_BLOCKS * P)


def down_layout(w):
    return blocks(padded(w, FT * P, D)).reshape(KD, P, DOWN_BLOCKS * P)


def columns(v):
    return v.reshape(-1, P).T


def lay_out(i):
    a = {}
    dff = i["ffn1_w2"].shape[1]
    up, down = [], []
    for l in range(LAYERS):
        for n in ("ffn1", "ffn2"):
            w = i[n + "_w13"][l]
            up.append(up_layout(w[:, :dff], w[:, dff:]))
            down.append(down_layout(i[n + "_w2"][l]))
    for l in range(2):
        up.append(up_layout(i["ffn_w_gate_2"][l], i["ffn_w_up_2"][l]))
        down.append(down_layout(i["ffn_w_down_2"][l]))
    a["up_w"], a["down_w"] = np.stack(up), np.stack(down)
    ins = []
    for l in range(LAYERS):
        b = blocks(i["w_in"][l])
        buf = np.zeros((len(IN_GROUPS), P, 2 * KD * P), np.float32)
        z = 0
        for c, n in enumerate(IN_GROUPS):
            buf[c, :, :n * KD * P] = b[z:z + n].transpose(1, 0, 2, 3).reshape(P, -1)
            z += n
        ins.append(buf)
    a["in_w"] = np.stack(ins)
    outs = [i["w_out"][0], i["w_out"][1], i["ab_w_out_2"][0], i["cd_w_out_2"][0]]
    a["out_w"] = np.stack([tiles_to_chunks(w, 2) for w in outs])
    a["even_w"] = tiles_to_chunks(padded(i["ab_w_in_2"][0], D, 25 * P), 2, EVEN_ORDER)
    w = i["cd_w_in_2"][0]
    odd = np.zeros((D, 12 * P), np.float32)
    odd[:, :1408] = w[:, :1408]
    odd[:, 1408 + 64:1408 + 96] = w[:, 1408:1440]
    odd[:, 1408 + 96:1408 + 112] = w[:, 1424:1440]
    odd[:, 1408 + 112:1408 + 128] = w[:, 1408:1424]
    a["odd_w"] = tiles_to_chunks(odd, 2, ODD_ORDER)
    w = i["mla_w_uq_2"][0].reshape(384, 8, 96)
    w = np.concatenate([w, w[:, :, 80:96], w[:, :, 64:80]], axis=2).reshape(384, 8 * P)
    a["uq_w"] = blocks(w).reshape(2, 4, P, 3 * P).transpose(0, 2, 1, 3).reshape(2, P, 12 * P)
    w = i["mla_w_ukv_2"][0].reshape(256, 8, 2, 64)
    w = w.transpose(0, 2, 1, 3).reshape(2, P, 1024)
    a["ukv_w"] = w.transpose(1, 0, 2).reshape(P, 2048)
    mixw = np.zeros((LAYERS, P, 6, P), np.float32)
    for l in range(LAYERS):
        for g in range(4):
            r = 64 * (g % 2)
            mixw[l, r:r + 64, g // 2, r:r + 64] = i["pool_w"][l, g]
        mixw[l, :, 2:6] = i["conv_pw"][l].reshape(2, P, 2, P).transpose(1, 0, 2, 3).reshape(P, 4, P)
    a["mixw"] = mixw
    v = np.zeros((P, LAYERS, NV), np.float32)
    for l in range(LAYERS):
        for n in range(3):
            v[:, l, 16 * n:16 * n + 8] = columns(i["ln_g"][l, n])
            v[:, l, 16 * n + 8:16 * n + 16] = columns(i["ln_b"][l, n])
        for col, name, n in ((V_PSC, "pool_scale", 2), (V_CDB, "conv_db", 2), (V_CG, "conv_ln_g", 2),
                             (V_CB, "conv_ln_b", 2), (V_GN, "ret_gn_g", 4)):
            v[:, l, col:col + n] = columns(i[name][l])
        v[:, l, V_DW:] = i["conv_dw"][l].reshape(TAPS, 2, P).transpose(2, 1, 0).reshape(P, 2 * TAPS)
    a["vec"] = v
    u = np.zeros((P, NU), np.float32)
    u[:, U_ING:U_ING + 8] = columns(i["ln_in_g"])
    u[:, U_INB:U_INB + 8] = columns(i["ln_in_b"])
    for l in range(2):
        for n, name in enumerate(("norm_mix_pre_2", "norm_mix_post_2", "norm_ffn_pre_2", "norm_ffn_post_2")):
            c = U_RMS + 32 * l + 8 * n
            u[:, c:c + 8] = columns(i[name][l])
    u[:, U_GATEB:U_GATEB + 2] = columns(i["gla_b_gate_2"][0])
    u[:, U_GLAN] = i["gla_norm_2"][0]
    u[:, U_QN:U_QN + 3] = columns(i["mla_q_norm_2"][0])
    u[:, U_KVN:U_KVN + 2] = columns(i["mla_kv_norm_2"][0])
    a["uvec"] = u
    a["sinks"] = np.tile(i["swa_sinks_2"][0], (P, 1))
    gup = np.zeros((P, 2, P), np.float32)
    gup[0:16] = i["gla_w_gate_up_2"][0].reshape(16, 2, P)
    a["gup"] = gup
    a["x"], a["meta"] = i["x"][0], i["meta"]
    return {k: np.ascontiguousarray(w) for k, w in a.items()}


def kernel(**inputs):
    import concourse.bacc as bacc
    from concourse.bass_utils import run_bass_kernel_spmd

    arrays = lay_out({k: np.asarray(v) for k, v in inputs.items()})
    arrays.update(tables())
    nc = bacc.Bacc("TRN2", target_bir_lowering=False, num_devices=1)
    arrays = {f"in_{k}": v for k, v in arrays.items()}
    a = {k[3:]: nc.dram_tensor(k, v.shape, F32, kind="ExternalInput").ap() for k, v in arrays.items()}
    a["out"] = nc.dram_tensor("out", (SEQ, D), F32, kind="ExternalOutput").ap()
    forward(nc, a)
    r = run_bass_kernel_spmd(nc, [arrays], core_ids=[0])
    return r.results[0]["out"].reshape(1, SEQ, D)
```

```python
from contextlib import ExitStack

import numpy as np

import concourse.bass as bass
from concourse import mybir

F32 = mybir.dt.float32
F32R = mybir.dt.float32r
I32 = mybir.dt.int32
ALU = mybir.AluOpType
ACT = mybir.ActivationFunctionType
AX = mybir.AxisListType

P = 128
D = 1024
KD = D // P
META = 16
SEQ = 256
T = META + SEQ
LAYERS = 2
FT = 22
ALPHA = (2.0 * LAYERS) ** 0.25
LN_EPS = 1e-5
RMS_EPS = 1e-6
HEADS = 4
TAPS = 31
KTOK = [(0, 128), (128, 128), (256, 16)]
UP_BLOCKS = 2 * KD
DOWN_BLOCKS = FT
SLOT = DOWN_BLOCKS * P
FFN_CHUNKS = FT + KD
IN_GROUPS = [2] * 10 + [1] * 2
OUT_CHUNKS = KD // 2
EVEN_GROUPS = [2] * 12 + [1]
ODD_GROUPS = [2] * 6
EVEN_ORDER = [0, 4, 8, 9, 1, 5, 24, 12, 2, 6, 10, 11, 3, 7, 13, 14, 15, 20, 16, 17, 18, 19, 21, 22, 23]
ODD_ORDER = [6, 7, 8, 9, 10, 11, 4, 5, 0, 1, 2, 3]
LAYER_CHUNKS = 2 * FFN_CHUNKS + len(IN_GROUPS) + OUT_CHUNKS
V_LN, V_PSC, V_CDB, V_CG, V_CB, V_GN, V_DW = 0, 48, 50, 52, 54, 56, 60
DVE_LINKS = 56
NV = V_DW + 2 * TAPS
U_ING, U_INB, U_RMS, U_GATEB, U_GLAN, U_QN, U_KVN = 0, 8, 16, 80, 82, 83, 86
NU = 88


class Seen:

    def __init__(self, per_layer):
        self.n, self.per, self.layer = {}, per_layer, None

    def at(self, sem, ahead):
        v = self.n.get(sem.name, 0) + ahead
        return v if self.layer is None else self.layer * self.per[sem.name] + v

    def skip(self, sem, by):
        self.n[sem.name] = self.n.get(sem.name, 0) + by

    def next(self, sem, by=1):
        self.skip(sem, by)
        return self.at(sem, 0)

    def enter(self, layer):
        self.layer, self.before = layer, dict(self.n)

    def leave(self):
        self.layer = None
        self.n = {s: self.before.get(s, 0) + LAYERS * self.per[s] for s in self.per}


class Stream:

    def __init__(self):
        self.c, self.layer = 0, None

    def value(self, ahead, pairs=0, plus=0):
        v = pairs * 2 + (self.c + ahead + plus)
        return v if self.layer is None else self.layer * LAYER_CHUNKS + v

    def loads(self, ahead, pairs=0):
        v = pairs * 16 + ((self.c + ahead) // 2 + 1) * 16
        return v if self.layer is None else self.layer * (8 * LAYER_CHUNKS) + v

    def slot(self, ahead):
        return (self.c + ahead) % 2

    def enter(self, layer):
        assert self.c == 0
        self.layer = layer

    def leave(self):
        assert self.c == LAYER_CHUNKS
        self.layer, self.c = None, LAYERS * LAYER_CHUNKS


def region(*spans):
    spans = [list(s) for s in spans]

    def take(size):
        size = -(-size // 32) * 32
        for s in spans:
            if s[1] - s[0] >= size:
                s[0] += size
                return s[0] - size
        raise AssertionError((size, spans))

    take.spans = spans
    return take


def pairs_of(eng, n, step):
    for j in range(2):
        step(0, j, False)
    with eng.Fori(1, n // 2 - 1) as i:
        for j in range(2):
            step(i, j, False)
    for j in range(2):
        step(n // 2 - 1, j, j == 1)


def forward(nc, a):
    with ExitStack() as ctx:
        cursor = [-(-nc.sbuf_base // 32) * 32]
        limit = nc.sbuf_usable_end
        T4 = T * 4
        S = SEQ

        def place(name, shape, dt=F32, offset=None):
            if offset is None:
                offset = cursor[0]
                cursor[0] += -(-int(np.prod(shape[1:])) * 4 // 32) * 32
                assert cursor[0] <= limit, (name, cursor[0], limit)
            return nc.alloc_sbuf_tensor_at(name, list(shape), dt, offset=offset)

        def placer(take):
            return lambda name, shape, dt=F32: place(name, shape, dt, take(int(np.prod(shape[1:])) * 4))

        raw = place("raw", [P, 2, SLOT])
        w_hi = place("w_hi", [P, 2, SLOT], F32R)
        w_lo = place("w_lo", [P, 2, SLOT], F32R)
        h = place("h", [P, KD, T])
        h_hi = place("h_hi", [P, KD * T + P], F32R)
        h_lo = place("h_lo", [P, KD * T + P], F32R)
        y = place("y", [P, KD, T])
        sq_at = cursor[0]
        sq = place("sq", [P, KD, T])
        ghi_at = cursor[0]
        g_hi = place("g_hi", [P, FT, T], F32R)
        glo_at = cursor[0]
        g_lo = place("g_lo", [P, FT, T], F32R)
        g_end = cursor[0]
        ones = place("ones", [P, P])
        ident = place("ident", [P, P])
        vec = place("vec", [P, LAYERS, NV])
        uvec = place("uvec", [P, NU])
        sinks = place("sinks", [P, 8])
        eps = place("eps", [P, 2])
        std = place("std", [P, T])
        rstd = place("rstd", [P, T])
        acc = place("acc", [P, T])
        sig = place("sig", [P, 2, T])
        gf = place("gf", [P, 2, T])
        decay_at = cursor[0]
        decay = place("decay", [P, 3, HEADS, T])
        rope_cos = place("rope_cos", [P, T])
        rope_sin = place("rope_sin", [P, T])
        inv_count = place("inv_count", [P, 2, T])
        mixw = place("mixw", [P, 6, P])
        rest_at = cursor[0]

        spans = ((ghi_at + KD * T4, glo_at), (glo_at + KD * T4, g_end), (rest_at, limit))
        one = placer(region(*spans))
        xpad = one("xpad", [P, 2, 16 + T])
        upad = one("upad", [P, 2, TAPS - 1 + T])
        ca = one("ca", [P, 2, T])
        cg = one("cg", [P, 2, T])
        qk_raw = one("qk_raw", [P, 2, T])
        qk_swap = one("qk_swap", [P, 2, T])
        qT = one("qT", [P, HEADS, T])
        kT = one("kT", [P, HEADS, T])
        v_tok = one("v_tok", [P, 3, HEADS * P])
        gate_s = one("gate_s", [P, HEADS, T])
        conv_y = one("conv_y", [P, 2, T])
        conv_t = one("conv_t", [P, 2, T])
        taps = one("taps", [P, TAPS + 1])
        conv_sq = one("conv_sq", [P, 2, T])
        o_sq = conv_sq
        pool_y = one("pool_y", [P, 2, T])
        o_c = one("o_c", [P, HEADS, T])
        o_rstd = one("o_rstd", [P, HEADS, T])
        win = [place(f"win{i}", [P, 2, 16 + T], offset=sq_at + i * 2 * (16 + T) * 4) for i in range(3)]
        pT = place("pT", [P, 2, 3, T], offset=sq_at)
        o_std = place("o_std", [P, 2, T], offset=sq_at + 6 * T4)
        x_tok = place("x_tok", [P, 3, D], offset=ghi_at)

        table = placer(region((decay_at, rest_at)))
        rel_a = table("rel_a", [P, 2, S])
        logc = table("logc", [P, 2, S])
        rel_c = table("rel_c", [P, 2, S])
        mask_d = table("mask_d", [P, 2, S])
        tril = table("tril", [P, P])
        scan_m = table("scan_m", [P, S])
        gup = table("gup", [P, 2, P])
        rcos = table("rcos", [P, S])
        rsin = table("rsin", [P, S])
        both_at = region(*spans)
        both = placer(both_at)
        att_s = both("att_s", [P, 2, 2, S + 1])
        att_p = both("att_p", [P, 2, 2, S + 1])
        att_pT = both("att_pT", [P, 2, 4, P])
        att_max = both("att_max", [P, 2, 2])
        att_sum = both("att_sum", [P, 2, 2])
        att_inv = both("att_inv", [P, 2, 2])
        even = placer(region(*both_at.spans))
        odd = placer(region(*both_at.spans))
        qa = even("qa", [P, 4, S])
        ka = even("ka", [P, 4, S])
        va = even("va", [P, 2, 512])
        qb = even("qb", [P, 2, S])
        kb = even("kb", [P, 2, S])
        vb = even("vb", [P, 2, 512])
        rb = even("rb", [P, 4, S])
        gb = even("gb", [P, S])
        bc = even("bc", [P, 2, S])
        khat = even("khat", [P, 2, S])
        qhat = even("qhat", [P, 2, S])
        att = even("att", [P, 2, 4, P])
        za = place("za", [P, 2, S], offset=sq_at)
        zb = place("zb", [P, 2, S], offset=sq_at + 2048)
        dmid = place("dmid", [P, 2, S], offset=sq_at + 4096)
        dlast = place("dlast", [P, 2, S], offset=sq_at + 6144)
        k_tok = place("k_tok", [P, 2, 2, P], offset=sq_at)
        state = place("state", [P, 3, 2, P], offset=sq_at + 2048)
        dec = place("dec", [P, 2, 4], offset=sq_at + 5120)
        g_sq, g_std = qa, ka
        qc = odd("qc", [P, 4, S])
        kdup = odd("kdup", [P, 2, S])
        vc = odd("vc", [P, 2, P])
        qd = odd("qd", [P, 8, S])
        kd = odd("kd", [P, 8, S])
        vd = odd("vd", [P, 2, 512])
        rt = odd("rt", [P, 2, S])
        cqkv = place("cqkv", [P, 5, S], offset=sq_at)

        ps = [ctx.enter_context(nc.psum_tensor(f"bank{i}", [P, 512], F32)) for i in range(8)]

        per_layer = {}

        def sem(name, in_layer=0):
            s = ctx.enter_context(nc.semaphore(name))
            per_layer[s.name] = in_layer
            return s

        loaded = [sem(f"raw_loaded{i}") for i in range(2)]
        w_hi_done = sem("w_hi_done")
        w_ready = sem("w_ready")
        chunk_used = sem("chunk_used")
        tile_ready = sem("tile_ready", 8 + OUT_CHUNKS)
        x_loaded = sem("x_loaded")
        consts_loaded = sem("consts_loaded")
        consts_set = sem("consts_set")
        tables_loaded = sem("tables_loaded")
        mixw_loaded = sem("mixw_loaded", 16)
        xT_ready = sem("xT_ready")
        y_ready = sem("y_ready", 3 * KD)
        mean_ready = sem("mean_ready", 3)
        acc_added = sem("acc_added", 3 * (KD - 3))
        acc_ready = sem("acc_ready", 3)
        centered = sem("centered", 3 * KD)
        squared = sem("squared", 3 * KD)
        var_ready = sem("var_ready", 3)
        std_ready = sem("std_ready", 3)
        normed = sem("normed", 3 * KD)
        affine = sem("affine", 3 * KD)
        h_done = sem("h_done", 3)
        h_ready = sem("h_ready", 3 * KD)
        up_free = sem("up_free", 2 * FT)
        silu_ready = sem("silu_ready", 2 * FT)
        g_hi_done = sem("g_hi_done", 2 * FT)
        g_ready = sem("g_ready", 2 * FT)
        z_copied = sem("z_copied", 22)
        rope_ready = sem("rope_ready", 2 * HEADS)
        pool_in = sem("pool_in", 1)
        pool_mixed = sem("pool_mixed", 2)
        small_done = sem("small_done", 4)
        conv_in = sem("conv_in", 1)
        conv_mul = sem("conv_mul", TAPS - 1)
        conv_sum = sem("conv_sum", TAPS - 1)
        conv_done = sem("conv_done", 2)
        conv_mean = sem("conv_mean", 1)
        conv_cent = sem("conv_cent", 2)
        conv_sqd = sem("conv_sqd", 2)
        conv_var = sem("conv_var", 1)
        conv_std = sem("conv_std", 1)
        conv_nrm = sem("conv_nrm", 2)
        conv_act = sem("conv_act", 2)
        conv_pwd = sem("conv_pwd", 2)
        ret_s = sem("ret_s", 3 * HEADS)
        ret_p = sem("ret_p", 3 * HEADS)
        ret_o = sem("ret_o", HEADS)
        ret_oc = sem("ret_oc", HEADS)
        ret_mean = sem("ret_mean", HEADS)
        ret_cent = sem("ret_cent", HEADS)
        ret_sqd = sem("ret_sqd", HEADS)
        ret_var = sem("ret_var", HEADS)
        ret_std = sem("ret_std", HEADS)
        ret_done = sem("ret_done", HEADS)
        mix_hi = sem("mix_hi", KD)
        mix_ready = sem("mix_ready", KD)
        x_ready = sem("x_ready")
        z2_copied = sem("z2_copied")
        at_s = sem("at_s")
        at_max = sem("at_max")
        at_exp = sem("at_exp")
        at_inv = sem("at_inv")
        at_norm = sem("at_norm")
        at_t = sem("at_t")
        at_tc = sem("at_tc")
        at_o = sem("at_o")
        at_done = sem("at_done")
        gate_ready = sem("gate_ready")
        gate_log = sem("gate_log")
        gate_cum = sem("gate_cum")
        gate_exp = sem("gate_exp")
        gla_in = sem("gla_in")
        gla_s = sem("gla_s")
        gla_kt = sem("gla_kt")
        gla_att = sem("gla_att")
        gla_ktc = sem("gla_ktc")
        gla_ds = sem("gla_ds")
        gla_state = sem("gla_state")
        gla_o = sem("gla_o")
        gla_sqd = sem("gla_sqd")
        gla_var = sem("gla_var")
        gla_std = sem("gla_std")
        gla_done = sem("gla_done")
        c_sqd = sem("c_sqd")
        c_var = sem("c_var")
        c_std = sem("c_std")
        c_nrm = sem("c_nrm")
        c_hi = sem("c_hi")
        c_ready = sem("c_ready")
        qd_ready = sem("qd_ready")
        qd_copied = sem("qd_copied")
        qd_roped = sem("qd_roped")
        kn_ready = sem("kn_ready")
        kn_copied = sem("kn_copied")
        vd_ready = sem("vd_ready")
        vd_copied = sem("vd_copied")
        kd_ready = sem("kd_ready")
        out_t = sem("out_t")
        out_c = sem("out_c")
        stored = sem("stored")
        dve_seq = sem("dve_seq", DVE_LINKS)
        act_seq = sem("act_seq")
        block = ctx.enter_context(nc.Block())

        def hs(buf, k, lo=0, n=T):
            return buf[:, k * T + lo:k * T + lo + n]

        def half(buf, hd, lo, n):
            return buf[64 * (hd % 2):64 * (hd % 2) + 64, hd // 2, lo:lo + n]

        def xk(k):
            return h[:, k, META:T]

        UNITS = [(t, j) for j in range(4) for t in range(2)]
        UN = len(UNITS)

        def unit_banks(u, start):
            return ps[0:4] if u >= start and u % 2 else ps[4:8]

        def same_banks(u, start):
            v = u - 1 if u <= start else u - 2
            return v if v >= 0 and unit_banks(v, start)[0] is unit_banks(u, start)[0] else None

        QK = range(6, 14)
        VALUES = range(14, 18)
        EVEN_TOKEN = (8, 9, 10, 11, 16, 17, 18, 19)
        ODD_TOKEN = (5,)

        @block.sync
        def _(sp):
            st = Stream()
            sp.dma_start(x_tok[0:META, 0, :], a["meta"]).then_inc(x_loaded, 16)
            sp.dma_start(x_tok[META:P, 0, :], a["x"][0:P - META, :]).then_inc(x_loaded, 16)
            sp.dma_start(x_tok[:, 1, :], a["x"][P - META:2 * P - META, :]).then_inc(x_loaded, 16)
            sp.dma_start(x_tok[0:META, 2, :], a["x"][2 * P - META:SEQ, :]).then_inc(x_loaded, 16)
            sp.dma_start(ident[:], a["ident"]).then_inc(x_loaded, 16)

            def load(src, blocks, ahead, pairs=0):
                slot = st.slot(ahead)
                sp.wait_ge(w_ready, st.value(ahead, pairs, 1))
                sp.dma_start(raw[:, slot, 0:blocks * P], src).then_inc(loaded[slot], 16)

            def ffn(i):
                for name, n, blocks in (("up_w", FT, UP_BLOCKS), ("down_w", KD, DOWN_BLOCKS)):
                    src = a[name].rearrange("f c p n -> (f c) p n")
                    with sp.Fori(0, n // 2) as c:
                        for j in range(2):
                            load(src[bass.ds(c * 2 + i * n + j, 1)].rearrange("a p n -> (a p) n"), blocks, j, c)
                    st.c += n

            def straight(chunks):
                for i, (src, blocks) in enumerate(chunks):
                    load(src, blocks, i)
                st.c += len(chunks)

            with sp.Fori(0, LAYERS) as l:
                st.enter(l)
                ffn(l * 2)
                src = a["in_w"][bass.ds(l, 1)].rearrange("a c p n -> (a c) p n")
                straight([(src[c, :, 0:n * KD * P], n * KD) for c, n in enumerate(IN_GROUPS)])
                src = a["out_w"][bass.ds(l, 1)].rearrange("a c p n -> (a c) p n")
                straight([(src[c], 2 * KD) for c in range(OUT_CHUNKS)])
                ffn(l * 2 + 1)
            st.leave()
            straight([(a["even_w"][c, :, 0:n * KD * P], n * KD) for c, n in enumerate(EVEN_GROUPS)])
            straight([(a["out_w"][2, c], 2 * KD) for c in range(OUT_CHUNKS)])
            ffn(4)
            straight([(a["odd_w"][c, :, 0:n * KD * P], n * KD) for c, n in enumerate(ODD_GROUPS)])
            straight([(a["ukv_w"], 16)] + [(a["uq_w"][c], 12) for c in range(2)])
            straight([(a["out_w"][3, c], 2 * KD) for c in range(OUT_CHUNKS)])
            ffn(5)
            for half_d in range(2):
                sp.wait_ge(out_c, KD // 2 * (half_d + 1))
                cols = slice(half_d * D // 2, (half_d + 1) * D // 2)
                sp.dma_start(a["out"][:, cols].rearrange("(t p) n -> p t n", p=P), x_tok[:, 0:2, cols])\
                    .then_inc(stored, 16)
            sp.wait_ge(stored, 32)

        @block.gpsimd
        def _(pool):
            seen = Seen(per_layer)
            for dst, name in ((vec, "vec"), (uvec, "uvec"), (decay, "decay"), (rope_cos, "rope_cos"),
                              (rope_sin, "rope_sin"), (inv_count, "inv_count"), (sinks, "sinks")):
                pool.dma_start(dst[:], a[name]).then_inc(consts_loaded, 16)

            def add_tiles(ready, source, n):
                for m in range(1, KD - 1):
                    pool.wait_ge(ready, seen.at(ready, m + 1))
                    if m > 1:
                        pool.wait_ge(acc_added, seen.next(acc_added))
                    pool.tensor_tensor(acc[:, 0:n], acc[:, 0:n] if m > 1 else source[:, 0, 0:n], source[:, m, 0:n],
                                       ALU.add).then_inc(acc_added if m < KD - 2 else acc_ready, 1)
                seen.skip(ready, KD)

            add_tiles(y_ready, y, T)
            for l in range(LAYERS):
                pool.wait_ge(h_ready, l * (3 * KD) + KD)
                pool.dma_start(mixw[:], a["mixw"][l])\
                    .then_inc(mixw_loaded, 16)
                add_tiles(y_ready, y, T)
                pool.wait_ge(conv_in, seen.next(conv_in))

                def product(i):
                    if i >= 3:
                        pool.wait_ge(conv_sum, seen.at(conv_sum, i - 1))
                    pool.tensor_scalar(conv_t[:, i % 2, :], upad[:, 1, i:i + T], taps[:, i:i + 1], 0.0,
                                       ALU.mult, ALU.add).then_inc(conv_mul, 1)

                pool.tensor_scalar(conv_y[:, 1, :], upad[:, 1, 0:T], taps[:, 0:1], taps[:, TAPS:TAPS + 1],
                                   ALU.mult, ALU.add).then_inc(conv_sum, 1)
                product(1)
                for i in range(1, TAPS):
                    if i + 1 < TAPS:
                        product(i + 1)
                    pool.wait_ge(conv_mul, seen.at(conv_mul, i))
                    pool.wait_ge(conv_sum, seen.at(conv_sum, i))
                    pool.tensor_tensor(conv_y[:, 1, :], conv_y[:, 1, :], conv_t[:, i % 2, :], ALU.add)\
                        .then_inc(conv_done if i == TAPS - 1 else conv_sum, 1)
                seen.skip(conv_mul, TAPS - 1)
                seen.skip(conv_sum, TAPS - 1)
                add_tiles(y_ready, y, T)
                if l == LAYERS - 1:
                    pool.wait_ge(h_ready, KD + (LAYERS - 1) * 3 * KD + 2 * KD)
                    for dst, name in ((rel_a, "rel_a"), (logc, "logc"), (rel_c, "rel_c"), (mask_d, "mask_d"),
                                      (tril, "tril"), (scan_m, "scan_m"), (gup, "gup"), (rcos, "rcos"),
                                      (rsin, "rsin")):
                        pool.dma_start(dst[:], a[name]).then_inc(tables_loaded, 16)
                add_tiles(y_ready, y, T)
            seen.skip(squared, KD + LAYERS * 3 * KD)

            def divide(units):
                for u in units:
                    t, b = UNITS[u % UN][0], u % 2
                    pool.wait_ge(at_inv, u + 1)
                    for e in range(2):
                        last = pool.tensor_scalar(att_p[:, b, e, 1:1 + P * (t + 1)],
                                                  att_p[:, b, e, 1:1 + P * (t + 1)],
                                                  att_inv[:, b, e:e + 1], None, ALU.mult)
                    last.then_inc(at_norm, 1)

            for units in (range(UN), range(UN, 3 * UN)):
                seen.skip(squared, KD)
                divide(units)
                add_tiles(squared, sq, S)
                seen.skip(squared, KD)
                add_tiles(squared, sq, S)

        @block.tensor
        def _(pe):
            seen, st = Seen(per_layer), Stream()

            def mm3(out, w, x, first, last):
                pe.matmul(out, w[0], x[0], start=first, stop=False)
                pe.matmul(out, w[0], x[1], start=False, stop=False)
                return pe.matmul(out, w[1], x[0], start=False, stop=last)

            def wpair(slot, b, n=1):
                return w_hi[:, slot, b * P:(b + n) * P], w_lo[:, slot, b * P:(b + n) * P]

            def hpair(k, lo=0, n=T):
                return hs(h_hi, k, lo, n), hs(h_lo, k, lo, n)

            def chunk_is_split(ahead, pairs=0):
                return st.value(ahead, pairs, 3)

            def squares_sum(n=T):
                for k in range(KD):
                    pe.wait_ge(squared, seen.next(squared))
                    last = pe.matmul(ps[7][:, 0:n], ones[:], sq[:, k, 0:n], start=k == 0, stop=k == KD - 1)
                last.then_inc(var_ready, 1)

            def output_sum(n):
                ready, source, bank = (y_ready, y, ps[6]) if n == T else (squared, sq, ps[7])
                pe.wait_ge(acc_ready, seen.next(acc_ready))
                pe.matmul(bank[:, 0:n], ones[:], acc[:, 0:n], start=True, stop=False)
                if n < T:
                    seen.skip(y_ready, KD)
                pe.wait_ge(ready, seen.next(ready, KD))
                pe.matmul(bank[:, 0:n], ones[:], source[:, KD - 1, 0:n], start=False, stop=True)\
                    .then_inc(mean_ready if n == T else var_ready, 1)

            def first_chunk(tiles, banks, n, slot):
                for k in range(KD):
                    pe.wait_ge(h_ready, seen.next(h_ready))
                    lasts = [mm3(bank[:, 0:n], wpair(slot, k * tiles + e), hpair(k, 0, n), k == 0, k == KD - 1)
                             for e, bank in zip(range(tiles), banks)]
                return lasts

            def ffn(n=T):
                def up(i, j):
                    slot = st.slot(j)
                    pe.wait_ge(w_ready, chunk_is_split(j, i))
                    pe.wait_ge(up_free, seen.at(up_free, i * 2 + (j + 1)))
                    if isinstance(i, int) and (i, j) == (0, 0):
                        last = first_chunk(2, ps[0:2], n, slot)[-1]
                    else:
                        for e in range(2):
                            for k in range(KD):
                                last = mm3(ps[2 * j + e][:, 0:n], wpair(slot, 2 * k + e), hpair(k, 0, n),
                                           k == 0, k == KD - 1)
                    last.then_inc(chunk_used, 1)

                def down(i, j):
                    slot = st.slot(j)
                    pe.wait_ge(w_ready, chunk_is_split(j, i))
                    pe.wait_ge(y_ready, seen.at(y_ready, i * 2 + (j - 1)))
                    if isinstance(i, int) and (i, j) == (0, 0):
                        pe.wait_ge(g_ready, seen.at(g_ready, FT - 2))
                    for k in range(FT):
                        if isinstance(i, int) and (i, j, k) == (0, 0, FT - 2):
                            pe.wait_ge(g_ready, seen.at(g_ready, FT))
                        last = mm3(ps[4 + j][:, 0:n], wpair(slot, k), (g_hi[:, k, 0:n], g_lo[:, k, 0:n]),
                                   k == 0, k == FT - 1)
                    last.then_inc(chunk_used, 1)

                up(0, 0)
                up(0, 1)
                with pe.Fori(1, FT // 2) as i:
                    up(i, 0)
                    up(i, 1)
                st.c += FT
                seen.skip(up_free, FT)
                down(0, 0)
                down(0, 1)
                with pe.Fori(1, KD // 2) as i:
                    down(i, 0)
                    down(i, 1)
                st.c += KD
                seen.skip(g_ready, FT)
                output_sum(n)

            def project_first(tiles, n=T):
                if 0 in tiles:
                    pe.wait_ge(w_ready, chunk_is_split(0))
                for k in tiles:
                    pe.wait_ge(mix_ready, seen.next(mix_ready))
                    lasts = [mm3(ps[4 + e][:, 0:n], wpair(st.slot(0), e * KD + k),
                                 (g_hi[:, k, 0:n], g_lo[:, k, 0:n]), k == 0, k == KD - 1) for e in range(2)]
                if KD - 1 in tiles:
                    lasts[0].then_inc(tile_ready, 1)
                    lasts[1].then_inc(chunk_used, 1)

            def project_out(n=T):
                for c in range(1, OUT_CHUNKS):
                    pe.wait_ge(w_ready, chunk_is_split(c))
                    for e in range(2):
                        pe.wait_ge(y_ready, seen.at(y_ready, 2 * c + e - 1))
                        for k in range(KD):
                            last = mm3(ps[4 + e][:, 0:n], wpair(st.slot(c), e * KD + k),
                                       (g_hi[:, k, 0:n], g_lo[:, k, 0:n]), k == 0, k == KD - 1)
                        last.then_inc(chunk_used if e else tile_ready, 1)
                st.c += OUT_CHUNKS
                output_sum(n)

            def in_tiles(sizes, order, by_token, tokens, banks, copied, n, between):
                z = 0

                def bank_is_free(z):
                    if z >= banks:
                        pe.wait_ge(copied, seen.at(copied, z - banks + 1))

                for c, tiles in enumerate(sizes):
                    pe.wait_ge(w_ready, chunk_is_split(c))
                    slot = st.slot(c)
                    if c == 0:
                        lasts = first_chunk(tiles, ps, n, slot)
                    if order[z] in by_token:
                        for e in range(2):
                            bank_is_free(z + e)
                        for t, m in enumerate(tokens):
                            bank, o = ps[(z + t // 2) % banks], (t % 2) * 2 * P
                            for k in range(KD):
                                last = mm3(bank[0:m, o:o + 2 * P], hpair(k, t * P, m), wpair(slot, 2 * k, 2),
                                           k == 0, k == KD - 1)
                        last.then_inc(chunk_used, 1)
                        z += 2
                    else:
                        for e in range(tiles):
                            bank_is_free(z)
                            if c == 0:
                                last = lasts[e]
                            elif e and order[z] in ODD_TOKEN and sizes is ODD_GROUPS:
                                for t in range(2):
                                    for k in range(KD):
                                        last = mm3(ps[z % banks][:, t * 2 * P:(t + 1) * 2 * P], hpair(k, t * P, P),
                                                   wpair(slot, 2 * k, 2), k == 0, k == KD - 1)
                            else:
                                for k in range(KD):
                                    last = mm3(ps[z % banks][:, 0:n], wpair(slot, k * tiles + e), hpair(k, 0, n),
                                               k == 0, k == KD - 1)
                            last.then_inc(chunk_used if e == tiles - 1 else tile_ready, 1)
                            z += 1
                    between(c)
                st.c += len(sizes)
                pe.wait_ge(copied, seen.next(copied, z))

            pe.wait_ge(x_loaded, 80)
            for k in range(KD):
                if k >= 4:
                    pe.wait_ge(y_ready, k - 3)
                for t, (lo, m) in enumerate(KTOK):
                    last = pe.transpose(ps[k % 4][:, lo:lo + m], x_tok[0:m, t, k * P:(k + 1) * P], ident[0:m, 0:m])
                last.then_inc(xT_ready, 1)
            pe.wait_ge(consts_set, 1)
            output_sum(T)
            squares_sum()

            with pe.Fori(0, LAYERS) as l:
                seen.enter(l)
                st.enter(l)
                ffn()
                squares_sum()
                in_tiles(IN_GROUPS, range(22), VALUES, [m for _, m in KTOK], 4, z_copied, T, lambda c: None)
                pe.wait_ge(mixw_loaded, seen.next(mixw_loaded, 16))
                pe.wait_ge(pool_in, seen.next(pool_in))
                for j in range(2):
                    pe.matmul(ps[j][:, 0:T], mixw[:, j, :], pool_y[:, j, :], start=True, stop=True)\
                        .then_inc(pool_mixed, 1)
                pe.wait_ge(conv_done, seen.next(conv_done, 2))
                for j in range(2):
                    last = pe.matmul(ps[6][:, 0:T], ones[:], conv_y[:, j, :], start=j == 0, stop=j == 1)
                last.then_inc(conv_mean, 1)
                for j in range(2):
                    pe.wait_ge(conv_sqd, seen.next(conv_sqd))
                    last = pe.matmul(ps[7][:, 0:T], ones[:], conv_sq[:, j, :], start=j == 0, stop=j == 1)
                last.then_inc(conv_var, 1)
                pe.wait_ge(rope_ready, seen.next(rope_ready, 2 * HEADS))
                pe.wait_ge(small_done, seen.next(small_done, 2))

                def scores(hd):
                    for t, (lo, m) in enumerate(KTOK):
                        n = 3 * hd + t
                        if n >= 4:
                            pe.wait_ge(ret_p, seen.at(ret_p, n - 3))
                        pe.matmul(ps[n % 4][0:m, 0:T], kT[:, hd, lo:lo + m], qT[:, hd, :],
                                  start=True, stop=True).then_inc(ret_s, 1)

                def values(hd):
                    if hd >= 2:
                        pe.wait_ge(ret_oc, seen.at(ret_oc, hd - 1))
                    for t, (lo, m) in enumerate(KTOK):
                        pe.wait_ge(ret_p, seen.at(ret_p, 3 * hd + t + 1))
                        last = pe.matmul(ps[4 + hd % 2][:, 0:T], v_tok[0:m, t, hd * P:(hd + 1) * P],
                                         pT[0:m, hd % 2, t, :], start=t == 0, stop=t == 2)
                    last.then_inc(ret_o, 1)

                def mean(hd):
                    if hd == 0:
                        pe.wait_ge(small_done, seen.next(small_done, 2))
                    else:
                        pe.wait_ge(ret_cent, seen.at(ret_cent, hd))
                    pe.wait_ge(ret_oc, seen.at(ret_oc, hd + 1))
                    pe.matmul(ps[6][:, 0:T], ones[:], o_c[:, hd, :], start=True, stop=True).then_inc(ret_mean, 1)

                def variance(hd):
                    if hd:
                        pe.wait_ge(ret_std, seen.at(ret_std, hd))
                    pe.wait_ge(ret_sqd, seen.at(ret_sqd, hd + 1))
                    pe.matmul(ps[7][:, 0:T], ones[:], o_sq[:, hd % 2, :], start=True, stop=True)\
                        .then_inc(ret_var, 1)

                for i in range(HEADS + 3):
                    if i < HEADS:
                        scores(i)
                    if i == 1:
                        pe.wait_ge(conv_act, seen.next(conv_act, 2))
                        for j in range(2):
                            for k in range(2):
                                last = pe.matmul(ps[6 + j][:, 0:T], mixw[:, 2 + 2 * k + j, :], conv_y[:, k, :],
                                                 start=k == 0, stop=k == 1)
                            last.then_inc(conv_pwd, 1)
                    if 0 <= i - 1 < HEADS:
                        values(i - 1)
                    if 0 <= i - 2 < HEADS:
                        mean(i - 2)
                    if i == HEADS + 2:
                        project_first(range(4))
                    if 0 <= i - 3:
                        variance(i - 3)
                seen.skip(ret_p, 3 * HEADS)
                for s in (ret_oc, ret_cent, ret_std, ret_sqd):
                    seen.skip(s, HEADS)
                project_first(range(4, KD))
                project_out()
                squares_sum()
                ffn()
                squares_sum()
            seen.leave()
            st.leave()

            def attention(u, units, start, base, q, k, v, ready, v_ready):
                if u < units:
                    t, j = UNITS[u % UN]
                    before = same_banks(u, start)
                    ready(u)
                    if before is not None:
                        pe.wait_ge(at_max, base + before + 1)
                    for e in range(2):
                        last = pe.matmul(unit_banks(u, start)[e][:, 0:P * (t + 1)], q(u, 2 * j + e, t),
                                         k(u, 2 * j + e, t), start=True, stop=True)
                    last.then_inc(at_s, 1)
                if 0 <= u - 3 < units:
                    u -= 3
                    t, j = UNITS[u % UN]
                    before = same_banks(u, start)
                    v_ready(u)
                    pe.wait_ge(at_tc, base + u + 1)
                    if before is not None:
                        pe.wait_ge(at_done, base + before + 1)
                    for e in range(2):
                        for kt in range(t + 1):
                            last = pe.matmul(unit_banks(u, start)[3][64 * e:64 * e + 64, 0:P], v(u, 2 * j + e, kt),
                                             att_pT[:, u % 2, 2 * e + kt, :], start=kt == 0, stop=kt == t)
                    last.then_inc(at_o, 1)
                    u += 3
                if 0 <= u - 2 < units:
                    u -= 2
                    t, j = UNITS[u % UN]
                    before = same_banks(u, start)
                    pe.wait_ge(at_norm, base + u + 1)
                    if before is not None:
                        pe.wait_ge(at_tc, base + before + 1)
                    for e in range(2):
                        for kt in range(t + 1):
                            last = pe.transpose(unit_banks(u, start)[2][:, (2 * e + kt) * P:(2 * e + kt + 1) * P],
                                                att_p[:, u % 2, e, 1 + kt * P:1 + (kt + 1) * P], ident[:])
                    last.then_inc(at_t, 1)

            pe.wait_ge(tables_loaded, 16 * 9)
            seen.skip(h_ready, KD)
            squares_sum(S)

            def step_a(u):
                attention(u, UN, UN, 0, lambda u, hd, t: half(qa, hd, t * P, P),
                          lambda u, hd, t: half(ka, hd, 0, P * (t + 1)),
                          lambda u, hd, kt: va[:, kt, hd * 64:hd * 64 + 64],
                          lambda u: pe.wait_ge(z2_copied, 4 * (u // 2) + 2),
                          lambda u: pe.wait_ge(z2_copied, 4 if u < 4 else 12))

            def between(c):
                if c == 4:
                    pe.wait_ge(z2_copied, 7)
                    for j in range(2):
                        last = pe.matmul(ps[3][:, j * S:(j + 1) * S], gup[0:16, j, :], gb[0:16, :],
                                         start=True, stop=True)
                    last.then_inc(gate_ready, 1)
                if 1 <= c < UN + 4:
                    step_a(c - 1)

            in_tiles(EVEN_GROUPS, EVEN_ORDER, EVEN_TOKEN, (P, P), 3, z2_copied, S, between)
            pe.wait_ge(at_done, UN)
            pe.wait_ge(gla_in, 1)
            for t in range(2):
                for hd in range(4):
                    last = pe.matmul(ps[2 * (hd % 2) + t][:, (hd // 2) * P:(hd // 2 + 1) * P], half(kb, hd, t * P, P),
                                     half(qb, hd, t * P, P), start=True, stop=True)
            last.then_inc(gla_s, 1)
            for t in range(2):
                for j in range(2):
                    last = pe.transpose(ps[7][:, (2 * t + j) * P:(2 * t + j + 1) * P],
                                        khat[:, j, t * P:(t + 1) * P], ident[:])
            last.then_inc(gla_kt, 1)
            pe.wait_ge(gla_ktc, 1)
            for n in range(3):
                r = 64 * (n % 2)
                for hd in range(4):
                    e = 64 * (hd % 2)
                    last = pe.matmul(ps[4 + n][e:e + 64, (hd // 2) * P:(hd // 2 + 1) * P],
                                     k_tok[r:r + 64, n // 2, hd // 2, e:e + 64],
                                     vb[r:r + 64, n // 2, hd * P:(hd + 1) * P], start=True, stop=True)
            last.then_inc(gla_ds, 1)
            pe.wait_ge(gla_att, 1)
            pe.wait_ge(gla_state, 1)
            for hd in range(5):
                if hd < 4:
                    bank = ps[4 + hd]
                    for t in range(2):
                        o = t * P
                        pe.matmul(bank[:, o:o + P], vb[:, t, hd * P:(hd + 1) * P], att[:, t, hd, :],
                                  start=True, stop=False)
                        across = (1,) if t == 0 else (2, 3)
                        for n in across:
                            o = 64 * n
                            last = pe.matmul(bank[:, o:o + 64], half(state[:, n - 1], hd, 0, P),
                                             half(qhat, hd, 64 * n, 64), start=False, stop=n == across[-1])
                    last.then_inc(gla_o, 1)
                if hd:
                    pe.wait_ge(gla_sqd, hd)
                    pe.matmul(ps[hd - 1][:, 0:S], ones[:], g_sq[:, hd - 1, :], start=True, stop=True)\
                        .then_inc(gla_var, 1)
            pe.wait_ge(gla_done, 2)
            project_first(range(KD), S)
            project_out(S)
            squares_sum(S)
            ffn(S)

            squares_sum(S)

            def step_cd(u):
                def ready(u):
                    if u < UN:
                        pe.wait_ge(z2_copied, 25 + 8 + u // 2 + 1)
                    else:
                        pe.wait_ge(qd_roped, 2 * (u % UN // 2) + 2)
                        pe.wait_ge(kd_ready, 1)

                attention(u, 2 * UN, UN, UN,
                          lambda u, hd, t: half(qc, hd, t * P, P) if u < UN else qd[0:96, hd, t * P:(t + 1) * P],
                          lambda u, hd, t: kdup[64 * (hd % 2):64 * (hd % 2) + 64, hd // 4, 0:P * (t + 1)]
                          if u < UN else kd[0:96, hd, 0:P * (t + 1)],
                          lambda u, hd, kt: vc[:, kt, (hd // 4) * 64:(hd // 4) * 64 + 64]
                          if u < UN else vd[:, kt, hd * 64:hd * 64 + 64], ready, lambda u: None)

            def between(c):
                if c == 3:
                    for g, (k0, n) in enumerate(((0, 3), (3, 2))):
                        pe.wait_ge(c_sqd, g + 1)
                        for k in range(n):
                            last = pe.matmul(ps[6 + g][:, 0:S], ones[:], y[:, k0 + k, 0:S],
                                             start=k == 0, stop=k == n - 1)
                        last.then_inc(c_var, 1)
                if c >= 4:
                    step_cd(c - 4)

            in_tiles(ODD_GROUPS, ODD_ORDER, (), (P, P), 3, z2_copied, S, between)

            def latent(k, lo, n):
                return g_hi[:, k, lo:lo + n], g_lo[:, k, lo:lo + n]

            pe.wait_ge(w_ready, chunk_is_split(0))
            pe.wait_ge(c_ready, 5)
            for j in range(4):
                if j >= 2:
                    pe.wait_ge(kn_copied, j - 1)
                for k in range(2):
                    last = mm3(ps[j % 2][:, 0:S], wpair(st.slot(0), 8 * k + j), latent(3 + k, 0, S), k == 0, k == 1)
                last.then_inc(kn_ready, 1)
            step_cd(2)
            for t in range(2):
                for k in range(2):
                    last = mm3(ps[2 + t][:, 0:512], latent(3 + k, t * P, P), wpair(st.slot(0), 8 * k + 4, 4),
                               k == 0, k == 1)
                last.then_inc(chunk_used if t else vd_ready, 1)
            step_cd(3)
            pe.wait_ge(kn_copied, 4)
            pe.wait_ge(vd_copied, 2)
            for c in range(2):
                pe.wait_ge(w_ready, chunk_is_split(1 + c))
                for e in range(4):
                    z = 4 * c + e
                    if z >= 4:
                        pe.wait_ge(qd_copied, z - 3)
                    for k in range(3):
                        last = mm3(ps[z % 4][:, 0:S], wpair(st.slot(1 + c), 3 * e + k), latent(k, 0, S),
                                   k == 0, k == 2)
                    last.then_inc(chunk_used if e == 3 else qd_ready, 1)
                    if e % 2:
                        step_cd(4 + z // 2)
            st.c += 3
            pe.wait_ge(qd_copied, 8)
            for u in range(UN, 2 * UN + 3):
                step_cd(u)
            pe.wait_ge(at_done, 3 * UN)
            project_first(range(KD), S)
            project_out(S)
            squares_sum(S)
            ffn(S)
            for k in range(KD):
                pe.wait_ge(x_ready, 3 * KD + k + 1)
                for t in range(2):
                    last = pe.transpose(ps[k][:, t * P:(t + 1) * P], h[:, k, META + t * P:META + (t + 1) * P],
                                        ident[:])
                last.then_inc(out_t, 1)

        @block.scalar
        def _(act):
            seen, st = Seen(per_layer), Stream()

            def split_next(blocks, pairs=0, ahead=1):
                if blocks:
                    slot = st.slot(ahead)
                    act.wait_ge(loaded[slot], st.loads(ahead, pairs))
                    act.wait_ge(chunk_used, st.value(ahead, pairs))
                    act.activation(w_hi[:, slot, 0:blocks * P], raw[:, slot, 0:blocks * P], ACT.Copy)\
                        .then_inc(w_hi_done, 1)

            def vcol(l, col):
                return vec[:, bass.ds(l, 1), col:col + 1].rearrange("p a b -> p (a b)")

            def squares(source, ready, n):
                for k in range(KD):
                    if ready is not None:
                        act.wait_ge(ready, seen.next(ready))
                    act.activation(sq[:, k, 0:n], source(k), ACT.Square).then_inc(squared, 1)

            def deviation(n):
                act.wait_ge(var_ready, seen.next(var_ready))
                act.activation(std[:, 0:n], ps[7][:, 0:n], ACT.Sqrt, scale=1.0 / D,
                               bias=eps[:, 0:1] if n == T else eps[:, 1:2]).then_inc(std_ready, 1)

            def layer_norm(bias, early):
                split_next(early)
                squares(lambda k: y[:, k, :], centered, T)
                deviation(T)
                for k in range(KD):
                    act.wait_ge(normed, seen.next(normed))
                    act.activation(hs(h_hi, k), y[:, k, :], ACT.Identity, bias=bias(k)).then_inc(affine, 1)
                for k in range(KD):
                    last = act.activation(h[:, k, :], y[:, k, :], ACT.Identity, bias=bias(k))
                last.then_inc(h_done, 1)

            def pre_norm(ready):
                squares(xk, ready, S)
                deviation(S)
                for k in range(KD):
                    act.wait_ge(normed, seen.next(normed))
                    act.activation(hs(h_hi, k, 0, S), y[:, k, 0:S], ACT.Copy).then_inc(affine, 1)

            def post_norm(early):
                split_next(early)
                deviation(S)
                seen.skip(normed, KD)

            def square_tile(m):
                act.wait_ge(y_ready, seen.at(y_ready, m + 1))
                f = bass.ds(m, 1)
                act.activation(sq[:, f, 0:S], y[:, f, 0:S], ACT.Square).then_inc(squared, 1)

            def ffn(after, n=T):
                def up(i, j, last):
                    if not (isinstance(i, int) and (i, j) == (0, 0)):
                        split_next(DOWN_BLOCKS if last else UP_BLOCKS, i, j + 1)
                    act.wait_ge(chunk_used, st.value(j, i, 2))
                    act.activation(sig[:, j, 0:n], ps[2 * j][:, 0:n], ACT.Silu).then_inc(silu_ready, 1)

                def down(i, j, last):
                    split_next(after if last else DOWN_BLOCKS, i, j + 1)
                    if n < T:
                        square_tile(i * 2 + j)

                pairs_of(act, FT, up)
                st.c += FT
                pairs_of(act, KD, down)
                st.c += KD
                seen.skip(y_ready, KD)

            def tile_is_ready(ahead, e, tiles):
                if e == tiles - 1:
                    act.wait_ge(chunk_used, st.value(ahead, 0, 2))
                else:
                    act.wait_ge(tile_ready, seen.next(tile_ready))

            def in_tiles(sizes, order, by_token, banks, after, copy, before=lambda c: None):
                z = 0
                for c, tiles in enumerate(sizes):
                    if c:
                        split_next(sizes[c + 1] * KD if c + 1 < len(sizes) else after, 0, c + 1)
                    before(c)
                    if order[z] in by_token:
                        tile_is_ready(c, 1, 2)
                        copy(order[z], ps[z % banks])
                        copy(order[z + 1], ps[(z + 1) % banks])
                        z += 2
                        continue
                    for e in range(tiles):
                        tile_is_ready(c, e, tiles)
                        copy(order[z], ps[z % banks])
                        z += 1
                st.c += len(sizes)

            def mix_split(k, n):
                act.activation(g_hi[:, k, 0:n], y[:, k, 0:n], ACT.Copy).then_inc(mix_hi, 1)

            def project_out(n=T):
                for c in range(OUT_CHUNKS):
                    if c:
                        split_next(2 * KD if c + 1 < OUT_CHUNKS else UP_BLOCKS, 0, c + 1)
                    if n < T:
                        square_tile(2 * c)
                        square_tile(2 * c + 1)
                seen.skip(tile_ready, OUT_CHUNKS)
                seen.skip(y_ready, KD)
                st.c += OUT_CHUNKS

            seen.skip(y_ready, KD)
            act.wait_ge(loaded[0], 16)
            act.activation(w_hi[:, 0, 0:UP_BLOCKS * P], raw[:, 0, 0:UP_BLOCKS * P], ACT.Copy)\
                .then_inc(w_hi_done, 1)
            act.wait_ge(consts_loaded, 16 * 7)
            act.wait_ge(consts_set, 1)
            layer_norm(lambda k: uvec[:, U_INB + k:U_INB + k + 1], UP_BLOCKS)
            with act.Fori(0, LAYERS) as l:
                seen.enter(l)
                st.enter(l)
                ffn(IN_GROUPS[0] * KD)
                layer_norm(lambda k: vcol(l, V_LN + 8 + k), IN_GROUPS[1] * KD)

                def copy(z, bank):
                    if z < 2:
                        last = act.activation(xpad[:, z, 16:16 + T], bank[:, 0:T], ACT.Copy)
                    elif z < 4:
                        last = act.activation(ca[:, z - 2, :], bank[:, 0:T], ACT.Copy)
                    elif z < 6:
                        last = act.activation(cg[:, z - 4, :], bank[:, 0:T], ACT.Sigmoid)
                    elif z in QK:
                        i = z - QK[0]
                        if i >= 2:
                            act.wait_ge(rope_ready, seen.at(rope_ready, i - 1))
                        act.activation(qk_raw[:, i % 2, :], bank[:, 0:T], ACT.Copy)
                        act.activation(qk_swap[0:64, i % 2, :], bank[64:128, 0:T], ACT.Copy)
                        last = act.activation(qk_swap[64:128, i % 2, :], bank[0:64, 0:T], ACT.Copy)
                    elif z in VALUES:
                        i = (z - VALUES[0]) // 2 * 2
                        if z % 2 == 0:
                            last = act.activation(v_tok[:, 0:2, i * P:(i + 2) * P],
                                                  bank[:, :].rearrange("p (t n) -> p t n", t=2), ACT.Copy)
                        else:
                            m = KTOK[2][1]
                            last = act.activation(v_tok[0:m, 2, i * P:(i + 2) * P], bank[0:m, 0:2 * P], ACT.Copy)
                    else:
                        last = act.activation(gate_s[:, z - 18, :], bank[:, 0:T], ACT.Silu)
                    last.then_inc(z_copied, 1)

                in_tiles(IN_GROUPS, range(22), VALUES, 4, 2 * KD, copy)
                for j in range(2):
                    act.wait_ge(pool_mixed, seen.next(pool_mixed))
                    act.activation(y[:, j, :], ps[j][:, 0:T], ACT.Identity, scale=vcol(l, V_PSC + j))\
                        .then_inc(small_done, 1)
                for j in range(2):
                    act.wait_ge(conv_cent, seen.next(conv_cent))
                    act.activation(conv_sq[:, j, :], conv_y[:, j, :], ACT.Square).then_inc(conv_sqd, 1)
                act.wait_ge(conv_var, seen.next(conv_var))
                act.activation(std[:], ps[7][:, 0:T], ACT.Sqrt, scale=1.0 / (2 * P), bias=eps[:, 0:1])\
                    .then_inc(conv_std, 1)
                for j in range(2):
                    act.wait_ge(conv_nrm, seen.next(conv_nrm))
                    act.activation(conv_y[:, j, :], conv_y[:, j, :], ACT.Silu, scale=vcol(l, V_CG + j),
                                   bias=vcol(l, V_CB + j)).then_inc(conv_act, 1)
                split_next(2 * KD, 0, 1)
                for j in range(2):
                    act.wait_ge(conv_pwd, seen.next(conv_pwd))
                    act.activation(y[:, 2 + j, :], ps[6 + j][:, 0:T], ACT.Copy).then_inc(small_done, 1)
                act.wait_ge(small_done, seen.next(small_done, 4))
                for k in range(4):
                    mix_split(k, T)
                for i in range(HEADS + 2):
                    if i < HEADS:
                        act.wait_ge(ret_cent, seen.at(ret_cent, i + 1))
                        act.activation(o_sq[:, i % 2, :], o_c[:, i, :], ACT.Square).then_inc(ret_sqd, 1)
                    if 0 <= i - 1 < HEADS:
                        hd = i - 1
                        act.wait_ge(ret_var, seen.next(ret_var))
                        act.activation(o_std[:, hd % 2, :], ps[7][:, 0:T], ACT.Sqrt, scale=1.0 / P,
                                       bias=eps[:, 0:1]).then_inc(ret_std, 1)
                    if i >= 2:
                        act.wait_ge(ret_done, seen.next(ret_done))
                        mix_split(4 + i - 2, T)
                seen.skip(ret_cent, HEADS)
                project_out()
                layer_norm(lambda k: vcol(l, V_LN + 24 + k), UP_BLOCKS)
                ffn(UP_BLOCKS)
                layer_norm(lambda k: vcol(l, V_LN + 40 + k), UP_BLOCKS)
            seen.leave()
            st.leave()

            def attention(u, units, start, base, low, tile):
                if 0 <= u - 2 < units:
                    v = u - 2
                    bank = unit_banks(v, start)[2]
                    act.wait_ge(at_t, base + v + 1)
                    if UNITS[v % UN][0]:
                        last = act.activation(att_pT[:, v % 2].rearrange("p a n -> p (a n)"), bank[:, :], ACT.Copy)
                    else:
                        last = act.activation(att_pT[:, v % 2, 0:3:2, :],
                                              bank[:, :].rearrange("p (a n) -> p a n", n=P)[:, 0:3:2, :], ACT.Copy)
                    last.then_inc(at_tc, 1)
                if u < units:
                    t, j = UNITS[u % UN]
                    act.wait_ge(at_max, base + u + 1)
                    for e in range(2):
                        last = act.activation(att_p[:, u % 2, e, low(u):1 + P * (t + 1)],
                                              att_s[:, u % 2, e, low(u):1 + P * (t + 1)], ACT.Exp,
                                              bias=att_max[:, u % 2, e:e + 1], accum_out=att_sum[:, u % 2, e:e + 1])
                    last.then_inc(at_exp, 1)
                if 0 <= u - 3 < units:
                    v = u - 3
                    t, j = UNITS[v % UN]
                    act.wait_ge(at_o, base + v + 1)
                    act.activation(y[:, tile(v) + j, t * P:(t + 1) * P], unit_banks(v, start)[3][:, 0:P], ACT.Copy)\
                        .then_inc(at_done, 1)

            act.wait_ge(h_done, 1 + 3 * LAYERS)
            pre_norm(None)
            EIGHTH = 64 ** -0.5

            def copy(z, bank):
                if z < 4:
                    last = act.activation(qa[:, z, :], bank[:, 0:S], ACT.Copy, scale=EIGHTH)
                elif z < 8:
                    last = act.activation(ka[:, z - 4, :], bank[:, 0:S], ACT.Copy)
                elif z in EVEN_TOKEN:
                    dst, i = (va, z - 8) if z < 12 else (vb, z - 16)
                    if z % 2:
                        return
                    act.activation(dst[:, :, i * P:(i + 2) * P],
                                   bank[:, :].rearrange("p (t n) -> p t n", t=2), ACT.Copy).then_inc(z2_copied, 2)
                    return
                elif z < 14:
                    last = act.activation(qb[:, z - 12, :], bank[:, 0:S], ACT.Copy, scale=EIGHTH)
                elif z < 16:
                    last = act.activation(kb[:, z - 14, :], bank[:, 0:S], ACT.Copy)
                elif z < 24:
                    last = act.activation(rb[:, z - 20, :], bank[:, 0:S], ACT.Silu)
                else:
                    last = act.activation(gb[0:16, :], bank[0:16, 0:S], ACT.Copy)
                last.then_inc(z2_copied, 1)

            def before(c):
                if 2 <= c < UN + 5:
                    attention(c - 2, UN, UN, 0, lambda u: 1, lambda u: 0)
                if c == 5:
                    act.wait_ge(gate_ready, 1)
                    for j in range(2):
                        last = act.activation(zb[:, j, :], ps[3][:, j * S:(j + 1) * S], ACT.Abs,
                                              bias=uvec[:, U_GATEB + j:U_GATEB + j + 1])
                    last.then_inc(act_seq, 1)
                    act.wait_ge(act_seq, 1)
                    act.activation(zb[:], zb[:], ACT.Exp, scale=-1.0).then_inc(act_seq, 1)
                    act.wait_ge(act_seq, 2)
                    act.activation(zb[:], zb[:], ACT.Ln, bias=1.0).then_inc(gate_log, 1)
                if c == 8:
                    act.wait_ge(gate_cum, 1)
                    act.activation(za[:], dmid[:], ACT.Exp)
                    act.activation(zb[:], dmid[:], ACT.Exp, scale=-1.0)
                    act.activation(qhat[:], bc[:], ACT.Exp)
                    act.activation(khat[:], dlast[:], ACT.Exp).then_inc(gate_exp, 1)

            in_tiles(EVEN_GROUPS, EVEN_ORDER, EVEN_TOKEN, 3, 2 * KD, copy, before)
            act.wait_ge(gla_kt, 1)
            act.activation(k_tok[:].rearrange("p t j n -> p (t j n)"), ps[7][:, :], ACT.Copy).then_inc(gla_ktc, 1)
            act.wait_ge(at_done, UN)
            for k in range(4):
                mix_split(k, S)
            split_next(2 * KD, 0, 1)
            for hd in range(6):
                if hd < 4:
                    act.wait_ge(gla_o, hd + 1)
                    act.activation(g_sq[:, hd, :], ps[4 + hd][:, 0:S], ACT.Square).then_inc(gla_sqd, 1)
                if 1 <= hd < 5:
                    act.wait_ge(gla_var, hd)
                    act.activation(g_std[:, hd - 1, :], ps[hd - 1][:, 0:S], ACT.Sqrt, scale=1.0 / P,
                                   bias=eps[:, 1:2]).then_inc(gla_std, 1)
                if hd >= 2:
                    act.wait_ge(gla_done, hd - 1)
                    mix_split(4 + hd - 2, S)
            project_out(S)
            post_norm(UP_BLOCKS)
            pre_norm(x_ready)
            ffn(ODD_GROUPS[0] * KD, S)
            post_norm(ODD_GROUPS[1] * KD)

            pre_norm(x_ready)
            SCALE_D = 96 ** -0.5

            def copy(z, bank):
                if z < 4:
                    last = act.activation(qc[:, z, :], bank[:, 0:S], ACT.Copy, scale=EIGHTH)
                elif z == 4:
                    for kv in range(2):
                        for e in range(2):
                            last = act.activation(kdup[64 * e:64 * e + 64, kv, :], bank[64 * kv:64 * kv + 64, 0:S],
                                                  ACT.Copy)
                elif z == 5:
                    last = act.activation(vc[:], bank[:, :].rearrange("p (t n) -> p t n", t=2)[:, :, P:2 * P],
                                          ACT.Copy)
                elif z < 11:
                    last = act.activation(cqkv[:, z - 6, :], bank[:, 0:S], ACT.Copy)
                else:
                    act.activation(rt[64:96, 0, :], bank[64:96, 0:S], ACT.Copy)
                    last = act.activation(rt[64:96, 1, :], bank[96:128, 0:S], ACT.Copy)
                last.then_inc(z2_copied, 1)

            seen.skip(z2_copied, 25)

            def step_cd(u):
                attention(u, 2 * UN, UN, UN, lambda u: 0 if u < UN else 1, lambda u: 0 if u < UN else 4)

            def before(c):
                if c == 3:
                    act.wait_ge(z2_copied, 25 + 6)
                    for k in range(5):
                        last = act.activation(y[:, k, 0:S], cqkv[:, k, :], ACT.Square)
                        if k in (2, 4):
                            last.then_inc(c_sqd, 1)
                elif c == 4:
                    for g, width in enumerate((384, 256)):
                        act.wait_ge(c_var, g + 1)
                        act.activation(sig[:, g, 0:S], ps[6 + g][:, 0:S], ACT.Sqrt, scale=1.0 / width,
                                       bias=eps[:, 1:2]).then_inc(c_std, 1)
                elif c == 5:
                    for k in range(5):
                        act.wait_ge(c_nrm, k + 1)
                        act.activation(g_hi[:, k, 0:S], cqkv[:, k, :], ACT.Copy).then_inc(c_hi, 1)
                    step_cd(0)

            in_tiles(ODD_GROUPS, ODD_ORDER, (), 3, 16, copy, before)
            split_next(12, 0, 1)
            step_cd(1)
            for j in range(4):
                act.wait_ge(kn_ready, j + 1)
                act.activation(kd[0:64, 2 * j, :], ps[j % 2][0:64, 0:S], ACT.Copy)
                act.activation(kd[0:64, 2 * j + 1, :], ps[j % 2][64:128, 0:S], ACT.Copy).then_inc(kn_copied, 1)
            step_cd(2)
            for t in range(2):
                if t:
                    act.wait_ge(chunk_used, st.value(0, 0, 2))
                else:
                    act.wait_ge(vd_ready, 1)
                act.activation(vd[:, t, :], ps[2 + t][:, :], ACT.Copy).then_inc(vd_copied, 1)
            split_next(12, 0, 2)
            step_cd(3)
            for c in range(2):
                if c:
                    split_next(2 * KD, 0, 3)
                    step_cd(5)
                for e in range(4):
                    z = 4 * c + e
                    if e == 3:
                        act.wait_ge(chunk_used, st.value(1 + c, 0, 2))
                    else:
                        act.wait_ge(qd_ready, 3 * c + e + 1)
                    if z < 2:
                        act.wait_ge(kd_ready, 1)
                    else:
                        act.wait_ge(qd_roped, z - 1)
                    act.activation(qd[0:96, z, :], ps[z % 4][0:96, 0:S], ACT.Copy, scale=SCALE_D)
                    act.activation(rt[64:96, z % 2, :], ps[z % 4][96:128, 0:S], ACT.Copy, scale=SCALE_D)\
                        .then_inc(qd_copied, 1)
                    if e == 1:
                        step_cd(4 + 2 * c)
            st.c += 3
            for u in range(UN - 1, 2 * UN + 3):
                step_cd(u)
                if UN + 4 <= u < UN + 8:
                    act.wait_ge(at_done, 2 * UN)
                    mix_split(u - UN - 4, S)
            act.wait_ge(at_done, 3 * UN)
            for k in range(4, KD):
                mix_split(k, S)
            split_next(2 * KD, 0, 1)
            project_out(S)
            post_norm(UP_BLOCKS)
            pre_norm(x_ready)
            ffn(0, S)
            post_norm(0)
            for k in range(KD):
                act.wait_ge(out_t, k + 1)
                act.activation(x_tok[:, 0:2, k * P:(k + 1) * P],
                               ps[k][:, 0:2 * P].rearrange("p (t n) -> p t n", t=2), ACT.Copy).then_inc(out_c, 1)

        @block.vector
        def _(dve):
            seen, st = Seen(per_layer), Stream()

            def link(ins):
                ins.then_inc(dve_seq, 1)
                dve.wait_ge(dve_seq, seen.next(dve_seq))

            def split_next(blocks, pairs=0, ahead=1):
                if blocks:
                    slot = st.slot(ahead)
                    dve.wait_ge(w_hi_done, st.value(ahead, pairs, 1))
                    dve.tensor_tensor(w_lo[:, slot, 0:blocks * P], raw[:, slot, 0:blocks * P],
                                      w_hi[:, slot, 0:blocks * P].bitcast(F32), ALU.subtract).then_inc(w_ready, 1)

            def vcol(l, col):
                return vec[:, bass.ds(l, 1), col:col + 1].rearrange("p a b -> p (a b)")

            def inverse_std(n):
                dve.wait_ge(std_ready, seen.next(std_ready))
                link(dve.reciprocal(rstd[:, 0:n], std[:, 0:n]))

            def layer_norm(gain, bias, early):
                dve.wait_ge(mean_ready, seen.next(mean_ready))
                for k in range(KD):
                    dve.scalar_tensor_tensor(y[:, k, :], ps[6][:, 0:T], -1.0 / D, y[:, k, :], ALU.mult, ALU.add)\
                        .then_inc(centered, 1)
                split_next(early)
                inverse_std(T)
                for k in range(KD + 1):
                    if k < KD:
                        dve.scalar_tensor_tensor(y[:, k, :], y[:, k, :], gain(k), rstd[:], ALU.mult, ALU.mult)\
                            .then_inc(normed, 1)
                    if k:
                        dve.wait_ge(affine, seen.next(affine))
                        dve.scalar_tensor_tensor(hs(h_lo, k - 1), y[:, k - 1, :], bias(k - 1),
                                                 hs(h_hi, k - 1).bitcast(F32), ALU.add, ALU.subtract)\
                            .then_inc(h_ready, 1)
                seen.skip(normed, KD)

            def scaled(k, source, col):
                dve.scalar_tensor_tensor(y[:, k, 0:S], source, uvec[:, col + k:col + k + 1], rstd[:, 0:S],
                                         ALU.mult, ALU.mult).then_inc(normed, 1)

            def pre_norm(col):
                inverse_std(S)
                for k in range(KD + 1):
                    if k < KD:
                        scaled(k, xk(k), col)
                    if k:
                        dve.wait_ge(affine, seen.next(affine))
                        dve.tensor_tensor(hs(h_lo, k - 1, 0, S), y[:, k - 1, 0:S],
                                          hs(h_hi, k - 1, 0, S).bitcast(F32), ALU.subtract).then_inc(h_ready, 1)
                seen.skip(normed, KD)

            def post_norm(col, early):
                split_next(early)
                inverse_std(S)
                for k in range(KD + 1):
                    if k < KD:
                        scaled(k, y[:, k, 0:S], col)
                    if k:
                        dve.wait_ge(normed, seen.next(normed))
                        dve.tensor_tensor(xk(k - 1), xk(k - 1), y[:, k - 1, 0:S], ALU.add).then_inc(x_ready, 1)

            def take_tile(m, bank, first_block):
                if first_block:
                    dve.wait_ge(h_done, seen.at(h_done, 0))
                    ins = dve.scalar_tensor_tensor(y[:, m, :].rearrange("p a n -> p (a n)"),
                                                   h[:, m, :].rearrange("p a n -> p (a n)"), ALPHA,
                                                   bank[:, 0:T], ALU.mult, ALU.add)
                else:
                    ins = dve.tensor_copy(y[:, m, 0:S].rearrange("p a n -> p (a n)"), bank[:, 0:S])
                ins.then_inc(y_ready, 1)

            def ffn(after, first_block=True):
                n = T if first_block else S

                def up(i, j, last):
                    if not (isinstance(i, int) and (i, j) == (0, 0)):
                        split_next(DOWN_BLOCKS if last else UP_BLOCKS, i, j + 1)
                    dve.wait_ge(silu_ready, seen.at(silu_ready, i * 2 + (j + 1)))
                    dve.scalar_tensor_tensor(gf[:, j, 0:n], sig[:, j, 0:n], 0.5 if first_block else 1.0,
                                             ps[2 * j + 1][:, 0:n], ALU.mult, ALU.mult).then_inc(up_free, 1)
                    dve.wait_ge(up_free, seen.at(up_free, i * 2 + (j + 1)))
                    f = bass.ds(i * 2 + j, 1)
                    hi = g_hi[:, f, 0:n].rearrange("p a n -> p (a n)")
                    dve.tensor_copy(hi, gf[:, j, 0:n]).then_inc(g_hi_done, 1)
                    dve.wait_ge(g_hi_done, seen.at(g_hi_done, i * 2 + (j + 1)))
                    dve.tensor_tensor(g_lo[:, f, 0:n].rearrange("p a n -> p (a n)"), gf[:, j, 0:n],
                                      hi.bitcast(F32), ALU.subtract).then_inc(g_ready, 1)

                def down(i, j, last):
                    split_next(after if last else DOWN_BLOCKS, i, j + 1)
                    dve.wait_ge(chunk_used, st.value(j, i, 2))
                    take_tile(bass.ds(i * 2 + j, 1), ps[4 + j], first_block)

                pairs_of(dve, FT, up)
                for s in (silu_ready, up_free, g_hi_done):
                    seen.skip(s, FT)
                st.c += FT
                if first_block:
                    seen.skip(h_done, 1)
                pairs_of(dve, KD, down)
                st.c += KD

            def project_out(first_block):
                for c in range(OUT_CHUNKS):
                    if c:
                        split_next(2 * KD if c + 1 < OUT_CHUNKS else UP_BLOCKS, 0, c + 1)
                    dve.wait_ge(tile_ready, seen.next(tile_ready))
                    take_tile(bass.ds(2 * c, 1), ps[4], first_block)
                    dve.wait_ge(chunk_used, st.value(c, 0, 2))
                    take_tile(bass.ds(2 * c + 1, 1), ps[5], first_block)
                st.c += OUT_CHUNKS

            def mix_split(tiles, n):
                for k in tiles:
                    dve.wait_ge(mix_hi, seen.next(mix_hi))
                    dve.tensor_tensor(g_lo[:, k, 0:n], y[:, k, 0:n], g_hi[:, k, 0:n].bitcast(F32), ALU.subtract)\
                        .then_inc(mix_ready, 1)

            dve.memset(eps[:, 0:1], LN_EPS).then_inc(w_ready, 2)
            dve.memset(eps[:, 1:2], RMS_EPS).then_inc(chunk_used, 1)
            dve.memset(hs(h_hi, KD, 0, P).bitcast(F32), 0.0).then_inc(up_free, 2)
            dve.memset(hs(h_lo, KD, 0, P).bitcast(F32), 0.0)
            dve.memset(ones[:], 1.0).then_inc(consts_set, 1)
            seen.skip(up_free, 2)
            for k in range(KD):
                dve.wait_ge(xT_ready, k + 1)
                dve.tensor_copy(y[:, k, :], ps[k % 4][:, 0:T]).then_inc(y_ready, 1)
            split_next(UP_BLOCKS, 0, 0)
            dve.wait_ge(consts_loaded, 16 * 7)
            layer_norm(lambda k: uvec[:, U_ING + k:U_ING + k + 1], lambda k: uvec[:, U_INB + k:U_INB + k + 1],
                       UP_BLOCKS)
            with dve.Fori(0, LAYERS) as l:
                seen.enter(l)
                st.enter(l)
                def norm(i, early):
                    layer_norm(lambda k: vcol(l, V_LN + 16 * i + k), lambda k: vcol(l, V_LN + 16 * i + 8 + k), early)

                ffn(IN_GROUPS[0] * KD)
                norm(0, IN_GROUPS[1] * KD)
                dve.memset(xpad[:, :, 0:16], 0.0)
                link(dve.memset(upad[:, :, 0:TAPS - 1], 0.0))

                def pool_windows():
                    W = 16 + T
                    src = xpad
                    for i, w in enumerate((1, 2, 4, 8)):
                        dst = win[i % 3]
                        link(dve.tensor_tensor(dst[:, :, 2 * w - 1:W], src[:, :, 2 * w - 1:W],
                                               src[:, :, w - 1:W - w], ALU.add))
                        r, j = 64 * (i % 2), i // 2
                        last = dve.tensor_tensor(pool_y[r:r + 64, j, :], dst[r:r + 64, j, 16:W],
                                                 inv_count[r:r + 64, j, :], ALU.mult)
                        src = dst
                    link(last)
                    dve.tensor_tensor(pool_y[:], pool_y[:], xpad[:, :, 16:W], ALU.subtract).then_inc(pool_in, 1)

                def conv_tap(i):
                    u, w = upad[:, 0, i:i + T], vcol(l, V_DW + i)
                    if i == 0:
                        ins = dve.tensor_scalar(conv_y[:, 0, :], u, w, vcol(l, V_CDB), ALU.mult, ALU.add)
                    else:
                        ins = dve.scalar_tensor_tensor(conv_y[:, 0, :], u, w, conv_y[:, 0, :], ALU.mult, ALU.add)
                    if i == TAPS - 1:
                        ins.then_inc(conv_done, 1)
                    else:
                        link(ins)

                def rope(i):
                    dst = (qT if i < HEADS else kT)[:, i % HEADS, :]
                    dve.tensor_tensor(qk_raw[:, i % 2, :], qk_raw[:, i % 2, :], rope_cos[:], ALU.mult)
                    link(dve.tensor_tensor(qk_swap[:, i % 2, :], qk_swap[:, i % 2, :], rope_sin[:], ALU.mult))
                    dve.tensor_tensor(dst, qk_raw[:, i % 2, :], qk_swap[:, i % 2, :], ALU.add)\
                        .then_inc(rope_ready, 1)

                z, tap = 0, 0
                for c, tiles in enumerate(IN_GROUPS):
                    if c:
                        split_next(IN_GROUPS[c + 1] * KD if c + 1 < len(IN_GROUPS) else 2 * KD, 0, c + 1)
                    if c < 7:
                        dve.wait_ge(z_copied, seen.at(z_copied, z + tiles))
                    if c == 1:
                        pool_windows()
                    elif c == 2:
                        dve.tensor_copy(taps[:, 0:TAPS], vec[:, bass.ds(l, 1), V_DW + TAPS:V_DW + 2 * TAPS]
                                        .rearrange("p a b -> p (a b)"))
                        dve.tensor_copy(taps[:, TAPS:TAPS + 1], vcol(l, V_CDB + 1))
                        dve.tensor_tensor(upad[:, :, TAPS - 1:], ca[:], cg[:], ALU.mult).then_inc(conv_in, 1)
                        dve.wait_ge(conv_in, seen.next(conv_in))
                    elif c < 7 and c > 2:
                        rope(z - QK[0])
                        rope(z + 1 - QK[0])
                    if c >= 2:
                        for _ in range(2 if c < 7 else 4):
                            conv_tap(tap)
                            tap += 1
                    z += tiles
                while tap < TAPS:
                    conv_tap(tap)
                    tap += 1
                seen.skip(z_copied, 22)
                seen.skip(tile_ready, 8)
                st.c += len(IN_GROUPS)
                dve.wait_ge(conv_mean, seen.next(conv_mean))
                for j in range(2):
                    dve.scalar_tensor_tensor(conv_y[:, j, :], ps[6][:, 0:T], -1.0 / (2 * P), conv_y[:, j, :],
                                             ALU.mult, ALU.add).then_inc(conv_cent, 1)
                dve.wait_ge(conv_std, seen.next(conv_std))
                link(dve.reciprocal(rstd[:], std[:]))
                for j in range(2):
                    dve.tensor_tensor(conv_y[:, j, :], conv_y[:, j, :], rstd[:], ALU.mult).then_inc(conv_nrm, 1)
                dve.wait_ge(h_done, seen.next(h_done))
                for i in range(HEADS + 4):
                    if i < HEADS:
                        for t, (lo, m) in enumerate(KTOK):
                            dve.wait_ge(ret_s, seen.next(ret_s))
                            dve.tensor_tensor(pT[0:m, i % 2, t, :], ps[(3 * i + t) % 4][0:m, 0:T],
                                              decay[0:m, t, i, :], ALU.mult).then_inc(ret_p, 1)
                    if i == 1:
                        split_next(2 * KD, 0, 1)
                    if 0 <= i - 1 < HEADS:
                        dve.wait_ge(ret_o, seen.next(ret_o))
                        dve.tensor_copy(o_c[:, i - 1, :], ps[4 + (i - 1) % 2][:, 0:T]).then_inc(ret_oc, 1)
                    if 0 <= i - 2 < HEADS:
                        hd = i - 2
                        dve.wait_ge(ret_mean, seen.next(ret_mean))
                        dve.scalar_tensor_tensor(o_c[:, hd, :], ps[6][:, 0:T], -1.0 / P, o_c[:, hd, :],
                                                 ALU.mult, ALU.add).then_inc(ret_cent, 1)
                        dve.wait_ge(ret_cent, seen.next(ret_cent))
                        link(dve.scalar_tensor_tensor(y[:, 4 + hd, :], o_c[:, hd, :], vcol(l, V_GN + hd),
                                                      gate_s[:, hd, :], ALU.mult, ALU.mult))
                    if 0 <= i - 3 < HEADS:
                        hd = i - 3
                        dve.wait_ge(ret_std, seen.next(ret_std))
                        link(dve.reciprocal(o_rstd[:, hd, :], o_std[:, hd % 2, :]))
                        dve.tensor_tensor(y[:, 4 + hd, :], y[:, 4 + hd, :], o_rstd[:, hd, :], ALU.mult)\
                            .then_inc(ret_done, 1)
                    if i == 2:
                        mix_split(range(4), T)
                    if i >= 4:
                        mix_split((i,), T)
                project_out(True)
                norm(1, UP_BLOCKS)
                ffn(UP_BLOCKS)
                norm(2, UP_BLOCKS)
                assert seen.n[dve_seq.name] - seen.before[dve_seq.name] == DVE_LINKS
            seen.leave()
            st.leave()

            def logits(u, low, add_bias):
                t, j = UNITS[u % UN]
                b, keys = u % 2, P * (t + 1)
                dve.wait_ge(at_s, u + 1)
                if u >= 2:
                    dve.wait_ge(at_exp, u - 1)
                if low == 0:
                    dve.tensor_copy(att_s[:, b, :, 0], sinks[:, 2 * j:2 * j + 2])
                start = UN if u < UN else 2 * UN
                link(add_bias(unit_banks(u, start), b, t, j, keys))
                dve.tensor_reduce(att_max[:, b, :], att_s[:, b, :, low:1 + keys], AX.X, ALU.max, negate=True)\
                    .then_inc(at_max, 1)

            def inverse(u):
                dve.wait_ge(at_exp, u + 1)
                dve.reciprocal(att_inv[:, u % 2, :], att_sum[:, u % 2, :]).then_inc(at_inv, 1)

            def sloped(rel):
                def add(banks, b, t, j, keys):
                    for e in range(2):
                        last = dve.scalar_tensor_tensor(att_s[:, b, e, 1:1 + keys], rel[:, t, 0:keys],
                                                        2.0 ** -(2 * j + e + 1), banks[e][:, 0:keys],
                                                        ALU.mult, ALU.add)
                    return last
                return add

            def dilated(banks, b, t, j, keys):
                link(sloped(rel_a)(banks, b, t, j, keys))
                for e in range(2):
                    last = dve.tensor_tensor(att_s[:, b, e, 1:1 + keys], att_s[:, b, e, 1:1 + keys],
                                             logc[:, t, 0:keys], ALU.add)
                return last

            def causal(banks, b, t, j, keys):
                for e in range(2):
                    last = dve.tensor_tensor(att_s[:, b, e, 1:1 + keys], banks[e][:, 0:keys],
                                             mask_d[:, t, 0:keys], ALU.add)
                return last

            def in_stream(sizes, after, before, then):
                for c in range(len(sizes)):
                    before(c)
                    if c:
                        split_next(sizes[c + 1] * KD if c + 1 < len(sizes) else after, 0, c + 1)
                    then(c)
                st.c += len(sizes)

            dve.wait_ge(tables_loaded, 16 * 9)
            dve.wait_ge(h_done, 1 + 3 * LAYERS)
            pre_norm(U_RMS)

            def before(c):
                if 2 <= c < UN + 2:
                    logits(c - 2, 1, dilated)
                if 3 <= c < UN + 3:
                    inverse(c - 3)

            def then(c):
                if c == 6:
                    dve.wait_ge(gate_log, 1)
                    for j in range(2):
                        last = dve.tensor_scalar(za[:, j, :], ps[3][:, j * S:(j + 1) * S],
                                                 uvec[:, U_GATEB + j:U_GATEB + j + 1], 0.0, ALU.add, ALU.min)
                    link(last)
                    link(dve.tensor_tensor(za[:], za[:], zb[:], ALU.subtract))
                    for j in range(2):
                        last = dve.tensor_tensor_scan(bc[:, j, :], scan_m[:], za[:, j, :], 0.0, ALU.mult, ALU.add)
                    link(last)
                elif c == 7:
                    link(dve.tensor_scalar(bc[:], bc[:], 1.0 / 16.0, None, ALU.mult))
                    for j in range(2):
                        by_chunk = bc[:, j, :].rearrange("p (c i) -> p c i", i=64)
                        dve.tensor_tensor(dmid[:, j, :].rearrange("p (c i) -> p c i", i=64), by_chunk,
                                          by_chunk[:, :, 31:32].broadcast_to([P, 4, 64]), ALU.subtract)
                        last = dve.tensor_tensor(dlast[:, j, :].rearrange("p (c i) -> p c i", i=64),
                                                 by_chunk[:, :, 63:64].broadcast_to([P, 4, 64]), by_chunk,
                                                 ALU.subtract)
                    last.then_inc(gate_cum, 1)
                elif c == 10:
                    dve.wait_ge(z2_copied, 17)
                    gla_inputs()

            def gla_inputs():
                dve.wait_ge(gate_exp, 1)
                link(dve.memset(att[:], 0.0))
                link(dve.tensor_copy(dec[:], qhat[:].rearrange("p j (c i) -> p j c i", i=64)[:, :, :, 63]))
                dve.tensor_tensor(qhat[:], qhat[:], qb[:], ALU.mult)
                link(dve.tensor_tensor(khat[:], khat[:], kb[:], ALU.mult))
                dve.tensor_tensor(qb[:], qb[:], za[:], ALU.mult)
                dve.tensor_tensor(kb[:], kb[:], zb[:], ALU.mult).then_inc(gla_in, 1)

            in_stream(EVEN_GROUPS, 2 * KD, before, then)
            seen.skip(tile_ready, 8)
            dve.wait_ge(gla_s, 1)
            for t in range(2):
                for hd in range(4):
                    last = dve.copy_predicated(att[:, t, hd, :], tril[:].bitcast(I32),
                                               ps[2 * (hd % 2) + t][:, (hd // 2) * P:(hd // 2 + 1) * P])
            last.then_inc(gla_att, 1)
            dve.wait_ge(gla_ds, 1)
            link(dve.tensor_copy(state[:, 0].rearrange("p j n -> p (j n)"), ps[4][:, 0:2 * P]))
            for n in (1, 2):
                for j in range(2):
                    last = dve.scalar_tensor_tensor(state[:, n, j, :], state[:, n - 1, j, :], dec[:, j, n:n + 1],
                                                    ps[4 + n][:, j * P:(j + 1) * P], ALU.mult, ALU.add)
                if n == 1:
                    link(last)
                else:
                    last.then_inc(gla_state, 1)
            mix_split(range(4), S)
            split_next(2 * KD, 0, 1)
            for i in range(6):
                if i < 4:
                    dve.wait_ge(gla_sqd, i + 1)
                    dve.scalar_tensor_tensor(y[:, 4 + i, 0:S], ps[4 + i][:, 0:S], uvec[:, U_GLAN:U_GLAN + 1],
                                             rb[:, i, :], ALU.mult, ALU.mult)
                if 1 <= i < 5:
                    dve.wait_ge(gla_std, i)
                    link(dve.reciprocal(g_std[:, i - 1, :], g_std[:, i - 1, :]))
                    dve.tensor_tensor(y[:, 3 + i, 0:S], y[:, 3 + i, 0:S], g_std[:, i - 1, :], ALU.mult)\
                        .then_inc(gla_done, 1)
                if i >= 2:
                    mix_split((i + 2,), S)
            project_out(False)
            post_norm(U_RMS + 8, UP_BLOCKS)
            pre_norm(U_RMS + 16)
            ffn(ODD_GROUPS[0] * KD, False)
            post_norm(U_RMS + 24, ODD_GROUPS[1] * KD)

            pre_norm(U_RMS + 32)

            def step_cd(u):
                if u < 2 * UN:
                    logits(UN + u, 0 if u < UN else 1, sloped(rel_c) if u < UN else causal)
                if u >= 1:
                    inverse(UN + u - 1)

            def before(c):
                if c == 5:
                    step_cd(0)

            def then(c):
                if c == 3:
                    dve.wait_ge(z2_copied, 25 + 6)
                    dve.tensor_tensor(rt[64:96, 0, :], rt[64:96, 0, :], rcos[64:96, :], ALU.mult)
                    link(dve.tensor_tensor(rt[64:96, 1, :], rt[64:96, 1, :], rsin[64:96, :], ALU.mult))
                    for hd in range(8):
                        last = dve.tensor_tensor(kd[64:96, hd, :], rt[64:96, 0, :], rt[64:96, 1, :], ALU.add)
                    last.then_inc(kd_ready, 1)
                elif c == 4:
                    dve.wait_ge(c_std, 2)
                    link(dve.reciprocal(gf[:, :, 0:S], sig[:, :, 0:S]))
                    for k in range(5):
                        g, col = (0, U_QN + k) if k < 3 else (1, U_KVN + k - 3)
                        dve.scalar_tensor_tensor(cqkv[:, k, :], cqkv[:, k, :], uvec[:, col:col + 1],
                                                 gf[:, g, 0:S], ALU.mult, ALU.mult).then_inc(c_nrm, 1)
                elif c == 5:
                    for k in range(5):
                        dve.wait_ge(c_hi, k + 1)
                        dve.tensor_tensor(g_lo[:, k, 0:S], cqkv[:, k, :], g_hi[:, k, 0:S].bitcast(F32),
                                          ALU.subtract).then_inc(c_ready, 1)

            in_stream(ODD_GROUPS, 16, before, then)
            seen.skip(tile_ready, 6)
            step_cd(1)
            split_next(12, 0, 1)
            step_cd(2)
            split_next(12, 0, 2)
            step_cd(3)
            for z in range(8):
                if z == 4:
                    split_next(2 * KD, 0, 3)
                    step_cd(5)
                dve.wait_ge(qd_copied, z + 1)
                dve.tensor_tensor(qd[64:96, z, :], qd[64:96, z, :], rcos[64:96, :], ALU.mult)
                link(dve.tensor_tensor(rt[64:96, z % 2, :], rt[64:96, z % 2, :], rsin[64:96, :], ALU.mult))
                dve.tensor_tensor(qd[64:96, z, :], qd[64:96, z, :], rt[64:96, z % 2, :], ALU.add)\
                    .then_inc(qd_roped, 1)
                if z in (1, 5):
                    step_cd(4 + z // 2)
            st.c += 3
            for u in range(UN - 1, 2 * UN + 1):
                step_cd(u)
                if UN + 4 <= u < UN + 8:
                    mix_split((u - UN - 4,), S)
            mix_split(range(4, KD), S)
            split_next(2 * KD, 0, 1)
            project_out(False)
            post_norm(U_RMS + 40, UP_BLOCKS)
            pre_norm(U_RMS + 48)
            ffn(0, False)
            post_norm(U_RMS + 56, 0)


def tables():
    f8 = np.float64
    t = {}
    t["ident"] = np.eye(P)
    gamma = 1.0 - 2.0 ** (-5.0 - np.arange(HEADS, dtype=f8))
    pos = np.arange(T)
    chunk = (pos + (-META) % 64) // 64
    dist = np.abs(pos[:, None] - pos[None, :])
    seen = chunk[:, None] <= chunk[None, :]
    d = np.where(seen[None], gamma[:, None, None] ** dist[None], 0.0) * P ** -0.5
    dk = np.zeros((P, 3, HEADS, T))
    for i, (lo, m) in enumerate(KTOK):
        dk[0:m, i] = d[:, lo:lo + m, :].transpose(1, 0, 2)
    t["decay"] = dk
    inv = (10000.0 ** (-np.arange(0, P, 2, dtype=np.float32) / np.float32(P))).astype(np.float32)
    ang = (np.arange(T, dtype=np.float32)[:, None] * inv[None, :]).T.astype(f8)
    t["rope_cos"] = np.concatenate([np.cos(ang), np.cos(ang)])
    t["rope_sin"] = np.concatenate([-np.sin(ang), np.sin(ang)])
    ic = np.zeros((P, 2, T))
    for g, w in enumerate((2, 4, 8, 16)):
        ic[64 * (g % 2):64 * (g % 2) + 64, g // 2] = 1.0 / np.minimum(pos + 1, w)
    t["inv_count"] = ic
    rel = np.arange(SEQ)[:, None] - np.arange(SEQ)[None, :]
    count = ((rel >= 0) & (rel <= 128)) * 1 + ((rel >= 0) & (rel % 4 == 0)) * 1 + ((rel >= 0) & (rel % 16 == 0)) * 1

    def by_tile(m):
        return m.reshape(2, P, SEQ).transpose(1, 0, 2)

    t["rel_a"] = by_tile(np.where(count > 0, -rel, -1e30))
    t["logc"] = by_tile(np.log(np.maximum(count, 1)))
    t["rel_c"] = by_tile(np.where((rel >= 0) & (rel <= 127), -rel, -1e30))
    t["mask_d"] = by_tile(np.where(rel >= 0, 0.0, -1e30))
    i = np.arange(P)
    t["tril"] = (i[:, None] <= i[None, :]) & (i[:, None] // 64 == i[None, :] // 64)
    t["scan_m"] = np.tile(np.arange(SEQ) % 64 != 0, (P, 1))
    half = 16
    freqs = (10000.0 ** (-np.arange(half, dtype=np.float32) / np.float32(half))).astype(np.float32)
    ang = (np.arange(SEQ, dtype=np.float32)[:, None] * freqs[None, :]).T.astype(f8)
    c, s = np.zeros((P, SEQ)), np.zeros((P, SEQ))
    c[64:96] = np.concatenate([np.cos(ang), np.cos(ang)])
    s[64:96] = np.concatenate([-np.sin(ang), np.sin(ang)])
    t["rcos"], t["rsin"] = c, s
    return {k: np.ascontiguousarray(v, dtype=np.float32) for k, v in t.items()}


def blocks(w, cols=P):
    k, n = w.shape
    return w.reshape(k // P, P, n // cols, cols).transpose(2, 1, 0, 3)


def padded(w, k, n):
    out = np.zeros((k, n), w.dtype)
    out[:w.shape[0], :w.shape[1]] = w
    return out


def tiles_to_chunks(w, per):
    b = blocks(w)
    b = b.reshape(-1, per, P, KD, P).transpose(0, 2, 1, 3, 4)
    return b.reshape(b.shape[0], P, -1)


def in_chunks(w, groups, order):
    b = blocks(w)[list(order)]
    out = np.zeros((len(groups), P, 2 * KD * P), w.dtype)
    z = 0
    for c, n in enumerate(groups):
        out[c, :, :n * KD * P] = b[z:z + n].transpose(1, 2, 0, 3).reshape(P, -1)
        z += n
    return out


def up_layout(gate, up):
    f = FT * P
    g, u = blocks(padded(gate, D, f)), blocks(padded(up, D, f))
    return np.stack([g, u], axis=3).reshape(FT, P, UP_BLOCKS * P)


def down_layout(w):
    return blocks(padded(w, FT * P, D)).reshape(KD, P, DOWN_BLOCKS * P)


def columns(v):
    return v.reshape(-1, P).T


def lay_out(i):
    a = {}
    dff = i["ffn1_w2"].shape[1]
    up, down = [], []
    for l in range(LAYERS):
        for n in ("ffn1", "ffn2"):
            w = i[n + "_w13"][l]
            up.append(up_layout(w[:, :dff], w[:, dff:]))
            down.append(down_layout(i[n + "_w2"][l]))
    for l in range(2):
        up.append(up_layout(i["ffn_w_gate_2"][l], i["ffn_w_up_2"][l]))
        down.append(down_layout(i["ffn_w_down_2"][l]))
    a["up_w"], a["down_w"] = np.stack(up), np.stack(down)
    a["in_w"] = np.stack([in_chunks(i["w_in"][l], IN_GROUPS, range(22)) for l in range(LAYERS)])
    outs = [i["w_out"][0], i["w_out"][1], i["ab_w_out_2"][0], i["cd_w_out_2"][0]]
    a["out_w"] = np.stack([tiles_to_chunks(w, 2) for w in outs])
    a["even_w"] = in_chunks(padded(i["ab_w_in_2"][0], D, 25 * P), EVEN_GROUPS, EVEN_ORDER)
    w = i["cd_w_in_2"][0]
    odd = np.zeros((D, 12 * P), np.float32)
    odd[:, :1408] = w[:, :1408]
    odd[:, 1408 + 64:1408 + 96] = w[:, 1408:1440]
    odd[:, 1408 + 96:1408 + 112] = w[:, 1424:1440]
    odd[:, 1408 + 112:1408 + 128] = w[:, 1408:1424]
    a["odd_w"] = in_chunks(odd, ODD_GROUPS, ODD_ORDER)
    w = i["mla_w_uq_2"][0].reshape(384, 8, 96)
    w = np.concatenate([w, w[:, :, 80:96], w[:, :, 64:80]], axis=2).reshape(384, 8 * P)
    a["uq_w"] = blocks(w).reshape(2, 4, P, 3 * P).transpose(0, 2, 1, 3).reshape(2, P, 12 * P)
    w = i["mla_w_ukv_2"][0].reshape(256, 8, 2, 64)
    w = w.transpose(0, 2, 1, 3).reshape(2, P, 1024)
    a["ukv_w"] = w.transpose(1, 0, 2).reshape(P, 2048)
    mixw = np.zeros((LAYERS, P, 6, P), np.float32)
    for l in range(LAYERS):
        for g in range(4):
            r = 64 * (g % 2)
            mixw[l, r:r + 64, g // 2, r:r + 64] = i["pool_w"][l, g]
        mixw[l, :, 2:6] = i["conv_pw"][l].reshape(2, P, 2, P).transpose(1, 0, 2, 3).reshape(P, 4, P)
    a["mixw"] = mixw
    v = np.zeros((P, LAYERS, NV), np.float32)
    for l in range(LAYERS):
        for n in range(3):
            v[:, l, 16 * n:16 * n + 8] = columns(i["ln_g"][l, n])
            v[:, l, 16 * n + 8:16 * n + 16] = columns(i["ln_b"][l, n])
        for col, name, n in ((V_PSC, "pool_scale", 2), (V_CDB, "conv_db", 2), (V_CG, "conv_ln_g", 2),
                             (V_CB, "conv_ln_b", 2), (V_GN, "ret_gn_g", 4)):
            v[:, l, col:col + n] = columns(i[name][l])
        v[:, l, V_DW:] = i["conv_dw"][l].reshape(TAPS, 2, P).transpose(2, 1, 0).reshape(P, 2 * TAPS)
    a["vec"] = v
    u = np.zeros((P, NU), np.float32)
    u[:, U_ING:U_ING + 8] = columns(i["ln_in_g"])
    u[:, U_INB:U_INB + 8] = columns(i["ln_in_b"])
    for l in range(2):
        for n, name in enumerate(("norm_mix_pre_2", "norm_mix_post_2", "norm_ffn_pre_2", "norm_ffn_post_2")):
            c = U_RMS + 32 * l + 8 * n
            u[:, c:c + 8] = columns(i[name][l])
    u[:, U_GATEB:U_GATEB + 2] = columns(i["gla_b_gate_2"][0])
    u[:, U_GLAN] = i["gla_norm_2"][0]
    u[:, U_QN:U_QN + 3] = columns(i["mla_q_norm_2"][0])
    u[:, U_KVN:U_KVN + 2] = columns(i["mla_kv_norm_2"][0])
    a["uvec"] = u
    a["sinks"] = np.tile(i["swa_sinks_2"][0], (P, 1))
    gup = np.zeros((P, 2, P), np.float32)
    gup[0:16] = i["gla_w_gate_up_2"][0].reshape(16, 2, P)
    a["gup"] = gup
    a["x"], a["meta"] = i["x"][0], i["meta"]
    return {k: np.ascontiguousarray(w) for k, w in a.items()}


def kernel(**inputs):
    import concourse.bacc as bacc
    from concourse.bass_utils import run_bass_kernel_spmd

    arrays = lay_out({k: np.asarray(v) for k, v in inputs.items()})
    arrays.update(tables())
    nc = bacc.Bacc("TRN2", target_bir_lowering=False, num_devices=1)
    arrays = {f"in_{k}": v for k, v in arrays.items()}
    a = {k[3:]: nc.dram_tensor(k, v.shape, F32, kind="ExternalInput").ap() for k, v in arrays.items()}
    a["out"] = nc.dram_tensor("out", (SEQ, D), F32, kind="ExternalOutput").ap()
    forward(nc, a)
    r = run_bass_kernel_spmd(nc, [arrays], core_ids=[0])
    return r.results[0]["out"].reshape(1, SEQ, D)
```
